# Optimizing a Trainium2 kernel written in Bass

```python
import jax, jax.numpy as jnp
from jax import lax
import numpy as np
import math

D_MODEL = 1024
BATCH = 1
SEQ = 256
DEPTH = 1

A_HEADS = 8
A_KV_HEADS = 2
A_HEAD_DIM = 64
IDX_HEADS = 8
IDX_DIM = 64
TOPK_MAX = 256
B_HEADS = 8
B_HEAD_DIM = 64
A_WIDTH = A_HEADS * A_HEAD_DIM
B_WIDTH = B_HEADS * B_HEAD_DIM
MIX_WIDTH = A_WIDTH + B_WIDTH
A_KV_WIDTH = A_KV_HEADS * A_HEAD_DIM
IDX_Q_WIDTH = IDX_HEADS * IDX_DIM
IN_SPLITS = (A_WIDTH, A_KV_WIDTH, A_KV_WIDTH, IDX_Q_WIDTH, IDX_DIM, IDX_HEADS,
             B_WIDTH, B_WIDTH, B_WIDTH, B_HEADS)
IN_COLS = sum(IN_SPLITS)
Q_BLOCK = 128
N_GROUPS = 4
EXPERTS_PER_GROUP = 8
N_EXPERTS = N_GROUPS * EXPERTS_PER_GROUP
TOPK_EXPERT = 2
D_FF_EXPERT = D_MODEL // 4
N_MOD = 6
EPS = 1e-6


def rms_norm(x, g):
    xf = x.astype(jnp.float32)
    y = xf * lax.rsqrt(jnp.mean(xf * xf, axis=-1, keepdims=True) + EPS)
    return (y * g.astype(jnp.float32)).astype(x.dtype)

def alibi_slopes(n):
    return jnp.exp2(-8.0 * jnp.arange(1, n + 1, dtype=jnp.float32) / n)

def to_blocks(a, nb):
    return jnp.moveaxis(a.reshape(a.shape[0], nb, Q_BLOCK, *a.shape[2:]), 1, 0)

def dsa_attention(q, k, v, iq, ik, iw):
    bsz, L = q.shape[0], q.shape[1]
    n_top = min(TOPK_MAX, L // 4)
    nb = L // Q_BLOCK
    rep = A_HEADS // A_KV_HEADS
    slopes = alibi_slopes(A_HEADS).reshape(A_KV_HEADS, rep)
    scale = A_HEAD_DIM ** -0.5
    kpos = jnp.arange(L)
    ikf = ik.astype(jnp.float32)

    def block(args):
        qb, iqb, iwb, t0 = args
        tpos = t0 + jnp.arange(Q_BLOCK)
        dots = jnp.einsum('bqhd,bsd->bqhs', iqb.astype(jnp.float32), ikf)
        score = jnp.einsum('bqh,bqhs->bqs', iwb.astype(jnp.float32), jax.nn.relu(dots))
        causal = kpos[None, :] <= tpos[:, None]
        score = jnp.where(causal[None], score, -jnp.inf)
        _, idx = lax.top_k(score, n_top)
        valid = idx <= tpos[None, :, None]
        ksel = jax.vmap(lambda kb, ib: kb[ib])(k, idx)
        vsel = jax.vmap(lambda vb, ib: vb[ib])(v, idx)
        qg = qb.reshape(bsz, Q_BLOCK, A_KV_HEADS, rep, A_HEAD_DIM)
        logits = jnp.einsum('bqgrd,bqkgd->bqgrk', qg, ksel).astype(jnp.float32) * scale
        dist = (tpos[None, :, None] - idx).astype(jnp.float32)
        logits = logits - slopes[None, None, :, :, None] * dist[:, :, None, None, :]
        logits = jnp.where(valid[:, :, None, None, :], logits, -jnp.inf)
        p = jax.nn.softmax(logits, axis=-1).astype(v.dtype)
        o = jnp.einsum('bqgrk,bqkgd->bqgrd', p, vsel)
        return o.reshape(bsz, Q_BLOCK, A_WIDTH)

    out = lax.map(block, (to_blocks(q, nb), to_blocks(iq, nb), to_blocks(iw, nb),
                          jnp.arange(nb, dtype=jnp.int32) * Q_BLOCK))
    return jnp.moveaxis(out, 0, 1).reshape(bsz, L, A_WIDTH)

def forgetting_attention(q, k, v, log_f):
    bsz, L = q.shape[0], q.shape[1]
    nb = L // Q_BLOCK
    scale = B_HEAD_DIM ** -0.5
    cum = jnp.cumsum(log_f, axis=1)
    cum_k = jnp.transpose(cum, (0, 2, 1))
    kpos = jnp.arange(L)

    def block(args):
        qb, cb, t0 = args
        tpos = t0 + jnp.arange(Q_BLOCK)
        logits = jnp.einsum('bqhd,bshd->bhqs', qb, k).astype(jnp.float32) * scale
        logits = logits + jnp.transpose(cb, (0, 2, 1))[..., None] - cum_k[:, :, None, :]
        causal = kpos[None, :] <= tpos[:, None]
        logits = jnp.where(causal[None, None], logits, -jnp.inf)
        p = jax.nn.softmax(logits, axis=-1).astype(v.dtype)
        o = jnp.einsum('bhqs,bshd->bqhd', p, v)
        return o.reshape(bsz, Q_BLOCK, B_WIDTH)

    out = lax.map(block, (to_blocks(q, nb), to_blocks(cum, nb),
                          jnp.arange(nb, dtype=jnp.int32) * Q_BLOCK))
    return jnp.moveaxis(out, 0, 1).reshape(bsz, L, B_WIDTH)

def hybrid_mixer(h, w_in, b_forget, g_out_a, g_out_b, w_out):
    bsz, L, _ = h.shape
    proj = h @ w_in
    (aq, ak, av, iq, ik, iw, bq, bk, bv, bf) = jnp.split(
        proj, list(np.cumsum(IN_SPLITS)[:-1]), axis=-1)
    oa = dsa_attention(aq.reshape(bsz, L, A_HEADS, A_HEAD_DIM),
                       ak.reshape(bsz, L, A_KV_HEADS, A_HEAD_DIM),
                       av.reshape(bsz, L, A_KV_HEADS, A_HEAD_DIM),
                       iq.reshape(bsz, L, IDX_HEADS, IDX_DIM), ik, iw)
    log_f = jax.nn.log_sigmoid(bf.astype(jnp.float32) + b_forget.astype(jnp.float32))
    ob = forgetting_attention(bq.reshape(bsz, L, B_HEADS, B_HEAD_DIM),
                              bk.reshape(bsz, L, B_HEADS, B_HEAD_DIM),
                              bv.reshape(bsz, L, B_HEADS, B_HEAD_DIM), log_f)
    o = jnp.concatenate([rms_norm(oa, g_out_a), rms_norm(ob, g_out_b)], axis=-1)
    return o @ w_out

def hierarchical_moe(h, w_group, b_group, w_router, b_router, w_gate, w_up, w_down):
    bsz, L, d = h.shape
    t = h.reshape(-1, d)
    g_logits = (t @ w_group).astype(jnp.float32) + b_group.astype(jnp.float32)
    g_prob = jax.nn.softmax(g_logits, axis=-1)
    g_sel = jnp.argmax(g_logits, axis=-1)
    p_group = jnp.take_along_axis(g_prob, g_sel[:, None], axis=1)[:, 0]
    e_all = jnp.einsum('nd,gde->nge', t, w_router).astype(jnp.float32) + b_router.astype(jnp.float32)
    e_logits = jnp.take_along_axis(e_all, g_sel[:, None, None], axis=1)[:, 0]
    top_v, top_i = lax.top_k(e_logits, TOPK_EXPERT)
    w_top = jax.nn.softmax(top_v, axis=-1) * p_group[:, None]
    eid = g_sel[:, None] * EXPERTS_PER_GROUP + top_i
    comb = jnp.sum(jax.nn.one_hot(eid, N_EXPERTS, dtype=jnp.float32) * w_top[..., None], axis=1)
    hg = jnp.einsum('nd,edf->nef', t, w_gate)
    hu = jnp.einsum('nd,edf->nef', t, w_up)
    a = jax.nn.silu(hg) * hu * comb[:, :, None].astype(h.dtype)
    y = jnp.einsum('nef,efd->nd', a, w_down)
    return y.reshape(bsz, L, d)

def first_inputs(seed: int = 0) -> dict:
    key = jax.random.key(seed)
    ks = jax.random.split(key, 20)
    f32 = jnp.float32
    nrm = lambda k, shape, s: jax.random.normal(k, shape, f32) * s
    return {
        'x': nrm(ks[0], (BATCH, SEQ, D_MODEL), 1.0),
        'c': nrm(ks[1], (BATCH, D_MODEL), 1.0),
        'w_ada': nrm(ks[2], (DEPTH, D_MODEL, N_MOD * D_MODEL), 0.5 * D_MODEL ** -0.5),
        'b_ada': nrm(ks[3], (DEPTH, N_MOD * D_MODEL), 0.01),
        'g_mix': 1.0 + nrm(ks[4], (DEPTH, D_MODEL), 0.01),
        'w_in': nrm(ks[5], (DEPTH, D_MODEL, IN_COLS), D_MODEL ** -0.5),
        'b_forget': jax.random.uniform(ks[6], (DEPTH, B_HEADS), f32, 1.0, 4.0),
        'g_out_a': 1.0 + nrm(ks[7], (DEPTH, A_WIDTH), 0.01),
        'g_out_b': 1.0 + nrm(ks[8], (DEPTH, B_WIDTH), 0.01),
        'w_out': nrm(ks[9], (DEPTH, MIX_WIDTH, D_MODEL), MIX_WIDTH ** -0.5),
        'g_ffn': 1.0 + nrm(ks[10], (DEPTH, D_MODEL), 0.01),
        'w_group': nrm(ks[11], (DEPTH, D_MODEL, N_GROUPS), D_MODEL ** -0.5),
        'b_group': nrm(ks[12], (DEPTH, N_GROUPS), 0.01),
        'w_router': nrm(ks[13], (DEPTH, N_GROUPS, D_MODEL, EXPERTS_PER_GROUP), D_MODEL ** -0.5),
        'b_router': nrm(ks[14], (DEPTH, N_GROUPS, EXPERTS_PER_GROUP), 0.01),
        'w_gate': nrm(ks[15], (DEPTH, N_EXPERTS, D_MODEL, D_FF_EXPERT), D_MODEL ** -0.5),
        'w_up': nrm(ks[16], (DEPTH, N_EXPERTS, D_MODEL, D_FF_EXPERT), D_MODEL ** -0.5),
        'w_down': nrm(ks[17], (DEPTH, N_EXPERTS, D_FF_EXPERT, D_MODEL), D_FF_EXPERT ** -0.5),
        'g_final': 1.0 + nrm(ks[18], (D_MODEL,), 0.01),
    }

def first_block(x, c, w_ada, b_ada, g_mix, w_in, b_forget, g_out_a, g_out_b, w_out,
              g_ffn, w_group, b_group, w_router, b_router, w_gate, w_up, w_down, g_final):
    for l in range(DEPTH):
        mod = (jax.nn.silu(c) @ w_ada[l] + b_ada[l])[:, None, :]
        shift_m, scale_m, gate_m, shift_f, scale_f, gate_f = jnp.split(mod, N_MOD, axis=-1)
        h = rms_norm(x, g_mix[l]) * (1.0 + scale_m) + shift_m
        x = x + gate_m * hybrid_mixer(h, w_in[l], b_forget[l], g_out_a[l], g_out_b[l], w_out[l])
        h = rms_norm(x, g_ffn[l]) * (1.0 + scale_f) + shift_f
        x = x + gate_f * hierarchical_moe(h, w_group[l], b_group[l], w_router[l], b_router[l],
                                          w_gate[l], w_up[l], w_down[l])
    return rms_norm(x, g_final)


HG_HEADS = 4
HG_KDIM = 128
HG_VDIM = 128
HG_WIDTH = HG_HEADS * HG_KDIM
CHUNK = 32
LRU_WIDTH = 512
LRU_BLOCKS = 8
LRU_BLOCK_DIM = LRU_WIDTH // LRU_BLOCKS
CONV_WIDTH = 4
LRU_C = 8.0
D_MIX = HG_WIDTH + LRU_WIDTH
D_IN = 4 * HG_WIDTH + 2 * LRU_WIDTH
D_FF = -(-8 * D_MODEL // (3 * 256)) * 256


def rms_norm_2(x, w):
    xf = x.astype(jnp.float32)
    y = xf * lax.rsqrt(jnp.mean(xf * xf, axis=-1, keepdims=True) + EPS)
    return (y * w.astype(jnp.float32)).astype(x.dtype)

def hgrn2_mix(q, f_logit, i, g, lb, norm_w):
    B, S, _ = q.shape
    out_dtype = q.dtype
    qf = jax.nn.silu(q.astype(jnp.float32))
    f = lb + (1.0 - lb) * jax.nn.sigmoid(f_logit.astype(jnp.float32))
    log_f = jnp.log(f)
    k = 1.0 - f
    v = i.astype(jnp.float32)
    n_chunks = S // CHUNK

    def to_chunks(t, d):
        return t.reshape(B, n_chunks, CHUNK, HG_HEADS, d).transpose(1, 0, 3, 2, 4)

    qc, kc, gc, vc = to_chunks(qf, HG_KDIM), to_chunks(k, HG_KDIM), to_chunks(log_f, HG_KDIM), to_chunks(v, HG_VDIM)
    causal = jnp.tril(jnp.ones((CHUNK, CHUNK), dtype=bool))

    def step(state, xs):
        q_, k_, lg, v_ = xs
        b = jnp.cumsum(lg, axis=-2)
        b_last = b[..., -1:, :]
        q_dec = q_ * jnp.exp(b)
        k_dec = k_ * jnp.exp(-b)
        scores = jnp.where(causal, jnp.einsum('bhtk,bhsk->bhts', q_dec, k_dec), 0.0)
        o = jnp.einsum('bhts,bhsv->bhtv', scores, v_) + jnp.einsum('bhtk,bhkv->bhtv', q_dec, state)
        k_state = k_ * jnp.exp(b_last - b)
        new_state = jnp.exp(b_last)[..., 0, :, None] * state + jnp.einsum('bhsk,bhsv->bhkv', k_state, v_)
        return new_state, o

    state0 = jnp.zeros((B, HG_HEADS, HG_KDIM, HG_VDIM), jnp.float32)
    _, o = lax.scan(step, state0, (qc, kc, gc, vc))
    o = o.transpose(1, 0, 3, 2, 4).reshape(B, S, HG_HEADS, HG_VDIM)
    o = o * lax.rsqrt(jnp.mean(o * o, axis=-1, keepdims=True) + EPS) * norm_w.astype(jnp.float32)
    o = o * jax.nn.silu(g.astype(jnp.float32).reshape(B, S, HG_HEADS, HG_VDIM))
    return o.reshape(B, S, HG_WIDTH).astype(out_dtype)

def rglru_mix(xb, gate_b, conv_w, conv_b, wa, ba, wx, bx, a_param):
    B, S, W = xb.shape
    out_dtype = xb.dtype
    x_pad = jnp.pad(xb, ((0, 0), (CONV_WIDTH - 1, 0), (0, 0)))
    xc = conv_b + sum(x_pad[:, tap:tap + S] * conv_w[tap] for tap in range(CONV_WIDTH))
    xc = xc.astype(jnp.float32)
    xblk = xc.reshape(B, S, LRU_BLOCKS, LRU_BLOCK_DIM)
    r = jax.nn.sigmoid(jnp.einsum('bsnd,nde->bsne', xblk, wa.astype(jnp.float32)).reshape(B, S, W) + ba)
    ig = jax.nn.sigmoid(jnp.einsum('bsnd,nde->bsne', xblk, wx.astype(jnp.float32)).reshape(B, S, W) + bx)
    log_a = -LRU_C * r * jax.nn.softplus(-a_param.astype(jnp.float32))
    a = jnp.exp(log_a)
    b_in = jnp.sqrt(-jnp.expm1(2.0 * log_a)) * (ig * xc)

    def combine(lhs, rhs):
        a1, b1 = lhs
        a2, b2 = rhs
        return a1 * a2, a2 * b1 + b2

    _, h = lax.associative_scan(combine, (a, b_in), axis=1)
    y = h * jax.nn.gelu(gate_b.astype(jnp.float32), approximate=True)
    return y.astype(out_dtype)

def second_inputs(seed: int = 0) -> dict:
    key = jax.random.key(seed)
    ks = jax.random.split(key, 20)
    f32 = jnp.float32
    nrm = lambda k, shape, scale: (jax.random.normal(k, shape, f32) * scale)
    s_lru = jax.random.uniform(ks[12], (DEPTH, LRU_WIDTH), f32, 0.9, 0.999) ** (1.0 / LRU_C)
    return {
        'x': nrm(ks[0], (BATCH, SEQ, D_MODEL), 1.0),
        'mix_norm_w': 1.0 + nrm(ks[1], (DEPTH, D_MODEL), 0.02),
        'w_in': nrm(ks[2], (DEPTH, D_MODEL, D_IN), D_MODEL ** -0.5),
        'hg_lb': nrm(ks[3], (DEPTH + 1, HG_WIDTH), 0.5),
        'hg_norm_w': 1.0 + nrm(ks[4], (DEPTH, HG_VDIM), 0.02),
        'conv_w': nrm(ks[5], (DEPTH, CONV_WIDTH, LRU_WIDTH), CONV_WIDTH ** -0.5),
        'conv_b': nrm(ks[6], (DEPTH, LRU_WIDTH), 0.02),
        'lru_wa': nrm(ks[7], (DEPTH, LRU_BLOCKS, LRU_BLOCK_DIM, LRU_BLOCK_DIM), LRU_BLOCK_DIM ** -0.5),
        'lru_ba': nrm(ks[8], (DEPTH, LRU_WIDTH), 0.02),
        'lru_wx': nrm(ks[9], (DEPTH, LRU_BLOCKS, LRU_BLOCK_DIM, LRU_BLOCK_DIM), LRU_BLOCK_DIM ** -0.5),
        'lru_bx': nrm(ks[10], (DEPTH, LRU_WIDTH), 0.02),
        'lru_a': jnp.log(s_lru) - jnp.log1p(-s_lru),
        'w_out': nrm(ks[11], (DEPTH, D_MIX, D_MODEL), D_MIX ** -0.5),
        'ffn_norm_w': 1.0 + nrm(ks[13], (DEPTH, D_MODEL), 0.02),
        'w_gate_up': nrm(ks[14], (DEPTH, D_MODEL, 2 * D_FF), D_MODEL ** -0.5),
        'w_down': nrm(ks[15], (DEPTH, D_FF, D_MODEL), D_FF ** -0.5),
        'final_norm_w': 1.0 + nrm(ks[16], (D_MODEL,), 0.02),
    }

def second_block(x, mix_norm_w, w_in, hg_lb, hg_norm_w, conv_w, conv_b, lru_wa, lru_ba,
              lru_wx, lru_bx, lru_a, w_out, ffn_norm_w, w_gate_up, w_down, final_norm_w):
    lb_all = jnp.cumsum(jax.nn.softmax(hg_lb.astype(jnp.float32), axis=0), axis=0)
    h = x
    for l in range(DEPTH):
        xn = rms_norm_2(h, mix_norm_w[l])
        proj = jnp.einsum('bsd,de->bse', xn, w_in[l])
        q, f_logit, i_v, g, lru_x, lru_gate = jnp.split(
            proj, [HG_WIDTH, 2 * HG_WIDTH, 3 * HG_WIDTH, 4 * HG_WIDTH, 4 * HG_WIDTH + LRU_WIDTH], axis=-1)
        o_hg = hgrn2_mix(q, f_logit, i_v, g, lb_all[l], hg_norm_w[l])
        o_lru = rglru_mix(lru_x, lru_gate, conv_w[l], conv_b[l], lru_wa[l], lru_ba[l],
                          lru_wx[l], lru_bx[l], lru_a[l])
        mixed = jnp.concatenate([o_hg, o_lru], axis=-1)
        h = h + jnp.einsum('bse,ed->bsd', mixed, w_out[l])
        hn = rms_norm_2(h, ffn_norm_w[l])
        gate, up = jnp.split(jnp.einsum('bsd,df->bsf', hn, w_gate_up[l]), 2, axis=-1)
        h = h + jnp.einsum('bsf,fd->bsd', jax.nn.silu(gate) * up, w_down[l])
    return rms_norm_2(h, final_norm_w)


def setup_inputs(seed=0):
    out = dict(first_inputs(seed))
    for name, value in second_inputs(seed + 1).items():
        if name != "x":
            out[name + "_2"] = value
    return out


def reference(
    x, c, w_ada, b_ada, g_mix, w_in, b_forget, g_out_a, g_out_b, w_out, g_ffn, w_group, b_group,
    w_router, b_router, w_gate, w_up, w_down, g_final, mix_norm_w_2, w_in_2, hg_lb_2,
    hg_norm_w_2, conv_w_2, conv_b_2, lru_wa_2, lru_ba_2, lru_wx_2, lru_bx_2, lru_a_2, w_out_2,
    ffn_norm_w_2, w_gate_up_2, w_down_2, final_norm_w_2,
):
    x = first_block(
        x, c, w_ada, b_ada, g_mix, w_in, b_forget, g_out_a, g_out_b, w_out, g_ffn, w_group,
        b_group, w_router, b_router, w_gate, w_up, w_down, g_final,
    )
    return second_block(
        x, mix_norm_w_2, w_in_2, hg_lb_2, hg_norm_w_2, conv_w_2, conv_b_2, lru_wa_2, lru_ba_2,
        lru_wx_2, lru_bx_2, lru_a_2, w_out_2, ffn_norm_w_2, w_gate_up_2, w_down_2,
        final_norm_w_2,
    )


_drawn_inputs = setup_inputs


def setup_inputs(seed=0):
    import zlib

    import numpy as np

    out = dict(_drawn_inputs(seed))
    spreads = {}
    factors = {'g_mix': 2.753,
     'g_out_a': 8.0,
     'g_out_b': 8.0,
     'g_ffn': 7.174,
     'b_group': 8.0,
     'b_router': 8.0,
     'g_final': 15.637,
     'mix_norm_w_2': 3.579,
     'hg_norm_w_2': 24.143,
     'lru_ba_2': 55.975,
     'lru_bx_2': 40.81,
     'ffn_norm_w_2': 13.013,
     'final_norm_w_2': 7.468,
     'conv_b_2': 5.985}
    for name, (base, spread) in spreads.items():
        noise = np.random.default_rng([zlib.crc32(name.encode()), seed]).standard_normal(out[name].shape)
        drawn = base * np.exp(spread * noise) if base else spread * noise
        out[name] = __import__('jax').numpy.asarray(drawn.astype(out[name].dtype))
    for name, factor in factors.items():
        out[name] = (out[name] * factor).astype(out[name].dtype)
    return out
```

```python
from contextlib import ExitStack

import concourse.bass as bass
from concourse import mybir

F32 = mybir.dt.float32
I32 = mybir.dt.int32
U32 = mybir.dt.uint32
ALU = mybir.AluOpType
ACT = mybir.ActivationFunctionType
AX = mybir.AxisListType
ENG = mybir.EngineType

P = 128
L = 256
BLK = L // P
D = 1024
KT = D // P
EPS = 1e-6

HEADS = 8
HD = 64
SCALE = HD ** -0.5
TOPK = min(256, L // 4)
IN_COLS = 2896
AQ, AK, AV, IQ, IK, IW, BQ, BK, BV, BF = 0, 512, 640, 768, 1280, 1344, 1352, 1864, 2376, 2888
GROUPS, PER_GROUP = 4, 8
EXPERTS = GROUPS * PER_GROUP
FE = 256
PAIRS = 2 * L
WIN = 64
WINDOWS = L // WIN
COLS = PAIRS + WIN

HG = 4
CHUNK = 32
CHUNKS = L // CHUNK
CONV = 4
LRU_C = 8.0
D_FF = 2816
FT = D_FF // P

MASKED = -3.0e38
TAKEN = -3.4e38
NEG = -1.0e30
BIG = 3.0e38

SLOTS = 4
SLOT_F = KT * 776
ADA_W = 768
ADA_N = 6 * D // ADA_W
IN_CHUNKS = [(IQ, BQ), (AQ, IQ), (BK + 256, IN_COLS), (BQ, BK + 256)]
C_IN = ADA_N
ADA_FIRST = 3
FFN_STEP = 3
FFN_N = -(-FT // FFN_STEP)
DOWN_STEP = 6
DOWN_N = -(-FT // DOWN_STEP)

ORDER = ([("ada", c, 1) for c in range(ADA_FIRST)] + [("in", c, 1) for c in range(4)]
         + [("ada", c, 1) for c in range(ADA_FIRST, ADA_N)] + [("out", c, 1) for c in range(2)]
         + [("expert", e, 3) for e in range(EXPERTS)]
         + [("in2", 0, 1), ("in2", 1, 2), ("in2", 2, 1), ("in2", 3, 2)]
         + [("out2", c, 1) for c in range(2)] + [("ffn", c, 2) for c in range(FFN_N)]
         + [("down", c, 1) for c in range(DOWN_N)])
NUMBER = {(kind, c): n for n, (kind, c, _) in enumerate(ORDER)}
ARRIVED = []
_counts = [0] * SLOTS
for _n, (_, _, _dmas) in enumerate(ORDER):
    _counts[_n % SLOTS] += 16 * _dmas
    ARRIVED.append(_counts[_n % SLOTS])
EXPERT0 = NUMBER["expert", 0]
assert EXPERTS % SLOTS == 0

PA_ROWS = {}
PB_ROWS = {}
for _rows, _list in ((PA_ROWS, [("c", 8), ("b_ada", 48), ("g_mix", 8), ("g_ffn", 8), ("g_final", 8)]),
                     (PB_ROWS, [("g_out_a", 4), ("g_out_b", 4), ("mix2", 8), ("ffn2", 8), ("final2", 8),
                                ("lb0", 4), ("lb1", 4), ("hg_norm", 1), ("conv_w", 16), ("conv_b", 4),
                                ("lru_ba", 4), ("lru_bx", 4), ("lru_a", 4)])):
    _at = 0
    for _name, _k in _list:
        _rows[_name] = (_at, _at + _k)
        _at += _k
PA_N = 80
N_CONST, N_PAR, N_WR = 12, 21, 5
PB_N = 73



class Count:

    def __init__(self):
        self.n = 0

    def up(self, k=1):
        self.n += k
        return self.n


def build(nc, x, c, w_ada, b_ada, g_mix, w_in, b_forget, g_out_a, g_out_b, w_out, g_ffn, w_group,
          b_group, w_router, b_router, w_gate, w_up, w_down, g_final, mix_norm_w_2, w_in_2, hg_lb_2,
          hg_norm_w_2, conv_w_2, conv_b_2, lru_wa_2, lru_ba_2, lru_wx_2, lru_bx_2, lru_a_2, w_out_2,
          ffn_norm_w_2, w_gate_up_2, w_down_2, final_norm_w_2, out):
    with ExitStack() as ctx:
        def sb(name, shape, dt=F32):
            return ctx.enter_context(nc.sbuf_tensor(name, shape, dt))

        def sem(name):
            return ctx.enter_context(nc.semaphore(name))

        ring = sb("ring", [P, SLOTS, SLOT_F])
        xT = sb("xT", [P, KT, L])
        hT = sb("hT", [P, KT, L])
        sq = sb("sq", [P, KT, L])
        mixT = sb("mixT", [P, KT, L])
        tok = sb("tok", [P, BLK, D])
        ident = sb("ident", [P, P])
        ones = sb("ones", [P, P])
        tri = sb("tri", [P, L])
        parA = sb("parA", [P, PA_N])
        parB = sb("parB", [P, PB_N])
        mod = sb("mod", [P, 48])
        gains = sb("gains", [P, 2, KT])
        silu_c = sb("silu_c", [P, KT])
        rstd = sb("rstd", [P, 2, L])
        small = sb("small", [P, 64])
        arena = sb("arena", [P, 15760])
        wins_i = sb("wins_i", [1, WINDOWS, EXPERTS], I32)
        flag_i = sb("flag_i", [1, 1], I32)
        idx_u = sb("idx_u", [P, 2, BLK, 8], U32)

        def cut(at, *shape):
            n = 1
            for s in shape:
                n *= s
            v = arena[:, at:at + n]
            if len(shape) == 2:
                v = v.rearrange("p (a b) -> p a b", b=shape[1])
            if len(shape) == 3:
                v = v.rearrange("p (a b c) -> p a b c", b=shape[1], c=shape[2])
            return v

        qA = cut(0, 4, L)
        qI = cut(1024, 4, L)
        qB = cut(2048, 4, L)
        kB = cut(3072, 4, L)
        kA = cut(4096, L)
        kI = cut(4352, L)
        kA_swap = cut(14240, L)
        vA = cut(4608, BLK, 128)
        vB = cut(4864, BLK, 512)
        NK = P + L
        score = cut(5888, NK)
        left = cut(6272, NK)
        relu = cut(6656, 2, NK)
        sel_bias = cut(7424, NK)
        with_alibi = cut(7808, NK)
        logit = cut(8192, 2, NK)
        prob = cut(8960, 2, NK)
        probT = cut(9728, 2, NK)
        diag = cut(10496, 2, BLK, P)
        causal = cut(11008, L)
        neg_dist = cut(11264, NK)
        head_row = cut(11648, HEADS, P)
        ncumT = cut(12672, L)
        iwT = cut(12928, BLK, 8)
        cum = cut(12944, BLK, 8)
        forget = cut(12960, 3, BLK * 8)
        att_small = cut(13008, 512)
        top8 = att_small[:, 0:16].rearrange("p (b k) -> p b k", b=BLK)
        neg_max = att_small[:, 16:48].rearrange("p (n b) -> p n b", b=BLK)
        p_sum = att_small[:, 48:80].rearrange("p (n b) -> p n b", b=BLK)
        p_rsum = att_small[:, 80:112].rearrange("p (n b) -> p n b", b=BLK)

        xsT = cut(0, KT, COLS)
        ysT = cut(4608, KT, COLS)
        ys = cut(0, PAIRS // P, D)
        pick = cut(9216, BLK, PAIRS)
        pickw = cut(10240, BLK, PAIRS)
        pickwT = cut(11264, PAIRS // P, L)
        act_g = cut(12288, 2, 2 * WIN)
        act_e = cut(12544, 2, 2, WIN)
        col_no = cut(13600, PAIRS)
        strict = cut(14112, P)
        tmp_cols = cut(14240, PAIRS)
        route = cut(14752, 624)
        wr = sb("wr", [P, KT, GROUPS + EXPERTS])
        brow = sb("brow", [1, 8 + GROUPS + EXPERTS])

        n1k = HG * L
        raw_q = cut(0, HG, L)
        f_ = cut(1024, HG, L)
        k_ = cut(2048, HG, L)
        b_ = cut(3072, HG, L)
        eb = cut(4096, HG, L)
        kd = cut(5120, HG, L)
        ks = cut(6144, HG, L)
        v_ = cut(7168, BLK, 512)
        g_ = cut(8192, HG, L)
        lx = cut(9216, 4, 260)
        lg = cut(10256, 4, L)
        xc = cut(11280, 4, L)
        r_ = cut(12304, 4, L)
        ig = cut(13328, 4, L)
        a_ = cut(14352, 4, L)
        th = cut(9216, 4, L)
        reset = cut(15376, L)
        in_chunk = cut(15632, P)
        ksT = b_.rearrange("p h t -> p (h t)").rearrange("p (b n) -> p b n", b=BLK)
        sc_ = f_.rearrange("p h t -> p (h t)").rearrange("p (b h t) -> p b h t", b=BLK, h=HG)
        o_ = kd
        gate_w = mixT[:, 0:4, :].rearrange("p a b -> p (a b)").rearrange("p (g j n) -> p g j n", g=2, j=4)
        ffn = cut(0, FT, L)
        silu_t = cut(5632, 2, L)

        sqf = sq[:].rearrange("p k t -> p (k t)")
        tokf = tok[:].rearrange("p b d -> p (b d)")

        def state(ch):
            return tokf[:, (ch - 1) * 512:ch * 512] if ch <= 4 else sqf[:, (ch - 5) * 512:(ch - 4) * 512]

        def piece(at, *shape):
            n = 1
            for v in shape:
                n *= v
            v = route[:, at:at + n]
            return v.rearrange("p (a b) -> p a b", b=shape[1]) if len(shape) == 2 else (
                v.rearrange("p (a b c) -> p a b c", b=shape[1], c=shape[2]) if len(shape) == 3 else v)

        g8 = piece(0, BLK, 8)
        g_top = piece(16, BLK, 8)
        e_log = piece(32, BLK, EXPERTS)
        e_top = piece(96, BLK, 8)
        R_one = piece(112, 2, BLK * EXPERTS)
        R_chosen = piece(240, BLK, EXPERTS)
        counts = piece(304, EXPERTS)
        upto = piece(336, EXPERTS)
        starts_f = piece(368, EXPERTS)
        place = piece(400, BLK, EXPERTS)
        g_one = piece(464, BLK, GROUPS)
        g_pen = piece(472, BLK, GROUPS)
        cols = piece(480, 2, BLK)
        e_idx = piece(484, BLK, 2)
        g_idx = piece(488, BLK)
        g_sum = piece(490, BLK)
        e_diff = piece(492, BLK)
        w_top = piece(494, 2, BLK)
        wins_f = piece(498, EXPERTS)
        most = piece(530, 1)
        lb = small[:, 0:4]
        one_lb = small[:, 4:8]
        lru_c = small[:, 8:12]
        lru_nc = small[:, 12:16]
        t4 = small[:, 16:20]
        u4 = small[:, 20:24]
        t8 = small[:, 24:32]
        m4 = small[:, 32:36]

        ps = ctx.enter_context(nc.psum_tensor("ps", [P, 8, 512], F32))

        arrived = [sem(f"arrived{i}") for i in range(SLOTS)]
        chunk_used = sem("chunk_used")
        x_there, par_there, wr_there, lru_there = sem("x_there"), sem("par_there"), sem("wr_there"), sem("lru_there")
        consts_ready = sem("consts_ready")
        pool_step, dve_step, act_step = sem("pool_step"), sem("dve_step"), sem("act_step")
        par_tr, par_taken = sem("par_tr"), sem("par_taken")
        xT_tr, xT_ready = sem("xT_tr"), sem("xT_ready")
        silu_c_ready, ada_done, mod_ready = sem("silu_c_ready"), sem("ada_done"), sem("mod_ready")
        sq_ready = [sem(f"sq_ready{i}") for i in range(7)]
        ssq_ready = [sem(f"ssq_ready{i}") for i in range(7)]
        std_ready = [sem(f"std_ready{i}") for i in range(7)]
        scaled = [sem(f"scaled{i}") for i in range(6)]
        h_ready = [sem(f"h_ready{i}") for i in range(2)]
        tile_ready, tile_taken = sem("tile_ready"), sem("tile_taken")
        dots_ready, dots_taken, relu_used = sem("dots_ready"), sem("dots_taken"), sem("relu_used")
        score_raw, score_masked = sem("score_raw"), sem("score_masked")
        sel_raw, sel_ready = sem("sel_raw"), sem("sel_ready")
        forget_abs, forget_ln, log_f_ready = sem("forget_abs"), sem("forget_ln"), sem("log_f_ready")
        cum_done, cum_taken = sem("cum_done"), sem("cum_taken")
        logits_done, logits_taken, logits_ready = sem("logits_done"), sem("logits_taken"), sem("logits_ready")
        probs_ready, diag_ready = sem("probs_ready"), sem("diag_ready")
        pt_done, pt_taken, pv_done, pv_taken = sem("pt_done"), sem("pt_taken"), sem("pv_done"), sem("pv_taken")
        mix_ready = sem("mix_ready")
        mo_done, mo_taken = sem("mo_done"), sem("mo_taken")
        route_done, gate_max, gate_exp = sem("route_done"), sem("gate_max"), sem("gate_exp")
        top_diff, top_exp = sem("top_diff"), sem("top_exp")
        htr_done, htr_taken_a, htr_taken_v = sem("htr_done"), sem("htr_taken_a"), sem("htr_taken_v")
        choice_ready, rank_done, pick_ready, windows_ready = sem("choice_ready"), sem("rank_done"), sem("pick_ready"), sem("windows_ready")
        pickw_ready, pickwT_done, pickwT_taken = sem("pickw_ready"), sem("pickwT_done"), sem("pickwT_taken")
        gather_done, gather_taken_a, gather_taken_v = sem("gather_done"), sem("gather_taken_a"), sem("gather_taken_v")
        k_moved = sem("k_moved")
        pad_ready, ys_complete = sem("pad_ready"), sem("ys_complete")
        gu_done, silu_done, act_ready, y_taken = sem("gu_done"), sem("silu_done"), sem("act_ready"), sem("y_taken")
        w_gu_done, w_silu_done, w_act_ready, w_y_done, w_y_taken = (
            sem("w_gu_done"), sem("w_silu_done"), sem("w_act_ready"), sem("w_y_done"), sem("w_y_taken"))
        ytr_done, ytr_taken_a, ytr_taken_v = sem("ytr_done"), sem("ytr_taken_a"), sem("ytr_taken_v")
        comb_done, comb_taken = sem("comb_done"), sem("comb_taken")
        u2_done, u2_taken = sem("u2_done"), sem("u2_taken")
        f_sig, f_ready, f_ln, b_ready = sem("f_sig"), sem("f_ready"), sem("f_ln"), sem("b_ready")
        decay_ready, last_diff, last_exp = sem("decay_ready"), sem("last_diff"), sem("last_exp")
        q_sig, kd_ready, ks_ready, qd_ready = sem("q_sig"), sem("kd_ready"), sem("ks_ready"), sem("qd_ready")
        kst_done, kst_taken, hsc_done, hsc_ready = sem("kst_done"), sem("kst_taken"), sem("hsc_done"), sem("hsc_ready")
        kv_done, o_done, o_taken, o_sq = sem("kv_done"), sem("o_done"), sem("o_taken"), sem("o_sq")
        o_ssq, g_sig, sg_ready = sem("o_ssq"), sem("g_sig"), sem("sg_ready")
        xc_ready, gates_done, gates_ready, decays_ready = sem("xc_ready"), sem("gates_done"), sem("gates_ready"), sem("decays_ready")
        o_std, half_power, power_root = sem("o_std"), sem("half_power"), sem("power_root")
        gelu_in, gelu_sig, lru_par = sem("gelu_in"), sem("gelu_sig"), sem("lru_par")
        lru_par_a = sem("lru_par_a")
        state_ready = sem("state_ready")
        mix2_ready = sem("mix2_ready")
        ffn_done, ffn_silu, ffn_taken = sem("ffn_done"), sem("ffn_silu"), sem("ffn_taken")
        down_done, down_taken = sem("down_done"), sem("down_taken")
        otr_done, otr_taken_a, otr_taken_v, stored = sem("otr_done"), sem("otr_taken_a"), sem("otr_taken_v"), sem("stored")

        block = ctx.enter_context(nc.Block())

        def slot(n):
            return ring[:, n % SLOTS, :]

        def weights(kind, c, k, n):
            return slot(NUMBER[kind, c])[:, 0:k * n].rearrange("p (k n) -> p k n", n=n)

        def expert_weights(s):
            v = ring[:, s, :]
            return (v[:, 0:KT * FE].rearrange("p (k n) -> p k n", n=FE),
                    v[:, KT * FE:2 * KT * FE].rearrange("p (k n) -> p k n", n=FE),
                    v[:, 2 * KT * FE:3 * KT * FE].rearrange("p (k n) -> p k n", n=D))

        @block.sync
        def _(sp):
            def free(n):
                if n >= SLOTS:
                    sp.wait_ge(chunk_used, n - SLOTS + 1)

            def load_ada(c):
                n = NUMBER["ada", c]
                free(n)
                sp.dma_start(weights("ada", c, KT, ADA_W),
                             w_ada[0].rearrange("(k p) n -> p k n", p=P)[:, :, c * ADA_W:(c + 1) * ADA_W]
                             ).then_inc(arrived[n % SLOTS], 16)

            for ch in range(ADA_FIRST):
                load_ada(ch)
            for ch, (lo, hi) in enumerate(IN_CHUNKS):
                n = NUMBER["in", ch]
                free(n)
                sp.dma_start(weights("in", ch, KT, hi - lo),
                             w_in[0].rearrange("(k p) n -> p k n", p=P)[:, :, lo:hi]
                             ).then_inc(arrived[n % SLOTS], 16)
            for ch in range(ADA_FIRST, ADA_N):
                load_ada(ch)
            for ch in range(2):
                n = NUMBER["out", ch]
                free(n)
                sp.dma_start(weights("out", ch, KT, 512),
                             w_out[0].rearrange("(k p) n -> p k n", p=P)[:, :, ch * 512:ch * 512 + 512]
                             ).then_inc(arrived[n % SLOTS], 16)
            gate_d = w_gate[0].rearrange("e (p k) f -> p e (k f)", k=KT)
            up_d = w_up[0].rearrange("e (p k) f -> p e (k f)", k=KT)
            down_d = w_down[0].rearrange("e (k p) d -> p e k d", p=P)
            with sp.Fori(0, EXPERTS // SLOTS) as i:
                for u in range(SLOTS):
                    s = (EXPERT0 + u) % SLOTS
                    g, up, dn = expert_weights(s)
                    sp.wait_ge(chunk_used, i * SLOTS + (EXPERT0 + u - SLOTS + 1))
                    e = bass.ds(i * SLOTS + u, 1)
                    sp.dma_start(g.rearrange("p k n -> p (k n)"), gate_d[:, e, :].rearrange("p e f -> p (e f)")
                                 ).then_inc(arrived[s], 16)
                    sp.dma_start(up.rearrange("p k n -> p (k n)"), up_d[:, e, :].rearrange("p e f -> p (e f)")
                                 ).then_inc(arrived[s], 16)
                    sp.dma_start(dn, down_d[:, e, :, :].rearrange("p e k d -> p (e k) d")
                                 ).then_inc(arrived[s], 16)
            in2 = w_in_2[0].rearrange("(k p) n -> p k n", p=P)
            for ch, parts in enumerate([[(256, 1024)], [(0, 256), (1024, 1536)], [(2048, 2816)],
                                        [(2816, 3072), (1536, 2048)]]):
                n = NUMBER["in2", ch]
                free(n)
                w, at = weights("in2", ch, KT, 768), 0
                for lo, hi in parts:
                    sp.dma_start(w[:, :, at:at + hi - lo], in2[:, :, lo:hi]).then_inc(arrived[n % SLOTS], 16)
                    at += hi - lo
            for ch in range(2):
                n = NUMBER["out2", ch]
                free(n)
                sp.dma_start(weights("out2", ch, KT, 512),
                             w_out_2[0].rearrange("(k p) n -> p k n", p=P)[:, :, ch * 512:ch * 512 + 512]
                             ).then_inc(arrived[n % SLOTS], 16)
            gu = w_gate_up_2[0].rearrange("(k p) n -> p k n", p=P)
            for ch in range(FFN_N):
                n = NUMBER["ffn", ch]
                free(n)
                k = min(FFN_STEP, FT - ch * FFN_STEP) * P
                w = weights("ffn", ch, KT, 2 * k)
                for half in range(2):
                    lo = half * D_FF + ch * FFN_STEP * P
                    sp.dma_start(w[:, :, half * k:(half + 1) * k], gu[:, :, lo:lo + k]
                                 ).then_inc(arrived[n % SLOTS], 16)
            for ch in range(DOWN_N):
                n = NUMBER["down", ch]
                free(n)
                k = min(DOWN_STEP, FT - ch * DOWN_STEP)
                sp.dma_start(weights("down", ch, k, D),
                             w_down_2[0, ch * DOWN_STEP * P:(ch * DOWN_STEP + k) * P].rearrange(
                                 "(k p) n -> p k n", p=P)).then_inc(arrived[n % SLOTS], 16)
            for b in range(BLK):
                sp.wait_ge(otr_taken_a, b + 1)
                sp.wait_ge(otr_taken_v, b + 1)
                sp.dma_start(out[0, b * P:(b + 1) * P, :], tok[:, b, :]).then_inc(stored, 16)
            sp.wait_ge(stored, 16 * BLK)

        @block.gpsimd
        def _(pool):
            step = Count()
            pool.memset(ident[:], 0.0).then_inc(pool_step, 1)
            pool.memset(ones[:], 1.0).then_inc(consts_ready, 1)
            pool.memset(tri[:], 1.0).then_inc(pool_step, 1)
            pool.memset(causal[:], 0.0).then_inc(pool_step, 1)
            pool.memset(head_row[:], 1.0).then_inc(pool_step, 1)
            pool.memset(strict[:], 1.0).then_inc(pool_step, 1)
            pool.memset(reset[:], 1.0).then_inc(pool_step, 1)
            pool.memset(ncumT[:], 0.0).then_inc(consts_ready, 1)
            pool.memset(in_chunk[:], 1.0).then_inc(pool_step, 1)
            pool.wait_ge(pool_step, step.up(7))
            pool.affine_select(out=ident[:], in_=ident[:], compare_op=ALU.not_equal, fill=1.0, base=0,
                               pattern=[[-1, P]], channel_multiplier=1).then_inc(consts_ready, 1)
            pool.affine_select(out=tri[:], in_=tri[:], compare_op=ALU.is_ge, fill=0.0, base=0,
                               pattern=[[1, L]], channel_multiplier=-1).then_inc(consts_ready, 1)
            pool.affine_select(out=causal[:, P:L], in_=causal[:, P:L], compare_op=ALU.is_ge, fill=NEG, base=0,
                               pattern=[[-1, P]], channel_multiplier=1).then_inc(consts_ready, 1)
            pool.affine_select(out=head_row[:], in_=head_row[:], compare_op=ALU.is_equal, fill=0.0,
                               base=0, pattern=[[1, HEADS], [0, P]], channel_multiplier=-1
                               ).then_inc(consts_ready, 1)
            pool.affine_select(out=strict[:], in_=strict[:], compare_op=ALU.is_gt, fill=0.0, base=0,
                               pattern=[[1, P]], channel_multiplier=-1).then_inc(consts_ready, 1)
            pool.affine_select(out=in_chunk[:], in_=in_chunk[:], compare_op=ALU.is_ge, fill=0.0, base=0,
                               pattern=[[1, P]], channel_multiplier=-1).then_inc(pool_step, 1)
            pool.wait_ge(pool_step, step.up())
            pool.affine_select(out=in_chunk[:], in_=in_chunk[:], compare_op=ALU.is_ge, fill=0.0, base=0,
                               pattern=[[-CHUNK, P // CHUNK], [0, CHUNK]], channel_multiplier=1
                               ).then_inc(consts_ready, 1)
            pool.memset(reset[:, 0:L:CHUNK], 0.0).then_inc(consts_ready, 1)
            pool.iota(neg_dist[:, 0:P], [[1, P]], base=0, channel_multiplier=-1,
                      allow_small_or_imprecise_dtypes=True).then_inc(consts_ready, 1)
            pool.iota(neg_dist[:, P:NK], [[1, L]], base=-P, channel_multiplier=-1,
                      allow_small_or_imprecise_dtypes=True).then_inc(consts_ready, 1)
            pool.iota(col_no[:], [[1, PAIRS]], base=0, channel_multiplier=0,
                      allow_small_or_imprecise_dtypes=True).then_inc(consts_ready, 1)

            def behind(t, fill, inc):
                pool.affine_select(out=t[:, 0:P], in_=t[:, 0:P], compare_op=ALU.is_ge, fill=fill, base=0,
                                   pattern=[[-1, P]], channel_multiplier=1).then_inc(inc, 1)
                pool.affine_select(out=t[:, P:NK], in_=t[:, P:NK], compare_op=ALU.is_ge, fill=fill, base=P,
                                   pattern=[[-1, L]], channel_multiplier=1).then_inc(inc, 1)

            pool.wait_ge(tile_taken, 2)
            pool.dma_start(kI[64:128, :], kI[0:64, :]).then_inc(k_moved, 16)
            pool.wait_ge(tile_taken, 7)
            pool.dma_start(kA_swap[64:128, :], kA[0:64, :]).then_inc(k_moved, 16)
            pool.dma_start(kA_swap[0:64, :], kA[64:128, :]).then_inc(k_moved, 16)
            pool.wait_ge(score_raw, 2 * HEADS)
            behind(score, MASKED, score_masked)
            pool.wait_ge(sel_raw, 1)
            behind(sel_bias, NEG, sel_ready)
            pool.wait_ge(mo_taken, KT)
            pool.memset(xsT[:, :, PAIRS:COLS], 0.0).then_inc(pad_ready, 1)
            pool.memset(gate_w[:], 0.0).then_inc(pool_step, 1)
            pool.wait_ge(pool_step, step.up())
            for g, w in enumerate((lru_wa_2, lru_wx_2)):
                for odd in range(2):
                    q = slice(64 * odd, 64 * odd + 64)
                    pool.dma_start(gate_w[q, g, :, q], w[0].rearrange("(j o) d e -> o d j e", o=2)[odd]
                                   ).then_inc(lru_there, 16)

        @block.tensor
        def _(pe):
            def chunk_there(kind, c):
                n = NUMBER[kind, c]
                pe.wait_ge(arrived[n % SLOTS], ARRIVED[n])

            def sum_squares(i, bank, col=0, tiles=range(KT), n=L):
                for k in tiles:
                    last = pe.matmul(ps[:, bank, col:col + n], lhsT=ones[:], rhs=sq[:, k, :],
                                     start=k == tiles[0], stop=k == tiles[-1])
                last.then_inc(ssq_ready[i], 1)

            def product(o, w_of, rhs_of, k_n=KT):
                for k in range(k_n):
                    last = pe.matmul(o, lhsT=w_of(k), rhs=rhs_of(k), start=k == 0, stop=k == k_n - 1)
                return last

            pe.wait_ge(consts_ready, N_CONST)
            pe.wait_ge(par_there, 16 * N_PAR)
            pe.transpose(ps[:, 2, 0:PA_N], hT[0:PA_N, 0, 0:P], ident[0:PA_N, 0:PA_N]).then_inc(par_tr, 1)
            pe.transpose(ps[:, 3, 0:PB_N], hT[0:PB_N, 1, 0:P], ident[0:PB_N, 0:PB_N]).then_inc(par_tr, 1)
            pe.wait_ge(x_there, 16)
            for q, bank in enumerate((0, 1, 4, 5)):
                for k in (2 * q, 2 * q + 1):
                    for b in range(BLK):
                        at = (k % 2) * L + b * P
                        last = pe.transpose(ps[:, bank, at:at + P], tok[:, b, k * P:(k + 1) * P], ident[:])
                last.then_inc(xT_tr, 1)

            def ada(lo, hi):
                for m in range(lo, hi):
                    ch, i = divmod(m, ADA_W // P)
                    if i == 0:
                        chunk_there("ada", ch)
                    w = weights("ada", ch, KT, ADA_W)
                    last = product(ps[:, 7, m:m + 1], lambda k: w[:, k, i * P:(i + 1) * P],
                                   lambda k: silu_c[:, k:k + 1])
                    if i == ADA_W // P - 1:
                        last.then_inc(chunk_used, 1)

            pe.wait_ge(sq_ready[0], 2)
            sum_squares(0, 6)
            pe.wait_ge(silu_c_ready, 1)
            ada(0, ADA_FIRST * ADA_W // P)

            unit = Count()

            def bank_of_unit():
                u = unit.up() - 1
                if u >= 2:
                    pe.wait_ge(tile_taken, u - 1)
                return ps[:, u % 2, :]

            def features(ch, cols):
                w = weights("in", ch, KT, IN_CHUNKS[ch][1] - IN_CHUNKS[ch][0])
                o = bank_of_unit()
                return product(o[:, 0:L], lambda k: cols(w[:, k, :]), lambda k: hT[:, k, :])

            def tokens(ch, lo, hi, blocks, bias=None):
                w = weights("in", ch, KT, IN_CHUNKS[ch][1] - IN_CHUNKS[ch][0])
                o, n = bank_of_unit(), hi - lo
                for i, b in enumerate(blocks):
                    for k in range(KT):
                        last = pe.matmul(o[:, i * n:(i + 1) * n], lhsT=hT[:, k, b * P:(b + 1) * P],
                                         rhs=w[:, k, lo:hi], start=k == 0, stop=k == KT - 1 and bias is None)
                    if bias is not None:
                        last = pe.matmul(o[:, i * n:(i + 1) * n], lhsT=ones[0:1, :], rhs=bias,
                                         start=False, stop=True)
                return last

            pe.wait_ge(h_ready[0], KT)
            chunk_there("in", 0)
            tokens(0, IW - IQ, BQ - IQ, (0, 1)).then_inc(tile_ready, 1)
            ik = IK - IQ
            w = weights("in", 0, KT, BQ - IQ)
            product(bank_of_unit()[0:64, 0:L], lambda k: w[:, k, ik:ik + 64], lambda k: hT[:, k, :]
                    ).then_inc(tile_ready, 1)
            for j in range(4):
                last = features(0, lambda w: w[:, j * P:(j + 1) * P]).then_inc(tile_ready, 1)
            pe.wait_ge(tile_taken, 6)
            pe.sem_inc(chunk_used, 1)

            def dots(h):
                bank, q = 2 + h % 2, slice(64 * (h % 2), 64 * (h % 2) + 64)
                if h >= 2:
                    pe.wait_ge(dots_taken, h - 1)
                pe.matmul(ps[:, bank, 0:P], lhsT=qI[q, h // 2, 0:P], rhs=kI[q, 0:P], start=True, stop=True)
                pe.matmul(ps[:, bank, P:NK], lhsT=qI[q, h // 2, P:L], rhs=kI[q, :],
                          start=True, stop=True).then_inc(dots_ready, 1)

            pe.wait_ge(par_taken, 2)
            pe.wait_ge(k_moved, 16)
            chunk_there("in", 1)
            dots(0)
            dots(1)
            features(1, lambda w: w[:, AK:AV]).then_inc(tile_ready, 1)
            dots(2)
            dots(3)
            tokens(1, AV, IQ, (0, 1)).then_inc(tile_ready, 1)
            for j in range(4):
                if j < 2:
                    dots(4 + 2 * j)
                    dots(5 + 2 * j)
                features(1, lambda w: w[:, j * P:(j + 1) * P]).then_inc(tile_ready, 1)
            pe.wait_ge(tile_ready, 12)
            pe.sem_inc(chunk_used, 1)

            def head(n):
                if n < HEADS:
                    kv, half = n // 4, n % 2
                    q = slice(64 * half, 64 * half + 64)
                    return q, qA[q, n // 2, :], (kA if kv == half else kA_swap)[q, :], vA[:, :, 64 * kv:64 * kv + 64]
                h = n - HEADS
                q = slice(64 * (h % 2), 64 * (h % 2) + 64)
                return q, qB[q, h // 2, :], kB[q, h // 2, :], vB[:, :, h * 64:(h + 1) * 64]

            def attend(n):
                if n < 2 * HEADS:
                    _, q, k, _ = head(n)
                    bank, more = 2 + n % 2, n >= HEADS
                    if n >= 2:
                        pe.wait_ge(logits_taken, n - 1)
                    else:
                        pe.wait_ge(dots_taken, HEADS)
                    for o, qb, keys in ((ps[:, bank, 0:P], 0, slice(0, P)), (ps[:, bank, P:NK], 1, slice(0, L))):
                        last = pe.matmul(o, lhsT=q[:, qb * P:(qb + 1) * P], rhs=k[:, keys], start=True,
                                         stop=not more)
                        if more:
                            last = pe.matmul(o, lhsT=head_row[:, n - HEADS, :], rhs=ncumT[:, keys],
                                             start=False, stop=True)
                    last.then_inc(logits_done, 1)
                if 1 <= n <= 2 * HEADS:
                    m = n - 1
                    bank = 4 + m % 2
                    pe.wait_ge(diag_ready, m + 1)
                    if m >= 2:
                        pe.wait_ge(pt_taken, m - 1)
                    for s in range(3):
                        last = pe.matmul(ps[:, bank, s * P:(s + 1) * P], lhsT=prob[:, m % 2, s * P:(s + 1) * P],
                                         rhs=diag[:, m % 2, min(s, 1), :], start=True, stop=True)
                    last.then_inc(pt_done, 1)
                if 2 <= n:
                    m = n - 2
                    q, _, _, v = head(m)
                    pe.wait_ge(pt_taken, m + 1)
                    if m % 2 == 0 and m:
                        pe.wait_ge(pv_taken, m // 2)
                    pe.matmul(ps[q, 6, 0:L], lhsT=v[:, 0, :], rhs=probT[:, m % 2, 0:L], start=True, stop=False)
                    pe.matmul(ps[q, 6, P:L], lhsT=v[:, 1, :], rhs=probT[:, m % 2, L:NK], start=False,
                              stop=True).then_inc(pv_done, 1)

            def bq(j):
                features(3, lambda w: w[:, j * P:(j + 1) * P]).then_inc(tile_ready, 1)

            pe.wait_ge(k_moved, 48)
            attend(0)
            chunk_there("in", 2)
            tokens(2, BF - BK - 256, BF - BK - 256 + 8, (0, 1), bias=brow[0:1, 0:8]).then_inc(tile_ready, 1)
            features(2, lambda w: w[:, 0:P]).then_inc(tile_ready, 1)
            attend(1)
            features(2, lambda w: w[:, P:2 * P]).then_inc(tile_ready, 1)
            attend(2)
            tokens(2, BV - BK - 256, BF - BK - 256, (0,)).then_inc(tile_ready, 1)
            attend(3)
            tokens(2, BV - BK - 256, BF - BK - 256, (1,)).then_inc(tile_ready, 1)
            pe.wait_ge(tile_ready, 17)
            pe.sem_inc(chunk_used, 1)
            attend(4)
            chunk_there("in", 3)
            bq(0)
            bq(1)
            attend(5)
            bq(2)
            bq(3)
            pe.wait_ge(log_f_ready, 1)
            pe.wait_ge(mod_ready, 1)
            lf = forget[:, 2, :].rearrange("p (b h) -> p b h", b=BLK)
            pe.matmul(ps[:, 7, 64:72], lhsT=tri[:, 0:P], rhs=lf[:, 0, :], start=True, stop=True)
            pe.matmul(ps[:, 7, 72:80], lhsT=ones[:], rhs=lf[:, 0, :], start=True, stop=False)
            pe.matmul(ps[:, 7, 72:80], lhsT=tri[:, 0:P], rhs=lf[:, 1, :], start=False, stop=True)
            pe.matmul(ps[0:HEADS, 7, 128:384], lhsT=lf[:, 0, :], rhs=tri[:], start=True, stop=False)
            pe.matmul(ps[0:HEADS, 7, 256:384], lhsT=lf[:, 1, :], rhs=tri[:, 0:P], start=False,
                      stop=True).then_inc(cum_done, 1)
            attend(6)
            bq(4)
            attend(7)
            bq(5)
            pe.wait_ge(tile_taken, 23)
            pe.sem_inc(chunk_used, 1)
            pe.wait_ge(cum_taken, 2)
            m0 = ADA_FIRST * ADA_W // P
            for n in range(HEADS, 2 * HEADS + 2):
                attend(n)
                ada(m0, m0 + 3)
                m0 += 3

            pe.wait_ge(sq_ready[5], 2)
            sum_squares(5, 6, 0, range(4))
            sum_squares(5, 6, L, range(4, 8))
            pe.wait_ge(mix_ready, KT)
            for m in range(KT):
                ch, i = divmod(m, 4)
                if i == 0:
                    chunk_there("out", ch)
                w = weights("out", ch, KT, 512)
                if m >= 4:
                    pe.wait_ge(mo_taken, m - 3)
                product(ps[:, m % 4, 0:L], lambda k: w[:, k, i * P:(i + 1) * P],
                        lambda k: mixT[:, k, :]).then_inc(mo_done, 1)
                if i == 3:
                    pe.wait_ge(mo_done, m + 1)
                    pe.sem_inc(chunk_used, 1)

            pe.wait_ge(sq_ready[1], 2)
            sum_squares(1, 6)
            pe.wait_ge(wr_there, 16 * N_WR)
            pe.wait_ge(h_ready[1], KT)
            nr = GROUPS + EXPERTS
            for b in range(BLK):
                for k in range(KT):
                    pe.matmul(ps[:, 4, b * nr:(b + 1) * nr], lhsT=hT[:, k, b * P:(b + 1) * P], rhs=wr[:, k, :],
                              start=k == 0, stop=False)
                last = pe.matmul(ps[:, 4, b * nr:(b + 1) * nr], lhsT=ones[0:1, :], rhs=brow[0:1, 8:8 + nr],
                                 start=False, stop=True)
            last.then_inc(route_done, 1)
            pe.wait_ge(mo_taken, KT)
            for i in range(4):
                b, half = divmod(i, 2)
                for k in range(4):
                    last = pe.transpose(ps[:, i, k * P:(k + 1) * P], hT[:, 4 * half + k, b * P:(b + 1) * P], ident[:])
                last.then_inc(htr_done, 1)
            pe.wait_ge(choice_ready, 1)
            pe.matmul(ps[:, 5, 0:32], lhsT=strict[:], rhs=R_chosen[:, 0, :], start=True, stop=True)
            pe.matmul(ps[:, 5, 32:64], lhsT=ones[:], rhs=R_chosen[:, 0, :], start=True, stop=False)
            pe.matmul(ps[:, 5, 32:64], lhsT=strict[:], rhs=R_chosen[:, 1, :], start=False, stop=True)
            pe.matmul(ps[:, 5, 64:96], lhsT=ones[:], rhs=R_chosen[:, 0, :], start=True, stop=False)
            pe.matmul(ps[:, 5, 64:96], lhsT=ones[:], rhs=R_chosen[:, 1, :], start=False,
                      stop=True).then_inc(rank_done, 1)
            pe.wait_ge(pick_ready, BLK)
            pe.wait_ge(htr_taken_a, 4)
            for j in range(KT):
                if j >= 4:
                    if j % 2 == 0:
                        pe.wait_ge(gather_taken_a, (j - 4) // 2 + 1)
                    else:
                        pe.wait_ge(gather_taken_v, (j - 4) // 2 + 1)
                for b in range(BLK):
                    last = pe.matmul(ps[:, j % 4, :], lhsT=tok[:, b, j * P:(j + 1) * P], rhs=pick[:, b, :],
                                     start=b == 0, stop=b == BLK - 1)
                last.then_inc(gather_done, 1)
            pe.wait_ge(pickw_ready, BLK)
            for s in range(PAIRS // P):
                for b in range(BLK):
                    at = (s % 2) * L + b * P
                    last = pe.transpose(ps[:, 6 + s // 2, at:at + P], pickw[:, b, s * P:(s + 1) * P], ident[:])
            last.then_inc(pickwT_done, 1)

            def gate_up(s, bank, start):
                g, up, _ = expert_weights(s)
                for i, w in enumerate((g, up)):
                    for f in range(2):
                        at = (2 * i + f) * WIN
                        last = product(ps[:, bank, at:at + WIN], lambda k: w[:, k, f * P:(f + 1) * P],
                                       lambda k: xsT[:, k, bass.ds(start, WIN)])
                return last

            def down(s, bank, a):
                _, _, dn = expert_weights(s)
                for j in range(KT):
                    last = product(ps[:, bank, j * WIN:(j + 1) * WIN], lambda k: dn[:, k, j * P:(j + 1) * P],
                                   lambda k: a[:, k, :], k_n=2)
                return last

            pe.wait_ge(gather_taken_a, 4)
            pe.wait_ge(gather_taken_v, 4)
            pe.wait_ge(pad_ready, 1)
            pe.wait_ge(windows_ready, 2)
            too_many = pe.value_load(flag_i[0:1, 0:1], min_val=0, max_val=1)
            with pe.If(too_many < 1):
                with pe.Fori(0, EXPERTS // SLOTS) as i:
                    _, starts = nc.values_load_multi_w_load_instructions(
                        wins_i[0:1, 0, bass.ds(i * SLOTS, SLOTS)], engines=(ENG.PE,), min_val=0, max_val=PAIRS)

                    def first(u):
                        s = (EXPERT0 + u) % SLOTS
                        pe.wait_ge(arrived[s], i * 48 + ARRIVED[EXPERT0 + u])
                        pe.wait_ge(act_ready, i * SLOTS + u + 1)
                        gate_up(s, u % 2, starts[u]).then_inc(gu_done, 1)

                    def second(u):
                        s = (EXPERT0 + u) % SLOTS
                        pe.wait_ge(act_ready, i * SLOTS + u + 3)
                        pe.wait_ge(y_taken, i * SLOTS + u + 1)
                        down(s, 2 + u % 2, act_e[:, u % 2]).then_inc(chunk_used, 1)

                    first(0)
                    for u in range(SLOTS):
                        if u + 1 < SLOTS:
                            first(u + 1)
                        second(u)
            with pe.Else():
                with pe.Fori(0, EXPERTS // SLOTS) as i:
                    for u in range(SLOTS):
                        s = (EXPERT0 + u) % SLOTS
                        with pe.Fori(0, WINDOWS) as w:
                            start = pe.value_load(
                                wins_i[:].rearrange("o w e -> o (w e)")[0:1, bass.ds(w * EXPERTS + i * SLOTS + u, 1)],
                                min_val=0, max_val=PAIRS)
                            done = i * (SLOTS * WINDOWS) + w + u * WINDOWS
                            pe.wait_ge(arrived[s], i * 48 + ARRIVED[EXPERT0 + u])
                            pe.wait_ge(w_y_taken, done + 1)
                            gate_up(s, 0, start).then_inc(w_gu_done, 1)
                            pe.wait_ge(w_act_ready, done + 1)
                            down(s, 2, act_e[:, 0]).then_inc(w_y_done, 1)
                        pe.wait_ge(w_y_done, (i * SLOTS + u + 1) * WINDOWS)
                        pe.sem_inc(chunk_used, 1)
            pe.wait_ge(chunk_used, EXPERT0 + EXPERTS)
            for i in range(8):
                s, half = divmod(i, 2)
                if i >= 4:
                    if i % 2 == 0:
                        pe.wait_ge(ytr_taken_a, (i - 4) // 2 + 1)
                    else:
                        pe.wait_ge(ytr_taken_v, (i - 4) // 2 + 1)
                else:
                    pe.wait_ge(ys_complete, 1)
                for k in range(4):
                    last = pe.transpose(ps[:, i % 4, k * P:(k + 1) * P], ysT[:, 4 * half + k, s * P:(s + 1) * P],
                                        ident[:])
                last.then_inc(ytr_done, 1)
            pe.wait_ge(ytr_taken_a, 4)
            pe.wait_ge(ytr_taken_v, 4)
            pe.wait_ge(pickwT_taken, 2)
            for j in range(KT):
                if j >= 4:
                    pe.wait_ge(comb_taken, j - 3)
                product(ps[:, 4 + j % 4, 0:L], lambda s: ys[:, s, j * P:(j + 1) * P],
                        lambda s: pickwT[:, s, :], k_n=PAIRS // P).then_inc(comb_done, 1)

            pe.wait_ge(sq_ready[2], 2)
            sum_squares(2, 6)
            pe.wait_ge(sq_ready[3], 2)
            sum_squares(3, 6)
            unit2 = Count()

            def bank2():
                u = unit2.up() - 1
                if u >= 4:
                    pe.wait_ge(u2_taken, u - 3)
                return ps[:, u % 4, :]

            def features2(ch, lo):
                w = weights("in2", ch, KT, 768)
                product(bank2()[:, 0:L], lambda k: w[:, k, lo:lo + P], lambda k: hT[:, k, :]).then_inc(u2_done, 1)

            def chunk2_used(units):
                pe.wait_ge(u2_done, units)
                pe.sem_inc(chunk_used, 1)

            pe.wait_ge(scaled[3], KT)
            chunk_there("in2", 0)
            for i in range(6):
                features2(0, i * P)
            chunk2_used(6)
            chunk_there("in2", 1)
            features2(1, 0)
            features2(1, P)
            w = weights("in2", 1, KT, 768)
            for b in range(BLK):
                product(bank2(), lambda k: hT[:, k, b * P:(b + 1) * P], lambda k: w[:, k, 256:768]).then_inc(u2_done, 1)
            chunk2_used(10)
            chunk_there("in2", 2)
            for i in range(6):
                features2(2, i * P)
            chunk2_used(16)

            pe.wait_ge(ks_ready, 1)
            for b in range(BLK):
                for h in range(HG):
                    last = pe.transpose(ps[:, 4 + b, h * P:(h + 1) * P], ks[:, h, b * P:(b + 1) * P], ident[:])
                last.then_inc(kst_done, 1)
            pe.wait_ge(kd_ready, 1)
            pe.wait_ge(qd_ready, 1)
            for b in range(BLK):
                t = slice(b * P, (b + 1) * P)
                for h in range(HG):
                    last = pe.matmul(ps[:, 6 + b, h * P:(h + 1) * P], lhsT=kd[:, h, t], rhs=raw_q[:, h, t],
                                     start=True, stop=True)
                last.then_inc(hsc_done, 1)
            chunk_there("in2", 3)
            features2(3, 0)
            features2(3, P)
            pe.wait_ge(kst_taken, 2)
            pe.wait_ge(hsc_ready, 2)
            for ch in range(CHUNKS - 1):
                b, r = divmod(ch, P // CHUNK)
                rows = slice(CHUNK * r, CHUNK * (r + 1))
                if ch >= 4:
                    pe.wait_ge(state_ready, ch - 3)
                for h in range(HG):
                    n = slice(h * P, (h + 1) * P)
                    last = pe.matmul(ps[:, 4 + ch % 4, n], lhsT=ksT[rows, b, n], rhs=v_[rows, b, n],
                                     start=True, stop=True)
                last.then_inc(kv_done, 1)
            pe.wait_ge(state_ready, CHUNKS - 1)
            pe.wait_ge(xc_ready, 4)
            pe.wait_ge(lru_there, 16 * 4)
            for g in range(2):
                for j in range(4):
                    last = pe.matmul(ps[:, 4 + 2 * g + j // 2, (j % 2) * L:(j % 2 + 1) * L],
                                     lhsT=gate_w[:, g, j, :], rhs=xc[:, j, :], start=True, stop=True)
                last.then_inc(gates_done, 1)
            for i in range(4):
                features2(3, 256 + i * P)
            chunk2_used(22)
            pe.wait_ge(gates_ready, 8)
            for h in range(HG):
                n = slice(h * P, (h + 1) * P)
                o = ps[:, 4 + h // 2, (h % 2) * L:(h % 2 + 1) * L]
                for b in range(BLK):
                    pe.matmul(o[:, b * P:(b + 1) * P], lhsT=v_[:, b, n], rhs=sc_[:, b, h, :],
                              start=h % 2 == 0 and b == 0, stop=False, skip_group_check=True)
                for ch in range(1, CHUNKS):
                    t = slice(ch * CHUNK, (ch + 1) * CHUNK)
                    last = pe.matmul(o[:, t], lhsT=state(ch)[:, n], rhs=raw_q[:, h, t], start=False,
                                     stop=ch == CHUNKS - 1, skip_group_check=True)
                if h % 2:
                    last.then_inc(o_done, 1)
            pe.wait_ge(o_sq, 2)
            for i in range(2):
                pe.matmul(ps[:, 6 + i, :], lhsT=ones[:], rhs=sqf[:, i * 512:(i + 1) * 512], start=True,
                          stop=True).then_inc(o_ssq, 1)

            pe.wait_ge(mix2_ready, 8)
            for m in range(KT):
                ch, i = divmod(m, 4)
                if i == 0:
                    chunk_there("out2", ch)
                w = weights("out2", ch, KT, 512)
                if m >= 4:
                    pe.wait_ge(mo_taken, KT + m - 3)
                else:
                    pe.wait_ge(u2_taken, 22)
                product(ps[:, m % 4, 0:L], lambda k: w[:, k, i * P:(i + 1) * P],
                        lambda k: mixT[:, k, :]).then_inc(mo_done, 1)
                if i == 3:
                    pe.wait_ge(mo_done, KT + m + 1)
                    pe.sem_inc(chunk_used, 1)

            pe.wait_ge(sq_ready[4], 2)
            sum_squares(4, 6)
            pe.wait_ge(scaled[4], KT)
            for t in range(FT):
                ch, i = divmod(t, FFN_STEP)
                n = min(FFN_STEP, FT - ch * FFN_STEP)
                if i == 0:
                    chunk_there("ffn", ch)
                w = weights("ffn", ch, KT, 2 * n * P)
                if t >= 4:
                    pe.wait_ge(ffn_taken, t - 3)
                else:
                    pe.wait_ge(mo_taken, 2 * KT)
                for half in range(2):
                    at = (half * n + i) * P
                    last = product(ps[:, t % 4, half * L:(half + 1) * L], lambda k: w[:, k, at:at + P],
                                   lambda k: hT[:, k, :])
                last.then_inc(ffn_done, 1)
                if i == n - 1:
                    pe.wait_ge(ffn_done, t + 1)
                    pe.sem_inc(chunk_used, 1)
            for t in range(FT):
                ch, i = divmod(t, DOWN_STEP)
                n = min(DOWN_STEP, FT - ch * DOWN_STEP)
                if i == 0:
                    chunk_there("down", ch)
                w = weights("down", ch, n, D)
                pe.wait_ge(ffn_taken, t + 1)
                for j in range(KT):
                    last = pe.matmul(ps[:, 4 + j // 2, (j % 2) * L:(j % 2 + 1) * L], lhsT=w[:, i, j * P:(j + 1) * P],
                                     rhs=ffn[:, t, :], start=t == 0 and j % 2 == 0, stop=t == FT - 1,
                                     skip_group_check=True)
                    if t == FT - 1 and j % 2:
                        last.then_inc(down_done, 1)
                if i == n - 1 and t < FT - 1:
                    last.then_inc(chunk_used, 1)

            pe.wait_ge(sq_ready[6], 2)
            sum_squares(6, 4)
            pe.wait_ge(scaled[5], KT)
            for i in range(4):
                b, half = divmod(i, 2)
                for k in range(4):
                    last = pe.transpose(ps[:, i, k * P:(k + 1) * P], hT[:, 4 * half + k, b * P:(b + 1) * P], ident[:])
                last.then_inc(otr_done, 1)

        @block.scalar
        def _(act):
            def rows(tile, names, name):
                lo, hi = names[name]
                return hT[lo:hi, tile, 0:P]

            for name, v in (("c", c[0]), ("b_ada", b_ada[0]), ("g_mix", g_mix[0]), ("g_ffn", g_ffn[0]),
                            ("g_final", g_final)):
                act.dma_start(rows(0, PA_ROWS, name), v.rearrange("(k p) -> k p", p=P)).then_inc(par_there, 16)
            for name, v in (("g_out_a", g_out_a[0]), ("g_out_b", g_out_b[0]), ("mix2", mix_norm_w_2[0]), ("ffn2", ffn_norm_w_2[0]),
                            ("final2", final_norm_w_2), ("lb0", hg_lb_2[0]), ("lb1", hg_lb_2[1]),
                            ("hg_norm", hg_norm_w_2[0]),
                            ("conv_w", conv_w_2[0].rearrange("w n -> (w n)")), ("conv_b", conv_b_2[0]),
                            ("lru_ba", lru_ba_2[0]), ("lru_bx", lru_bx_2[0]), ("lru_a", lru_a_2[0])):
                act.dma_start(rows(1, PB_ROWS, name), v.rearrange("(k p) -> k p", p=P)).then_inc(par_there, 16)
            act.dma_start(brow[0:1, 0:8], b_forget).then_inc(par_there, 16)
            act.dma_start(brow[0:1, 8:8 + GROUPS], b_group).then_inc(par_there, 16)
            act.dma_start(brow[0:1, 8 + GROUPS:8 + GROUPS + EXPERTS], b_router.rearrange("o g e -> o (g e)")
                          ).then_inc(par_there, 16)
            act.dma_start(tok[:], x[0].rearrange("(b p) d -> p b d", p=P)).then_inc(x_there, 16)
            act.dma_start(wr[:, :, 0:GROUPS], w_group[0].rearrange("(k p) g -> p k g", p=P)).then_inc(wr_there, 16)
            for g in range(GROUPS):
                act.dma_start(wr[:, :, GROUPS + PER_GROUP * g:GROUPS + PER_GROUP * (g + 1)],
                              w_router[0, g].rearrange("(k p) e -> p k e", p=P)).then_inc(wr_there, 16)

            def squares(i, src, ready, first, second):
                for half, n in ((0, first), (1, second)):
                    act.wait_ge(ready, n)
                    act.activation(sq[:, 4 * half:4 * half + 4, :], src[:, 4 * half:4 * half + 4, :], ACT.Square
                                   ).then_inc(sq_ready[i], 1)

            def std_of(i, n, bank=6, parts=1):
                act.wait_ge(ssq_ready[i], parts)
                act.activation(rstd[:].rearrange("p a t -> p (a t)")[:, 0:parts * L], ps[:, bank, 0:parts * L],
                               ACT.Sqrt, scale=1.0 / n, bias=EPS).then_inc(std_ready[i], 1)

            def add_shift(i, shift):
                for k in range(KT):
                    act.wait_ge(scaled[i], k + 1)
                    act.activation(hT[:, k, :], hT[:, k, :], ACT.Identity, bias=mod[:, shift + k:shift + k + 1]
                                   ).then_inc(h_ready[i], 1)

            for q, bank in enumerate((0, 1, 4, 5)):
                act.wait_ge(xT_tr, q + 1)
                act.activation(xT[:, 2 * q:2 * q + 2, :], ps[:, bank, :].rearrange("p (k t) -> p k t", k=2),
                               ACT.Copy).then_inc(xT_ready, 1)
            squares(0, xT, xT_ready, 2, 4)
            act.wait_ge(par_taken, 1)
            act.activation(silu_c[:], parA[:, 0:KT], ACT.Silu).then_inc(silu_c_ready, 1)
            std_of(0, D)
            act.wait_ge(mod_ready, 1)
            add_shift(0, 0)

            unit = Count()

            def take(dst, src, scale=1.0):
                u = unit.up() - 1
                act.wait_ge(tile_ready, u + 1)
                act.activation(dst, src(ps[:, u % 2, :]), ACT.Copy, scale=scale).then_inc(tile_taken, 1)

            def whole(o):
                return o[:, 0:L]

            def relu_dots(h):
                act.wait_ge(dots_ready, h + 1)
                if h >= 2:
                    act.wait_ge(score_raw, 2 * (h - 1))
                act.activation(relu[:, h % 2, :], ps[:, 2 + h % 2, 0:NK], ACT.Relu).then_inc(dots_taken, 1)

            take(iwT, lambda o: o[:, 0:16].rearrange("p (b h) -> p b h", b=BLK))
            take(kI[0:64, :], lambda o: o[0:64, 0:L])
            for j in range(4):
                take(qI[:, j, :], whole)
            relu_dots(0)
            relu_dots(1)
            take(kA, whole)
            relu_dots(2)
            relu_dots(3)
            take(vA, lambda o: o[:, 0:256].rearrange("p (b n) -> p b n", b=BLK))
            for j in range(4):
                if j < 2:
                    relu_dots(4 + 2 * j)
                    relu_dots(5 + 2 * j)
                take(qA[:, j, :], whole, SCALE)

            def attend(n):
                if n < 2 * HEADS:
                    act.wait_ge(logits_ready, 2 * (n + 1))
                    if n >= 2:
                        act.wait_ge(pt_done, n - 1)
                    act.activation(prob[:, n % 2, 0:P], logit[:, n % 2, 0:P], ACT.Exp,
                                   bias=neg_max[:, n, 0:1], accum_out=p_sum[:, n, 0:1]).then_inc(act_step, 1)
                    act.activation(prob[:, n % 2, P:NK], logit[:, n % 2, P:NK], ACT.Exp,
                                   bias=neg_max[:, n, 1:2], accum_out=p_sum[:, n, 1:2]).then_inc(probs_ready, 1)
                if 1 <= n <= 2 * HEADS:
                    m = n - 1
                    act.wait_ge(pt_done, m + 1)
                    if m >= 2:
                        act.wait_ge(pv_done, m - 1)
                    act.activation(probT[:, m % 2, :], ps[:, 4 + m % 2, 0:NK], ACT.Copy).then_inc(pt_taken, 1)
                if n >= 3 and n % 2:
                    act.wait_ge(pv_done, n - 1)
                    act.activation(mixT[:, (n - 3) // 2, :], ps[:, 6, 0:L], ACT.Copy).then_inc(pv_taken, 1)

            attend(0)
            take(forget[:, 0, :], lambda o: o[:, 0:16])
            take(kB[:, 2, :], whole)
            attend(1)
            take(kB[:, 3, :], whole)
            act.wait_ge(forget_abs, 1)
            act.activation(forget[:, 1, :], forget[:, 1, :], ACT.Exp).then_inc(forget_ln, 1)
            act.wait_ge(forget_ln, 1)
            act.activation(forget[:, 1, :], forget[:, 1, :], ACT.Ln, bias=1.0).then_inc(forget_ln, 1)
            attend(2)
            take(vB[:, 0, :], lambda o: o)
            attend(3)
            take(vB[:, 1, :], lambda o: o)
            attend(4)
            take(qB[:, 0, :], whole, SCALE)
            take(qB[:, 1, :], whole, SCALE)
            attend(5)
            take(qB[:, 2, :], whole, SCALE)
            take(qB[:, 3, :], whole, SCALE)
            attend(6)
            take(kB[:, 0, :], whole)
            attend(7)
            take(kB[:, 1, :], whole)
            for n in range(HEADS, 2 * HEADS + 2):
                attend(n)
            squares(5, mixT, pv_taken, 4, 8)
            std_of(5, 512, parts=2)
            squares(1, xT, mo_taken, 4, 8)
            std_of(1, D)
            act.wait_ge(mod_ready, 2)
            add_shift(1, 24)

            for i in range(4):
                b, half = divmod(i, 2)
                act.wait_ge(htr_done, i + 1)
                act.activation(tok[:, b, :].rearrange("t (j p) -> t j p", j=KT)[:, :, 64 * half:64 * half + 64],
                               ps[:, i, :].rearrange("t (p j) -> t j p", j=KT), ACT.Copy).then_inc(htr_taken_a, 1)
            act.wait_ge(gate_max, 1)
            for b in range(BLK):
                act.activation(g_pen[:, b, :], g8[:, b, 0:GROUPS], ACT.Exp, bias=w_top[:, 0, b:b + 1],
                               accum_out=g_sum[:, b:b + 1]).then_inc(gate_exp, 1)
            act.wait_ge(top_diff, 1)
            act.activation(e_diff, e_diff, ACT.Exp).then_inc(top_exp, 1)
            for j in range(0, KT, 2):
                act.wait_ge(gather_done, j + 1)
                act.activation(xsT[:, j, 0:PAIRS], ps[:, j % 4, :], ACT.Copy).then_inc(gather_taken_a, 1)
            act.wait_ge(pickwT_done, 1)
            for i in range(2):
                act.activation(pickwT[:, 2 * i:2 * i + 2, :], ps[:, 6 + i, :].rearrange("p (s t) -> p s t", s=2),
                               ACT.Copy).then_inc(pickwT_taken, 1)
            act.wait_ge(lru_par, 2)
            act.activation(t8, t8, ACT.Exp).then_inc(lru_par_a, 1)
            act.activation(t4, t4, ACT.Exp).then_inc(lru_par_a, 1)
            act.wait_ge(lru_par_a, 2)
            act.activation(t4, t4, ACT.Ln, bias=1.0).then_inc(lru_par_a, 1)
            act.wait_ge(windows_ready, 2)
            too_many = act.value_load(flag_i[0:1, 0:1], min_val=0, max_val=1)
            with act.If(too_many < 1):
                with act.Fori(0, EXPERTS // SLOTS) as i:
                    for u in range(SLOTS):
                        act.wait_ge(gu_done, i * SLOTS + u + 1)
                        act.wait_ge(act_ready, i * SLOTS + u + 1)
                        act.activation(act_g[:, u % 2, :], ps[:, u % 2, 0:2 * WIN], ACT.Silu).then_inc(silu_done, 1)
            with act.Else():
                with act.Fori(0, EXPERTS * WINDOWS) as i:
                    act.wait_ge(w_gu_done, i + 1)
                    act.activation(act_g[:, 0, :], ps[:, 0, 0:2 * WIN], ACT.Silu).then_inc(w_silu_done, 1)
            for i in range(0, 8, 2):
                act.wait_ge(ytr_done, i + 1)
                act.activation(ys[:, i // 2, 0:512], ps[:, i % 4, :], ACT.Copy).then_inc(ytr_taken_a, 1)
            squares(2, xT, comb_taken, 4, 8)
            std_of(2, D)
            squares(3, xT, scaled[2], 4, 8)
            std_of(3, D)

            unit2 = Count()

            def take2(dst, n=L):
                u = unit2.up() - 1
                act.wait_ge(u2_done, u + 1)
                act.activation(dst, ps[:, u % 4, 0:n], ACT.Copy).then_inc(u2_taken, 1)

            take2(raw_q[:, 2, :])
            take2(raw_q[:, 3, :])
            for h in range(HG):
                take2(f_[:, h, :])
            act.wait_ge(u2_taken, 6)
            act.activation(f_, f_, ACT.Sigmoid).then_inc(f_sig, 1)
            take2(raw_q[:, 0, :])
            take2(raw_q[:, 1, :])
            act.wait_ge(u2_taken, 8)
            act.activation(a_, raw_q, ACT.Sigmoid).then_inc(q_sig, 1)
            take2(v_[:, 0, :], 512)
            act.wait_ge(f_ready, 1)
            act.activation(f_, f_, ACT.Ln).then_inc(f_ln, 1)
            take2(v_[:, 1, :], 512)
            take2(lx[:, 0, 4:260])
            act.wait_ge(b_ready, HG)
            act.activation(eb, b_, ACT.Exp).then_inc(decay_ready, 1)
            act.activation(kd, b_, ACT.Exp, scale=-1.0).then_inc(decay_ready, 1)
            take2(lx[:, 1, 4:260])
            act.wait_ge(last_diff, 1)
            act.activation(ks, ks, ACT.Exp).then_inc(last_exp, 1)
            take2(lx[:, 2, 4:260])
            take2(lx[:, 3, 4:260])
            take2(lg[:, 0, :])
            take2(lg[:, 1, :])
            for b in range(BLK):
                act.wait_ge(kst_done, b + 1)
                act.activation(ksT[:, b, :], ps[:, 4 + b, :], ACT.Copy).then_inc(kst_taken, 1)
            take2(lg[:, 2, :])
            take2(lg[:, 3, :])
            for g in range(2):
                act.wait_ge(gates_done, g + 1)
                for j in range(4):
                    bias = parB[:, PB_ROWS["lru_bx" if g else "lru_ba"][0] + j:][:, 0:1]
                    act.activation((ig if g else r_)[:, j, :],
                                   ps[:, 4 + 2 * g + j // 2, (j % 2) * L:(j % 2 + 1) * L], ACT.Sigmoid,
                                   bias=bias).then_inc(gates_ready, 1)
            take2(g_[:, 0, :])
            take2(g_[:, 1, :])
            act.wait_ge(gates_ready, 8)
            act.wait_ge(lru_par, 3)
            for j in range(4):
                act.activation(th[:, j, :], r_[:, j, :], ACT.Tanh, scale=lru_c[:, j:j + 1]).then_inc(decays_ready, 1)
                act.activation(a_[:, j, :], r_[:, j, :], ACT.Exp, scale=lru_nc[:, j:j + 1]).then_inc(decays_ready, 1)
            take2(g_[:, 2, :])
            take2(g_[:, 3, :])
            act.wait_ge(half_power, 1)
            act.activation(th, th, ACT.Sqrt, scale=2.0).then_inc(power_root, 1)
            act.wait_ge(gelu_in, 1)
            act.activation(k_, k_, ACT.Sigmoid, scale=1.5957691216057308).then_inc(gelu_sig, 1)
            act.wait_ge(u2_taken, 22)
            act.activation(ks, g_, ACT.Sigmoid).then_inc(g_sig, 1)
            for i in range(2):
                act.wait_ge(o_done, i + 1)
                act.activation(o_[:, 2 * i:2 * i + 2, :], ps[:, 4 + i, :].rearrange("p (h t) -> p h t", h=2), ACT.Copy
                               ).then_inc(o_taken, 1)
            act.wait_ge(o_taken, 2)
            for i in range(2):
                act.activation(sq[:, 2 * i:2 * i + 2, :], o_[:, 2 * i:2 * i + 2, :], ACT.Square).then_inc(o_sq, 1)
            act.wait_ge(o_ssq, 2)
            act.activation(b_, ps[:, 6:8, :].rearrange("p a (h t) -> p (a h) t", h=2), ACT.Sqrt, scale=1.0 / P,
                           bias=EPS).then_inc(o_std, 1)
            squares(4, xT, mo_taken, KT + 4, KT + 8)
            std_of(4, D)

            for t in range(FT):
                act.wait_ge(ffn_done, t + 1)
                if t >= 2:
                    act.wait_ge(ffn_taken, t - 1)
                act.activation(silu_t[:, t % 2, :], ps[:, t % 4, 0:L], ACT.Silu).then_inc(ffn_silu, 1)
            squares(6, xT, down_taken, 2, 4)
            std_of(6, D, bank=4)
            for b in range(BLK):
                act.wait_ge(otr_done, 2 * b + 1)
                act.activation(tok[:, b, 0:512], ps[:, 2 * b, :], ACT.Copy).then_inc(otr_taken_a, 1)

        @block.vector
        def _(ve):
            step = Count()

            def own(k=1):
                ve.wait_ge(dve_step, step.up(k))

            def rstd_of(i, parts=1):
                ve.wait_ge(std_ready[i], 1)
                r = rstd[:].rearrange("p a t -> p (a t)")[:, 0:parts * L]
                ve.reciprocal(r, r).then_inc(dve_step, 1)
                own()

            def scale(i, dst, gain):
                for k in range(KT):
                    ve.scalar_tensor_tensor(dst[:, k, :], xT[:, k, :], gain[:, k:k + 1], rstd[:, 0, :],
                                            ALU.mult, ALU.mult).then_inc(scaled[i], 1)

            def par(tile, names, name, k=None):
                lo, hi = names[name]
                return tile[:, lo:hi] if k is None else tile[:, lo + k:lo + k + 1]

            ve.wait_ge(par_tr, 1)
            ve.tensor_copy(parA[:], ps[:, 2, 0:PA_N]).then_inc(par_taken, 1)
            ve.wait_ge(par_tr, 2)
            ve.tensor_copy(parB[:], ps[:, 3, 0:PB_N]).then_inc(par_taken, 1)
            ve.wait_ge(par_taken, 2)
            lb0, lb1, lru = par(parB, PB_ROWS, "lb0"), par(parB, PB_ROWS, "lb1"), par(parB, PB_ROWS, "lru_a")
            ve.tensor_tensor(m4, lb0, lb1, ALU.max).then_inc(dve_step, 1)
            ve.tensor_scalar(u4, lru, -1.0, 0.0, ALU.mult, ALU.max).then_inc(dve_step, 1)
            own(2)
            ve.tensor_tensor(t8[:, 0:4], lb0, m4, ALU.subtract).then_inc(dve_step, 1)
            ve.tensor_tensor(t8[:, 4:8], lb1, m4, ALU.subtract).then_inc(lru_par, 1)
            ve.scalar_tensor_tensor(t4, lru, -1.0, lru, ALU.mult, ALU.min).then_inc(lru_par, 1)
            own()
            rstd_of(0)
            m0 = ADA_FIRST * ADA_W // P
            b_lo = PA_ROWS["b_ada"][0]
            ve.wait_ge(par_taken, 2)
            ve.wait_ge(chunk_used, ADA_FIRST)
            ve.tensor_tensor(mod[:, 0:m0], ps[:, 7, 0:m0], parA[:, b_lo:b_lo + m0], ALU.add).then_inc(mod_ready, 1)
            ve.wait_ge(mod_ready, 1)
            ve.scalar_tensor_tensor(gains[:, 0, :], mod[:, 8:16], 1.0, par(parA, PA_ROWS, "g_mix"), ALU.add,
                                    ALU.mult).then_inc(dve_step, 1)
            own()
            scale(0, hT, gains[:, 0, :])

            keys = (slice(0, P), slice(P, NK))
            for h in range(HEADS):
                ve.wait_ge(dots_taken, h + 1)
                if h:
                    ve.wait_ge(score_raw, 2 * h)
                for b in range(BLK):
                    if h == 0:
                        ve.tensor_scalar(score[:, keys[b]], relu[:, 0, keys[b]], iwT[:, b, 0:1], None, ALU.mult
                                         ).then_inc(score_raw, 1)
                    else:
                        ve.scalar_tensor_tensor(score[:, keys[b]], relu[:, h % 2, keys[b]], iwT[:, b, h:h + 1],
                                                score[:, keys[b]], ALU.mult, ALU.add).then_inc(score_raw, 1)
            ve.wait_ge(score_masked, 2)
            for r in range(TOPK // 8):
                src = score if r == 0 else left
                for b in range(BLK):
                    ve.max(top8[:, b, :], src[:, keys[b]]).then_inc(dve_step, 1)
                own(2)
                for b in range(BLK):
                    ve.match_replace(left[:, keys[b]], top8[:, b, :], src[:, keys[b]], TAKEN).then_inc(dve_step, 1)
                own(2)
            ve.tensor_scalar(sel_bias, left, -3.2e38, NEG, ALU.is_gt, ALU.mult).then_inc(sel_raw, 1)

            def logits(n):
                ve.wait_ge(logits_done, n + 1)
                bank = 2 + n % 2
                if n < HEADS:
                    slope = 2.0 ** (-8.0 * (n + 1) / HEADS)
                    ve.scalar_tensor_tensor(with_alibi, neg_dist, slope, ps[:, bank, 0:NK], ALU.mult, ALU.add
                                            ).then_inc(logits_taken, 1)
                    ve.wait_ge(sel_ready, 2)
                    ve.wait_ge(logits_taken, n + 1)
                    ve.tensor_tensor(logit[:, n % 2, :], with_alibi, sel_bias, ALU.add).then_inc(dve_step, 1)
                    own()
                else:
                    h = n - HEADS
                    ve.scalar_tensor_tensor(logit[:, n % 2, 0:P], ps[:, bank, 0:P], cum[:, 0, h:h + 1],
                                            causal[:, P:L], ALU.add, ALU.add).then_inc(dve_step, 1)
                    ve.scalar_tensor_tensor(logit[:, n % 2, P:NK], ps[:, bank, P:NK], cum[:, 1, h:h + 1],
                                            causal[:], ALU.add, ALU.add).then_inc(logits_taken, 1)
                    own()
                    ve.wait_ge(logits_taken, n + 1)
                for b in range(BLK):
                    ve.tensor_reduce(neg_max[:, n, b:b + 1], logit[:, n % 2, keys[b]], AX.X, ALU.max, negate=True
                                     ).then_inc(logits_ready, 1)

            def diagonals(m):
                ve.wait_ge(probs_ready, m + 1)
                ve.reciprocal(p_rsum[:, m, :], p_sum[:, m, :]).then_inc(dve_step, 1)
                own()
                if m >= 2:
                    ve.wait_ge(pt_done, m - 1)
                for b in range(BLK):
                    i = ve.tensor_scalar(diag[:, m % 2, b, :], ident[:], p_rsum[:, m, b:b + 1], None, ALU.mult)
                i.then_inc(diag_ready, 1)

            for n in range(2 * HEADS + 1):
                if n < 2 * HEADS:
                    logits(n)
                if n:
                    diagonals(n - 1)
                if n == 0:
                    ve.wait_ge(tile_taken, 13)
                    ve.scalar_tensor_tensor(forget[:, 1, :], forget[:, 0, :], -1.0, forget[:, 0, :], ALU.mult,
                                            ALU.min).then_inc(forget_abs, 1)
                if n == 2:
                    ve.wait_ge(forget_ln, 2)
                    ve.scalar_tensor_tensor(forget[:, 2, :], forget[:, 0, :], 0.0, forget[:, 1, :], ALU.min,
                                            ALU.subtract).then_inc(log_f_ready, 1)
                if n == 5:
                    ve.wait_ge(cum_done, 1)
                    ve.tensor_copy(cum, ps[:, 7, 64:80].rearrange("p (b h) -> p b h", b=BLK)).then_inc(cum_taken, 1)
                    ve.tensor_scalar(ncumT[0:HEADS, :], ps[0:HEADS, 7, 128:384], -1.0, None, ALU.mult
                                     ).then_inc(cum_taken, 1)
                    ve.wait_ge(cum_taken, 2)
            ve.wait_ge(chunk_used, NUMBER["ada", ADA_N - 1] + 1)
            ve.tensor_tensor(mod[:, m0:48], ps[:, 7, m0:48], parA[:, b_lo + m0:b_lo + 48], ALU.add).then_inc(mod_ready, 1)
            ve.wait_ge(mod_ready, 2)
            ve.scalar_tensor_tensor(gains[:, 1, :], mod[:, 32:40], 1.0, par(parA, PA_ROWS, "g_ffn"), ALU.add,
                                    ALU.mult).then_inc(dve_step, 1)
            own()
            rstd_of(5, parts=2)
            for k in range(KT):
                ve.scalar_tensor_tensor(mixT[:, k, :], mixT[:, k, :], parB[:, k:k + 1], rstd[:, k // 4, :],
                                        ALU.mult, ALU.mult).then_inc(mix_ready, 1)
            for m in range(KT):
                ve.wait_ge(mo_done, m + 1)
                ve.scalar_tensor_tensor(xT[:, m, :], ps[:, m % 4, 0:L], mod[:, 16 + m:17 + m], xT[:, m, :], ALU.mult,
                                        ALU.add).then_inc(mo_taken, 1)

            rstd_of(1)
            scale(1, hT, gains[:, 1, :])
            nr = GROUPS + EXPERTS
            ve.memset(g8, -BIG).then_inc(dve_step, 1)
            own()
            ve.wait_ge(route_done, 1)
            logit_r = ps[:, 4, 0:BLK * nr].rearrange("p (b n) -> p b n", b=BLK)
            ve.tensor_copy(g8[:, :, 0:GROUPS], logit_r[:, :, 0:GROUPS]).then_inc(dve_step, 1)
            ve.tensor_copy(e_log, logit_r[:, :, GROUPS:nr]).then_inc(dve_step, 1)
            own(2)
            for b in range(BLK):
                ve.max(g_top[:, b, :], g8[:, b, :]).then_inc(dve_step, 1)
            own(2)
            ve.tensor_scalar(w_top[:, 0, :], g_top[:, :, 0], -1.0, None, ALU.mult).then_inc(gate_max, 1)
            for b in range(BLK):
                ve.max_index(idx_u[:, 0, b, :], g_top[:, b, :], g8[:, b, :]).then_inc(dve_step, 1)
            own(2)
            ve.tensor_copy(g_idx, idx_u[:, 0, :, 0]).then_inc(dve_step, 1)
            own()
            for b in range(BLK):
                ve.tensor_scalar(g_one[:, b, :], col_no[:, 0:GROUPS], g_idx[:, b:b + 1], None, ALU.is_equal
                                 ).then_inc(dve_step, 1)
            own(2)
            ve.wait_ge(gate_exp, 2)
            ve.tensor_scalar(g_pen, g_one, -1.0, BIG, ALU.add, ALU.mult).then_inc(dve_step, 1)
            one = g_one.rearrange("p b g -> p (b g)").unsqueeze(2).broadcast_to([P, BLK * GROUPS, PER_GROUP])
            pen = g_pen.rearrange("p b g -> p (b g)").unsqueeze(2).broadcast_to([P, BLK * GROUPS, PER_GROUP])
            e_3d = e_log.rearrange("p b (g e) -> p (b g) e", g=GROUPS)
            ve.tensor_tensor(e_3d, e_3d, one, ALU.mult).then_inc(dve_step, 1)
            own(2)
            ve.tensor_tensor(e_3d, e_3d, pen, ALU.add).then_inc(dve_step, 1)
            own()
            for b in range(BLK):
                ve.max(e_top[:, b, :], e_log[:, b, :]).then_inc(dve_step, 1)
            own(2)
            ve.tensor_tensor(e_diff, e_top[:, :, 1], e_top[:, :, 0], ALU.subtract).then_inc(top_diff, 1)
            for b in range(BLK):
                ve.max_index(idx_u[:, 1, b, :], e_top[:, b, :], e_log[:, b, :]).then_inc(dve_step, 1)
            own(2)
            ve.tensor_copy(e_idx, idx_u[:, 1, :, 0:2]).then_inc(dve_step, 1)
            own()
            for ch in range(2):
                for b in range(BLK):
                    ve.tensor_scalar(R_one[:, ch, b * EXPERTS:(b + 1) * EXPERTS], col_no[:, 0:EXPERTS],
                                     e_idx[:, b, ch:ch + 1], None, ALU.is_equal).then_inc(dve_step, 1)
            own(4)
            ve.tensor_tensor(R_chosen.rearrange("p b e -> p (b e)"), R_one[:, 0, :], R_one[:, 1, :], ALU.add
                             ).then_inc(choice_ready, 1)
            ve.wait_ge(rank_done, 1)
            ve.tensor_copy(counts, ps[:, 5, 64:96]).then_inc(dve_step, 1)
            own()
            ve.tensor_tensor_scan(upto, ones[:, 0:EXPERTS], counts, 0.0, ALU.mult, ALU.add).then_inc(dve_step, 1)
            own()
            ve.tensor_tensor(starts_f, upto, counts, ALU.subtract).then_inc(dve_step, 1)
            own()
            ve.tensor_tensor(place, ps[:, 5, 0:64].rearrange("p (b e) -> p b e", b=BLK),
                             starts_f.unsqueeze(1).broadcast_to([P, BLK, EXPERTS]), ALU.add).then_inc(dve_step, 1)
            own()
            prod = tmp_cols[:, 0:2 * BLK * EXPERTS].rearrange("p (c n) -> p c n", c=2)
            ve.tensor_tensor(prod, R_one, place.rearrange("p b e -> p (b e)").unsqueeze(1).broadcast_to(
                [P, 2, BLK * EXPERTS]), ALU.mult).then_inc(dve_step, 1)
            own()
            ve.tensor_reduce(cols.rearrange("p c b -> p (c b)"), prod.rearrange("p c (b e) -> p (c b) e", b=BLK),
                             AX.X, ALU.add).then_inc(dve_step, 1)
            own()
            for b in range(BLK):
                if b:
                    ve.wait_ge(pick_ready, b)
                ve.tensor_scalar(tmp_cols, col_no, cols[:, 1, b:b + 1], None, ALU.is_equal).then_inc(dve_step, 1)
                own()
                ve.scalar_tensor_tensor(pick[:, b, :], col_no, cols[:, 0, b:b + 1], tmp_cols, ALU.is_equal, ALU.add
                                        ).then_inc(pick_ready, 1)
            for w in range(WINDOWS):
                ve.tensor_scalar(wins_i[0:1, w, :], starts_f[0:1, :], float(w * WIN), float(PAIRS), ALU.add, ALU.min
                                 ).then_inc(dve_step, 1)
            ve.tensor_reduce(most, counts, AX.X, ALU.max).then_inc(dve_step, 1)
            own(WINDOWS + 1)
            ve.tensor_scalar(flag_i[0:1, 0:1], most[0:1, :], float(WIN), None, ALU.is_gt).then_inc(windows_ready, 2)
            ve.wait_ge(top_exp, 1)
            ve.scalar_tensor_tensor(w_top[:, 0, :], e_diff, 1.0, g_sum, ALU.add, ALU.mult).then_inc(dve_step, 1)
            own()
            ve.reciprocal(w_top[:, 0, :], w_top[:, 0, :]).then_inc(dve_step, 1)
            own()
            ve.tensor_tensor(w_top[:, 1, :], w_top[:, 0, :], e_diff, ALU.mult).then_inc(dve_step, 1)
            own()
            ve.wait_ge(pick_ready, BLK)
            for b in range(BLK):
                if b:
                    ve.wait_ge(pickw_ready, b)
                ve.tensor_scalar(tmp_cols, col_no, cols[:, 1, b:b + 1], w_top[:, 1, b:b + 1], ALU.is_equal, ALU.mult
                                 ).then_inc(dve_step, 1)
                ve.tensor_scalar(pickw[:, b, :], col_no, cols[:, 0, b:b + 1], w_top[:, 0, b:b + 1], ALU.is_equal,
                                 ALU.mult).then_inc(dve_step, 1)
                own(2)
                ve.tensor_tensor(pickw[:, b, :], pickw[:, b, :], tmp_cols, ALU.add).then_inc(pickw_ready, 1)
            for j in range(1, KT, 2):
                ve.wait_ge(gather_done, j + 1)
                ve.tensor_copy(xsT[:, j, 0:PAIRS], ps[:, j % 4, :]).then_inc(gather_taken_v, 1)

            too_many = ve.value_load(flag_i[0:1, 0:1], min_val=0, max_val=1)
            with ve.If(too_many < 1):
                ve.sem_inc(act_ready, 2)
                ve.sem_inc(y_taken, 2)
                with ve.Fori(0, EXPERTS // SLOTS) as i:
                    _, starts = nc.values_load_multi_w_load_instructions(
                        wins_i[0:1, 0, bass.ds(i * SLOTS, SLOTS)], engines=(ENG.DVE,), min_val=0, max_val=PAIRS)

                    def gated(u):
                        ve.wait_ge(silu_done, i * SLOTS + u + 1)
                        ve.wait_ge(chunk_used, i * SLOTS + (EXPERT0 + u - 1))
                        ve.tensor_tensor(act_e[:, u % 2].rearrange("p k n -> p (k n)"), act_g[:, u % 2, :],
                                         ps[:, u % 2, 2 * WIN:4 * WIN], ALU.mult).then_inc(act_ready, 1)

                    def result(u):
                        ve.wait_ge(chunk_used, i * SLOTS + (EXPERT0 + u + 1))
                        ve.wait_ge(y_taken, i * SLOTS + u + 2)
                        ve.tensor_copy(ysT[:, :, bass.ds(starts[u], WIN)],
                                       ps[:, 2 + u % 2, :].rearrange("p (j n) -> p j n", j=KT)).then_inc(y_taken, 1)

                    gated(0)
                    for u in range(SLOTS):
                        if u + 1 < SLOTS:
                            gated(u + 1)
                        result(u)
                ve.wait_ge(y_taken, EXPERTS + 2)
            with ve.Else():
                ve.sem_inc(w_y_taken, 1)
                with ve.Fori(0, EXPERTS) as i:
                    with ve.Fori(0, WINDOWS) as w:
                        start = ve.value_load(
                            wins_i[:].rearrange("o w e -> o (w e)")[0:1, bass.ds(w * EXPERTS + i, 1)],
                            min_val=0, max_val=PAIRS)
                        done = i * WINDOWS + w
                        ve.wait_ge(w_silu_done, done + 1)
                        ve.tensor_tensor(act_e[:, 0].rearrange("p k n -> p (k n)"), act_g[:, 0, :],
                                         ps[:, 0, 2 * WIN:4 * WIN], ALU.mult).then_inc(w_act_ready, 1)
                        ve.wait_ge(w_y_done, done + 1)
                        ve.wait_ge(w_y_taken, done + 1)
                        ve.tensor_copy(ysT[:, :, bass.ds(start, WIN)],
                                       ps[:, 2, :].rearrange("p (j n) -> p j n", j=KT)).then_inc(w_y_taken, 1)
                ve.wait_ge(w_y_taken, EXPERTS * WINDOWS + 1)
            ve.sem_inc(ys_complete, 1)
            for i in range(1, 8, 2):
                ve.wait_ge(ytr_done, i + 1)
                ve.tensor_copy(ys[:, i // 2, 512:1024], ps[:, i % 4, :]).then_inc(ytr_taken_v, 1)
            for j in range(KT):
                ve.wait_ge(comb_done, j + 1)
                ve.scalar_tensor_tensor(xT[:, j, :], ps[:, 4 + j % 4, 0:L], mod[:, 40 + j:41 + j], xT[:, j, :], ALU.mult,
                                        ALU.add).then_inc(comb_taken, 1)
            rstd_of(2)
            scale(2, xT, par(parA, PA_ROWS, "g_final"))
            rstd_of(3)
            scale(3, hT, par(parB, PB_ROWS, "mix2"))

            ve.wait_ge(lru_par_a, 3)
            ve.tensor_tensor(m4, t8[:, 0:4], t8[:, 4:8], ALU.add).then_inc(dve_step, 1)
            ve.tensor_tensor(u4, u4, t4, ALU.add).then_inc(dve_step, 1)
            own(2)
            ve.reciprocal(m4, m4).then_inc(dve_step, 1)
            ve.tensor_scalar(lru_c, u4, LRU_C, None, ALU.mult).then_inc(dve_step, 1)
            ve.tensor_scalar(lru_nc, u4, -LRU_C, None, ALU.mult).then_inc(lru_par, 1)
            own(2)
            ve.tensor_tensor(lb, t8[:, 0:4], m4, ALU.mult).then_inc(dve_step, 1)
            own()
            ve.tensor_scalar(one_lb, lb, -1.0, 1.0, ALU.mult, ALU.add).then_inc(dve_step, 1)
            ve.memset(lx[:, :, 1:4], 0.0).then_inc(dve_step, 1)
            own(2)
            ve.wait_ge(f_sig, 1)
            for h in range(HG):
                ve.tensor_scalar(f_[:, h, :], f_[:, h, :], one_lb[:, h:h + 1], lb[:, h:h + 1], ALU.mult, ALU.add
                                 ).then_inc(dve_step, 1)
            own(HG)
            ve.tensor_scalar(k_, f_, -1.0, 1.0, ALU.mult, ALU.add).then_inc(f_ready, 1)
            ve.wait_ge(q_sig, 1)
            ve.tensor_tensor(raw_q, raw_q, a_, ALU.mult).then_inc(dve_step, 1)
            own()
            ve.wait_ge(f_ln, 1)
            for h in range(HG):
                ve.tensor_tensor_scan(b_[:, h, :], reset, f_[:, h, :], 0.0, ALU.mult, ALU.add).then_inc(b_ready, 1)
            ve.wait_ge(b_ready, HG)
            ve.wait_ge(f_ready, 1)
            flat = "p h (c j) -> p (h c) j"
            bc = b_.rearrange(flat, j=CHUNK)
            ve.tensor_tensor(ks.rearrange(flat, j=CHUNK),
                             bc[:, :, CHUNK - 1:CHUNK].broadcast_to([P, HG * CHUNKS, CHUNK]), bc, ALU.subtract
                             ).then_inc(last_diff, 1)
            ve.wait_ge(decay_ready, 1)
            ve.tensor_tensor(raw_q, raw_q, eb, ALU.mult).then_inc(qd_ready, 1)
            ve.wait_ge(decay_ready, 2)
            ve.tensor_tensor(kd, kd, k_, ALU.mult).then_inc(kd_ready, 1)
            ve.wait_ge(last_exp, 1)
            ve.tensor_tensor(ks, ks, k_, ALU.mult).then_inc(ks_ready, 1)
            ve.wait_ge(u2_taken, 14)
            cw, cb = PB_ROWS["conv_w"][0], PB_ROWS["conv_b"][0]
            for tap in range(CONV):
                for j in range(4):
                    w_tap = parB[:, cw + 4 * tap + j:cw + 4 * tap + j + 1]
                    if tap == 0:
                        ve.tensor_scalar(xc[:, j, :], lx[:, j, 1:1 + L], w_tap, parB[:, cb + j:cb + j + 1], ALU.mult,
                                         ALU.add).then_inc(dve_step, 1)
                    else:
                        ve.scalar_tensor_tensor(xc[:, j, :], lx[:, j, 1 + tap:1 + tap + L], w_tap, xc[:, j, :],
                                                ALU.mult, ALU.add
                                                ).then_inc(xc_ready if tap == CONV - 1 else dve_step, 1)
                if tap < CONV - 1:
                    own(4)
            for b in range(BLK):
                ve.wait_ge(hsc_done, b + 1)
                ve.scalar_tensor_tensor(sc_[:, b], ps[:, 6 + b, :].rearrange("p (h t) -> p h t", h=HG), BIG,
                                        in_chunk.unsqueeze(1).broadcast_to([P, HG, P]), ALU.min, ALU.mult
                                        ).then_inc(hsc_ready, 1)
            for ch in range(CHUNKS - 1):
                ve.wait_ge(kv_done, ch + 1)
                if ch == 0:
                    ve.tensor_copy(state(1), ps[:, 4, :]).then_inc(state_ready, 1)
                    continue
                ve.wait_ge(state_ready, ch)
                for h in range(HG):
                    n = slice(h * P, (h + 1) * P)
                    last = ch * CHUNK + CHUNK - 1
                    i = ve.scalar_tensor_tensor(state(ch + 1)[:, n], state(ch)[:, n], eb[:, h, last:last + 1],
                                                ps[:, 4 + ch % 4, n], ALU.mult, ALU.add)
                i.then_inc(state_ready, 1)
            ve.wait_ge(u2_taken, 18)
            ve.wait_ge(ks_ready, 1)
            ve.tensor_tensor(k_, lg, lg, ALU.mult).then_inc(dve_step, 1)
            own()
            ve.tensor_scalar(k_, k_, 0.044715, 1.0, ALU.mult, ALU.add).then_inc(dve_step, 1)
            own()
            ve.tensor_tensor(k_, k_, lg, ALU.mult).then_inc(gelu_in, 1)
            ve.wait_ge(decays_ready, 8)
            ve.tensor_scalar(r_, th, 1.0, None, ALU.add).then_inc(dve_step, 1)
            ve.tensor_tensor(ig, ig, xc, ALU.mult).then_inc(dve_step, 1)
            own(2)
            ve.reciprocal(r_, r_).then_inc(dve_step, 1)
            own()
            ve.tensor_tensor(th, th, r_, ALU.mult).then_inc(half_power, 1)
            ve.wait_ge(power_root, 1)
            ve.tensor_tensor(ig, ig, th, ALU.mult).then_inc(dve_step, 1)
            own()
            for j in range(4):
                ve.tensor_tensor_scan(xc[:, j, :], a_[:, j, :], ig[:, j, :], 0.0, ALU.mult, ALU.add
                                      ).then_inc(dve_step, 1)
            own(4)
            ve.wait_ge(gelu_sig, 1)
            ve.tensor_tensor(lg, lg, k_, ALU.mult).then_inc(dve_step, 1)
            own()
            ve.tensor_tensor(mixT[:, 4:8, :], xc, lg, ALU.mult).then_inc(mix2_ready, 4)
            ve.wait_ge(g_sig, 1)
            ve.scalar_tensor_tensor(g_, g_, par(parB, PB_ROWS, "hg_norm"), ks, ALU.mult, ALU.mult).then_inc(dve_step, 1)
            ve.wait_ge(o_std, 1)
            ve.reciprocal(b_, b_).then_inc(dve_step, 1)
            own(2)
            ve.tensor_tensor(o_, o_, b_, ALU.mult).then_inc(dve_step, 1)
            own()
            ve.tensor_tensor(mixT[:, 0:4, :], o_, g_, ALU.mult).then_inc(mix2_ready, 4)
            for m in range(KT):
                ve.wait_ge(mo_done, KT + m + 1)
                ve.tensor_tensor(xT[:, m, :], ps[:, m % 4, 0:L], xT[:, m, :], ALU.add).then_inc(mo_taken, 1)

            rstd_of(4)
            scale(4, hT, par(parB, PB_ROWS, "ffn2"))
            for t in range(FT):
                ve.wait_ge(ffn_silu, t + 1)
                ve.tensor_tensor(ffn[:, t, :], silu_t[:, t % 2, :], ps[:, t % 4, L:2 * L], ALU.mult
                                 ).then_inc(ffn_taken, 1)
            for i in range(4):
                ve.wait_ge(down_done, i + 1)
                ve.tensor_tensor(xT[:, 2 * i:2 * i + 2, :], ps[:, 4 + i, :].rearrange("p (k t) -> p k t", k=2),
                                 xT[:, 2 * i:2 * i + 2, :], ALU.add).then_inc(down_taken, 1)
            rstd_of(6)
            scale(5, hT, par(parB, PB_ROWS, "final2"))
            for b in range(BLK):
                ve.wait_ge(otr_done, 2 * b + 2)
                ve.tensor_copy(tok[:, b, 512:1024], ps[:, 2 * b + 1, :]).then_inc(otr_taken_v, 1)


_INS = ['x', 'c', 'w_ada', 'b_ada', 'g_mix', 'w_in', 'b_forget', 'g_out_a', 'g_out_b', 'w_out', 'g_ffn',
        'w_group', 'b_group', 'w_router', 'b_router', 'w_gate', 'w_up', 'w_down', 'g_final',
        'mix_norm_w_2', 'w_in_2', 'hg_lb_2', 'hg_norm_w_2', 'conv_w_2', 'conv_b_2', 'lru_wa_2', 'lru_ba_2',
        'lru_wx_2', 'lru_bx_2', 'lru_a_2', 'w_out_2', 'ffn_norm_w_2', 'w_gate_up_2', 'w_down_2',
        'final_norm_w_2']


def kernel(**inputs):
    import numpy as np
    import concourse.bacc as bacc
    from concourse.bass_utils import run_bass_kernel_spmd

    nc = bacc.Bacc("TRN2", target_bir_lowering=False, num_devices=1)
    arrays, args = {}, []
    for name in _INS:
        a = np.ascontiguousarray(inputs[name])
        arrays[f"in_{name}"] = a
        args.append(nc.dram_tensor(f"in_{name}", a.shape, mybir.dt.from_np(a.dtype), kind="ExternalInput").ap())
    args.append(nc.dram_tensor("out_y", (1, L, D), F32, kind="ExternalOutput").ap())
    build(nc, *args)
    r = run_bass_kernel_spmd(nc, [arrays], core_ids=[0])
    return r.results[0]["out_y"]
```

```python
from contextlib import ExitStack

import concourse.bass as bass
from concourse import mybir

F32 = mybir.dt.float32
I32 = mybir.dt.int32
U32 = mybir.dt.uint32
ALU = mybir.AluOpType
ACT = mybir.ActivationFunctionType
AX = mybir.AxisListType
ENG = mybir.EngineType

P = 128
L = 256
BLK = L // P
D = 1024
KT = D // P
EPS = 1e-6

HEADS = 8
HD = 64
SCALE = HD ** -0.5
TOPK = min(256, L // 4)
IN_COLS = 2896
AQ, AK, AV, IQ, IK, IW, BQ, BK, BV, BF = 0, 512, 640, 768, 1280, 1344, 1352, 1864, 2376, 2888
GROUPS, PER_GROUP = 4, 8
EXPERTS = GROUPS * PER_GROUP
FE = 256
PAIRS = 2 * L
WIN = 64
WINDOWS = L // WIN
COLS = PAIRS + WIN

HG = 4
CHUNK = 32
CHUNKS = L // CHUNK
CONV = 4
LRU_C = 8.0
D_FF = 2816
FT = D_FF // P

MASKED = -3.0e38
TAKEN = -3.4e38
NEG = -1.0e30
BIG = 3.0e38

SLOTS = 4
SLOT_F = KT * 776
ADA_W = 768
ADA_N = 6 * D // ADA_W
IN_CHUNKS = [(IQ, BQ), (AQ, IQ), (BK + 256, IN_COLS), (BQ, BK + 256)]
C_IN = ADA_N
ADA_FIRST = 3
FFN_STEP = 3
FFN_N = -(-FT // FFN_STEP)
DOWN_STEP = 6
DOWN_N = -(-FT // DOWN_STEP)

ORDER = ([("ada", c, 1) for c in range(ADA_FIRST)] + [("in", c, 1) for c in range(4)]
         + [("ada", c, 1) for c in range(ADA_FIRST, ADA_N)] + [("out", c, 1) for c in range(2)]
         + [("expert", e, 3) for e in range(EXPERTS)]
         + [("in2", 0, 1), ("in2", 1, 2), ("in2", 2, 1), ("in2", 3, 2)]
         + [("out2", c, 1) for c in range(2)] + [("ffn", c, 2) for c in range(FFN_N)]
         + [("down", c, 1) for c in range(DOWN_N)])
NUMBER = {(kind, c): n for n, (kind, c, _) in enumerate(ORDER)}
ARRIVED = []
_counts = [0] * SLOTS
for _n, (_, _, _dmas) in enumerate(ORDER):
    _counts[_n % SLOTS] += 16 * _dmas
    ARRIVED.append(_counts[_n % SLOTS])
EXPERT0 = NUMBER["expert", 0]
PE_USED = [sum(kind != "ada" for kind, _, _ in ORDER[:n + 1]) for n in range(len(ORDER))]
USED0 = PE_USED[EXPERT0] - 1
assert EXPERTS % SLOTS == 0

PA_ROWS = {}
PB_ROWS = {}
for _rows, _list in ((PA_ROWS, [("c", 8), ("b_ada", 48), ("g_mix", 8), ("g_ffn", 8), ("g_final", 8)]),
                     (PB_ROWS, [("g_out_a", 4), ("g_out_b", 4), ("mix2", 8), ("ffn2", 8), ("final2", 8),
                                ("lb0", 4), ("lb1", 4), ("hg_norm", 1), ("conv_w", 16), ("conv_b", 4),
                                ("lru_ba", 4), ("lru_bx", 4), ("lru_a", 4)])):
    _at = 0
    for _name, _k in _list:
        _rows[_name] = (_at, _at + _k)
        _at += _k
PA_N = 80
N_CONST, N_PAR, N_WR = 12, 21, 5
PB_N = 73



class Count:

    def __init__(self):
        self.n = 0

    def up(self, k=1):
        self.n += k
        return self.n


def build(nc, x, c, w_ada, b_ada, g_mix, w_in, b_forget, g_out_a, g_out_b, w_out, g_ffn, w_group,
          b_group, w_router, b_router, w_gate, w_up, w_down, g_final, mix_norm_w_2, w_in_2, hg_lb_2,
          hg_norm_w_2, conv_w_2, conv_b_2, lru_wa_2, lru_ba_2, lru_wx_2, lru_bx_2, lru_a_2, w_out_2,
          ffn_norm_w_2, w_gate_up_2, w_down_2, final_norm_w_2, out):
    with ExitStack() as ctx:
        def sb(name, shape, dt=F32):
            return ctx.enter_context(nc.sbuf_tensor(name, shape, dt))

        def sem(name):
            return ctx.enter_context(nc.semaphore(name))

        ring = sb("ring", [P, SLOTS, SLOT_F])
        xT = sb("xT", [P, KT, L])
        hT = sb("hT", [P, KT, L])
        sq = sb("sq", [P, KT, L])
        mixT = sb("mixT", [P, KT, L])
        tok = sb("tok", [P, BLK, D])
        ident = sb("ident", [P, P])
        ones = sb("ones", [P, P])
        tri = sb("tri", [P, L])
        parA = sb("parA", [P, PA_N])
        parB = sb("parB", [P, PB_N])
        mod = sb("mod", [P, 48])
        gains = sb("gains", [P, 2, KT])
        silu_c = sb("silu_c", [P, KT])
        rstd = sb("rstd", [P, 2, L])
        small = sb("small", [P, 64])
        arena = sb("arena", [P, 15760])
        wins_i = sb("wins_i", [1, WINDOWS, EXPERTS + SLOTS], I32)
        flag_i = sb("flag_i", [1, 1], I32)
        idx_u = sb("idx_u", [P, 2, BLK, 8], U32)

        def cut(at, *shape):
            n = 1
            for s in shape:
                n *= s
            v = arena[:, at:at + n]
            if len(shape) == 2:
                v = v.rearrange("p (a b) -> p a b", b=shape[1])
            if len(shape) == 3:
                v = v.rearrange("p (a b c) -> p a b c", b=shape[1], c=shape[2])
            return v

        qA = cut(0, 4, L)
        qI = cut(1024, 4, L)
        qB = cut(2048, 4, L)
        kB = cut(3072, 4, L)
        kA = cut(4096, L)
        kI = cut(4352, L)
        kA_swap = cut(14240, L)
        vA = cut(4608, BLK, 128)
        vB = cut(4864, BLK, 512)
        NK = P + L
        score = cut(5888, NK)
        left = cut(6272, NK)
        relu = cut(6656, 2, NK)
        sel_bias = cut(7424, NK)
        with_alibi = cut(7808, NK)
        logit = cut(8192, 2, NK)
        prob = cut(8960, 2, NK)
        probT = cut(9728, 2, NK)
        diag = cut(10496, 2, BLK, P)
        causal = cut(11008, L)
        neg_dist = cut(11264, NK)
        head_row = cut(11648, HEADS, P)
        ncumT = cut(12672, L)
        iwT = cut(12928, BLK, 8)
        cum = cut(12944, BLK, 8)
        forget = cut(12960, 3, BLK * 8)
        att_small = cut(13008, 512)
        top8 = att_small[:, 0:16].rearrange("p (b k) -> p b k", b=BLK)
        neg_max = att_small[:, 16:48].rearrange("p (n b) -> p n b", b=BLK)
        p_sum = att_small[:, 48:80].rearrange("p (n b) -> p n b", b=BLK)
        p_rsum = att_small[:, 80:112].rearrange("p (n b) -> p n b", b=BLK)

        xsT = cut(0, KT, COLS)
        xw = cut(4608, 2 * KT, 2 * WIN).rearrange("p (u k) n -> p u k n", u=2)
        y_sb = cut(6656, D)
        act_g = cut(7680, FE)
        act_e = cut(7936, FE)
        put = cut(8192, 2 * BLK, 2, WIN).rearrange("p (u b) h r -> p u b h r", u=2)
        turned = cut(10240, 2, 512)
        rank = cut(11264, BLK, EXPERTS + 2)
        w_all = cut(11332, BLK, EXPERTS + 2)
        pick = cut(9216, BLK, PAIRS)
        col_no = cut(13600, PAIRS)
        strict = cut(14112, P)
        tmp_cols = cut(14240, PAIRS)
        route = cut(14752, 624)
        wr = sb("wr", [P, KT, GROUPS + EXPERTS])
        brow = sb("brow", [1, 8 + GROUPS + EXPERTS])

        n1k = HG * L
        raw_q = cut(0, HG, L)
        f_ = cut(1024, HG, L)
        k_ = cut(2048, HG, L)
        b_ = cut(3072, HG, L)
        eb = cut(4096, HG, L)
        kd = cut(5120, HG, L)
        ks = cut(6144, HG, L)
        v_ = cut(7168, BLK, 512)
        g_ = cut(8192, HG, L)
        lx = cut(9216, 4, 260)
        lg = cut(10256, 4, L)
        xc = cut(11280, 4, L)
        r_ = cut(12304, 4, L)
        ig = cut(13328, 4, L)
        a_ = cut(14352, 4, L)
        th = cut(9216, 4, L)
        reset = cut(15376, L)
        in_chunk = cut(15632, P)
        ksT = b_.rearrange("p h t -> p (h t)").rearrange("p (b n) -> p b n", b=BLK)
        sc_ = f_.rearrange("p h t -> p (h t)").rearrange("p (b h t) -> p b h t", b=BLK, h=HG)
        o_ = kd
        gate_w = mixT[:, 0:4, :].rearrange("p a b -> p (a b)").rearrange("p (g j n) -> p g j n", g=2, j=4)
        ffn = cut(0, FT, L)
        silu_t = cut(5632, 2, L)

        sqf = sq[:].rearrange("p k t -> p (k t)")
        tokf = tok[:].rearrange("p b d -> p (b d)")

        def state(ch):
            return tokf[:, (ch - 1) * 512:ch * 512] if ch <= 4 else sqf[:, (ch - 5) * 512:(ch - 4) * 512]

        def piece(at, *shape):
            n = 1
            for v in shape:
                n *= v
            v = route[:, at:at + n]
            return v.rearrange("p (a b) -> p a b", b=shape[1]) if len(shape) == 2 else (
                v.rearrange("p (a b c) -> p a b c", b=shape[1], c=shape[2]) if len(shape) == 3 else v)

        g8 = piece(0, BLK, 8)
        g_top = piece(16, BLK, 8)
        e_log = piece(32, BLK, EXPERTS)
        e_top = piece(96, BLK, 8)
        R_one = piece(112, 2, BLK * EXPERTS)
        R_chosen = piece(240, BLK, EXPERTS)
        counts = piece(304, EXPERTS)
        upto = piece(336, EXPERTS)
        starts_f = piece(368, EXPERTS)
        place = piece(400, BLK, EXPERTS)
        g_one = piece(464, BLK, GROUPS)
        g_pen = piece(472, BLK, GROUPS)
        cols = piece(480, 2, BLK)
        e_idx = piece(484, BLK, 2)
        g_idx = piece(488, BLK)
        g_sum = piece(490, BLK)
        e_diff = piece(492, BLK)
        w_top = piece(494, 2, BLK)
        wins_f = piece(498, EXPERTS)
        most = piece(530, 1)
        lb = small[:, 0:4]
        one_lb = small[:, 4:8]
        lru_c = small[:, 8:12]
        lru_nc = small[:, 12:16]
        t4 = small[:, 16:20]
        u4 = small[:, 20:24]
        t8 = small[:, 24:32]
        m4 = small[:, 32:36]

        ps = ctx.enter_context(nc.psum_tensor("ps", [P, 8, 512], F32))

        arrived = [sem(f"arrived{i}") for i in range(SLOTS)]
        chunk_used = sem("chunk_used")
        ada_used = sem("ada_used")
        x_there, par_there, wr_there, lru_there = sem("x_there"), sem("par_there"), sem("wr_there"), sem("lru_there")
        consts_ready = sem("consts_ready")
        pool_step, dve_step, act_step = sem("pool_step"), sem("dve_step"), sem("act_step")
        par_tr, par_taken = sem("par_tr"), sem("par_taken")
        xT_tr, xT_ready = sem("xT_tr"), sem("xT_ready")
        silu_c_ready, ada_done, mod_ready = sem("silu_c_ready"), sem("ada_done"), sem("mod_ready")
        sq_ready = [sem(f"sq_ready{i}") for i in range(7)]
        ssq_ready = [sem(f"ssq_ready{i}") for i in range(7)]
        std_ready = [sem(f"std_ready{i}") for i in range(7)]
        scaled = [sem(f"scaled{i}") for i in range(6)]
        h_ready = [sem(f"h_ready{i}") for i in range(2)]
        tile_ready, tile_taken = sem("tile_ready"), sem("tile_taken")
        dots_ready, dots_taken, relu_used = sem("dots_ready"), sem("dots_taken"), sem("relu_used")
        score_raw, score_masked = sem("score_raw"), sem("score_masked")
        sel_raw, sel_ready = sem("sel_raw"), sem("sel_ready")
        forget_abs, forget_ln, log_f_ready = sem("forget_abs"), sem("forget_ln"), sem("log_f_ready")
        cum_done, cum_taken = sem("cum_done"), sem("cum_taken")
        logits_done, logits_taken, logits_ready = sem("logits_done"), sem("logits_taken"), sem("logits_ready")
        probs_ready, diag_ready = sem("probs_ready"), sem("diag_ready")
        pt_done, pt_taken, pv_done, pv_taken = sem("pt_done"), sem("pt_taken"), sem("pv_done"), sem("pv_taken")
        mix_ready = sem("mix_ready")
        mo_done, mo_taken = sem("mo_done"), sem("mo_taken")
        route_done, gate_max, gate_exp = sem("route_done"), sem("gate_max"), sem("gate_exp")
        top_diff, top_exp = sem("top_diff"), sem("top_exp")
        htr_done, htr_taken_a, htr_taken_v = sem("htr_done"), sem("htr_taken_a"), sem("htr_taken_v")
        choice_ready, rank_done, pick_ready, windows_ready = sem("choice_ready"), sem("rank_done"), sem("pick_ready"), sem("windows_ready")
        gather_done, gather_taken_a, gather_taken_v = sem("gather_done"), sem("gather_taken_a"), sem("gather_taken_v")
        k_moved = sem("k_moved")
        pad_ready, w_all_ready = sem("pad_ready"), sem("w_all_ready")
        windows_copied, rows_found = sem("windows_copied"), sem("rows_found")
        gu_done, silu_done, act_ready = sem("gu_done"), sem("silu_done"), sem("act_ready")
        turn_done, turn_taken, y_taken_a, y_taken_v = sem("turn_done"), sem("turn_taken"), sem("y_taken_a"), sem("y_taken_v")
        w_y_done, w_comb_done = sem("w_y_done"), sem("w_comb_done")
        comb_done, comb_taken = sem("comb_done"), sem("comb_taken")
        u2_done, u2_taken = sem("u2_done"), sem("u2_taken")
        f_sig, f_ready, f_ln, b_ready = sem("f_sig"), sem("f_ready"), sem("f_ln"), sem("b_ready")
        decay_ready, last_diff, last_exp = sem("decay_ready"), sem("last_diff"), sem("last_exp")
        q_sig, kd_ready, ks_ready, qd_ready = sem("q_sig"), sem("kd_ready"), sem("ks_ready"), sem("qd_ready")
        kst_done, kst_taken, hsc_done, hsc_ready = sem("kst_done"), sem("kst_taken"), sem("hsc_done"), sem("hsc_ready")
        kv_done, o_done, o_taken, o_sq = sem("kv_done"), sem("o_done"), sem("o_taken"), sem("o_sq")
        o_ssq, g_sig, sg_ready = sem("o_ssq"), sem("g_sig"), sem("sg_ready")
        xc_ready, gates_done, gates_ready, decays_ready = sem("xc_ready"), sem("gates_done"), sem("gates_ready"), sem("decays_ready")
        o_std, half_power, power_root = sem("o_std"), sem("half_power"), sem("power_root")
        gelu_in, gelu_sig, lru_par = sem("gelu_in"), sem("gelu_sig"), sem("lru_par")
        lru_par_a = sem("lru_par_a")
        state_ready = sem("state_ready")
        mix2_ready = sem("mix2_ready")
        ffn_done, ffn_silu, ffn_taken = sem("ffn_done"), sem("ffn_silu"), sem("ffn_taken")
        down_done, down_taken = sem("down_done"), sem("down_taken")
        otr_done, otr_taken_a, otr_taken_v, stored = sem("otr_done"), sem("otr_taken_a"), sem("otr_taken_v"), sem("stored")

        block = ctx.enter_context(nc.Block())

        def ada_part(ch):
            if ch < ADA_FIRST:
                return cut(5888 + ch * ADA_W, ADA_W)
            return tokf[:, (ch % 2) * ADA_W:(ch % 2 + 1) * ADA_W]

        def ada_arrived(eng, ch):
            n = NUMBER["ada", ch]
            eng.wait_ge(arrived[n % SLOTS], ARRIVED[n])
            return weights("ada", ch, KT, ADA_W)

        def slot(n):
            return ring[:, n % SLOTS, :]

        def weights(kind, c, k, n):
            return slot(NUMBER[kind, c])[:, 0:k * n].rearrange("p (k n) -> p k n", n=n)

        def expert_weights(s):
            v = ring[:, s, :]
            return (v[:, 0:2 * KT * FE].rearrange("p (h k n) -> p h k n", h=2, k=KT),
                    v[:, 2 * KT * FE:3 * KT * FE].rearrange("p (k n) -> p k n", n=D))

        @block.sync
        def _(sp):
            def free(n):
                if n >= SLOTS:
                    kind, c, _ = ORDER[n - SLOTS]
                    if kind == "ada":
                        sp.wait_ge(ada_used, c + 1)
                    else:
                        sp.wait_ge(chunk_used, PE_USED[n - SLOTS])

            def load_ada(c):
                n = NUMBER["ada", c]
                free(n)
                sp.dma_start(weights("ada", c, KT, ADA_W),
                             w_ada[0].rearrange("(k p) n -> p k n", p=P)[:, :, c * ADA_W:(c + 1) * ADA_W]
                             ).then_inc(arrived[n % SLOTS], 16)

            sp.dma_start(tok[:], x[0].rearrange("(b p) d -> p b d", p=P)).then_inc(x_there, 16)
            for ch in range(ADA_FIRST):
                load_ada(ch)
            for ch, (lo, hi) in enumerate(IN_CHUNKS):
                n = NUMBER["in", ch]
                free(n)
                sp.dma_start(weights("in", ch, KT, hi - lo),
                             w_in[0].rearrange("(k p) n -> p k n", p=P)[:, :, lo:hi]
                             ).then_inc(arrived[n % SLOTS], 16)
            for ch in range(ADA_FIRST, ADA_N):
                load_ada(ch)
            for ch in range(2):
                n = NUMBER["out", ch]
                free(n)
                sp.dma_start(weights("out", ch, KT, 512),
                             w_out[0].rearrange("(k p) n -> p k n", p=P)[:, :, ch * 512:ch * 512 + 512]
                             ).then_inc(arrived[n % SLOTS], 16)
            gate_d = w_gate[0].rearrange("e (p k) f -> p e (k f)", k=KT)
            up_d = w_up[0].rearrange("e (p k) f -> p e (k f)", k=KT)
            down_d = w_down[0].rearrange("e (k p) d -> p e k d", p=P)
            sp.wait_ge(ada_used, ADA_N)
            with sp.Fori(0, EXPERTS // SLOTS) as i:
                for u in range(SLOTS):
                    s = (EXPERT0 + u) % SLOTS
                    gu_w, dn = expert_weights(s)
                    sp.wait_ge(chunk_used, i * SLOTS + (USED0 + u - SLOTS + 1))
                    e = bass.ds(i * SLOTS + u, 1)
                    sp.dma_start(gu_w[:, 0].rearrange("p k n -> p (k n)"), gate_d[:, e, :].rearrange("p e f -> p (e f)")
                                 ).then_inc(arrived[s], 16)
                    sp.dma_start(gu_w[:, 1].rearrange("p k n -> p (k n)"), up_d[:, e, :].rearrange("p e f -> p (e f)")
                                 ).then_inc(arrived[s], 16)
                    sp.dma_start(dn, down_d[:, e, :, :].rearrange("p e k d -> p (e k) d")
                                 ).then_inc(arrived[s], 16)
            in2 = w_in_2[0].rearrange("(k p) n -> p k n", p=P)
            for ch, parts in enumerate([[(256, 1024)], [(0, 256), (1024, 1536)], [(2048, 2816)],
                                        [(2816, 3072), (1536, 2048)]]):
                n = NUMBER["in2", ch]
                free(n)
                w, at = weights("in2", ch, KT, 768), 0
                for lo, hi in parts:
                    sp.dma_start(w[:, :, at:at + hi - lo], in2[:, :, lo:hi]).then_inc(arrived[n % SLOTS], 16)
                    at += hi - lo
            for ch in range(2):
                n = NUMBER["out2", ch]
                free(n)
                sp.dma_start(weights("out2", ch, KT, 512),
                             w_out_2[0].rearrange("(k p) n -> p k n", p=P)[:, :, ch * 512:ch * 512 + 512]
                             ).then_inc(arrived[n % SLOTS], 16)
            gu = w_gate_up_2[0].rearrange("(k p) n -> p k n", p=P)
            for ch in range(FFN_N):
                n = NUMBER["ffn", ch]
                free(n)
                k = min(FFN_STEP, FT - ch * FFN_STEP) * P
                w = weights("ffn", ch, KT, 2 * k)
                for half in range(2):
                    lo = half * D_FF + ch * FFN_STEP * P
                    sp.dma_start(w[:, :, half * k:(half + 1) * k], gu[:, :, lo:lo + k]
                                 ).then_inc(arrived[n % SLOTS], 16)
            for ch in range(DOWN_N):
                n = NUMBER["down", ch]
                free(n)
                k = min(DOWN_STEP, FT - ch * DOWN_STEP)
                sp.dma_start(weights("down", ch, k, D),
                             w_down_2[0, ch * DOWN_STEP * P:(ch * DOWN_STEP + k) * P].rearrange(
                                 "(k p) n -> p k n", p=P)).then_inc(arrived[n % SLOTS], 16)
            for b in range(BLK):
                sp.wait_ge(otr_taken_a, b + 1)
                sp.wait_ge(otr_taken_v, b + 1)
                sp.dma_start(out[0, b * P:(b + 1) * P, :], tok[:, b, :]).then_inc(stored, 16)
            sp.wait_ge(stored, 16 * BLK)

        @block.gpsimd
        def _(pool):
            step = Count()
            pool.memset(ident[:], 0.0).then_inc(pool_step, 1)
            pool.memset(ones[:], 1.0).then_inc(consts_ready, 1)
            pool.memset(tri[:], 1.0).then_inc(pool_step, 1)
            pool.memset(causal[:], 0.0).then_inc(pool_step, 1)
            pool.memset(head_row[:], 1.0).then_inc(pool_step, 1)
            pool.memset(strict[:], 1.0).then_inc(pool_step, 1)
            pool.memset(reset[:], 1.0).then_inc(pool_step, 1)
            pool.memset(ncumT[:], 0.0).then_inc(consts_ready, 1)
            pool.memset(in_chunk[:], 1.0).then_inc(pool_step, 1)
            pool.wait_ge(pool_step, step.up(7))
            pool.affine_select(out=ident[:], in_=ident[:], compare_op=ALU.not_equal, fill=1.0, base=0,
                               pattern=[[-1, P]], channel_multiplier=1).then_inc(consts_ready, 1)
            pool.affine_select(out=tri[:], in_=tri[:], compare_op=ALU.is_ge, fill=0.0, base=0,
                               pattern=[[1, L]], channel_multiplier=-1).then_inc(consts_ready, 1)
            pool.affine_select(out=causal[:, P:L], in_=causal[:, P:L], compare_op=ALU.is_ge, fill=NEG, base=0,
                               pattern=[[-1, P]], channel_multiplier=1).then_inc(consts_ready, 1)
            pool.affine_select(out=head_row[:], in_=head_row[:], compare_op=ALU.is_equal, fill=0.0,
                               base=0, pattern=[[1, HEADS], [0, P]], channel_multiplier=-1
                               ).then_inc(consts_ready, 1)
            pool.affine_select(out=strict[:], in_=strict[:], compare_op=ALU.is_gt, fill=0.0, base=0,
                               pattern=[[1, P]], channel_multiplier=-1).then_inc(consts_ready, 1)
            pool.affine_select(out=in_chunk[:], in_=in_chunk[:], compare_op=ALU.is_ge, fill=0.0, base=0,
                               pattern=[[1, P]], channel_multiplier=-1).then_inc(pool_step, 1)
            pool.wait_ge(pool_step, step.up())
            pool.affine_select(out=in_chunk[:], in_=in_chunk[:], compare_op=ALU.is_ge, fill=0.0, base=0,
                               pattern=[[-CHUNK, P // CHUNK], [0, CHUNK]], channel_multiplier=1
                               ).then_inc(consts_ready, 1)
            pool.memset(reset[:, 0:L:CHUNK], 0.0).then_inc(consts_ready, 1)
            pool.iota(neg_dist[:, 0:P], [[1, P]], base=0, channel_multiplier=-1,
                      allow_small_or_imprecise_dtypes=True).then_inc(consts_ready, 1)
            pool.iota(neg_dist[:, P:NK], [[1, L]], base=-P, channel_multiplier=-1,
                      allow_small_or_imprecise_dtypes=True).then_inc(consts_ready, 1)
            pool.iota(col_no[:], [[1, PAIRS]], base=0, channel_multiplier=0,
                      allow_small_or_imprecise_dtypes=True).then_inc(consts_ready, 1)

            def behind(t, fill, inc):
                pool.affine_select(out=t[:, 0:P], in_=t[:, 0:P], compare_op=ALU.is_ge, fill=fill, base=0,
                                   pattern=[[-1, P]], channel_multiplier=1).then_inc(inc, 1)
                pool.affine_select(out=t[:, P:NK], in_=t[:, P:NK], compare_op=ALU.is_ge, fill=fill, base=P,
                                   pattern=[[-1, L]], channel_multiplier=1).then_inc(inc, 1)

            def ada_sum(ch):
                w = ada_arrived(pool, ch)
                pool.tensor_tensor(w, w, silu_c[:].unsqueeze(2).broadcast_to([P, KT, ADA_W]), ALU.mult
                                   ).then_inc(pool_step, 1)
                for half in (4, 2):
                    pool.wait_ge(pool_step, step.up())
                    pool.tensor_tensor(w[:, 0:half, :], w[:, 0:half, :], w[:, half:2 * half, :], ALU.add
                                       ).then_inc(pool_step, 1)
                pool.wait_ge(pool_step, step.up())
                if ch >= ADA_FIRST + 2:
                    pool.wait_ge(ada_done, ch - 1)
                pool.tensor_tensor(ada_part(ch), w[:, 0, :], w[:, 1, :], ALU.add).then_inc(ada_used, 1)

            pool.wait_ge(tile_taken, 2)
            pool.dma_start(kI[64:128, :], kI[0:64, :]).then_inc(k_moved, 16)
            pool.wait_ge(tile_taken, 7)
            pool.dma_start(kA_swap[64:128, :], kA[0:64, :]).then_inc(k_moved, 16)
            pool.dma_start(kA_swap[0:64, :], kA[64:128, :]).then_inc(k_moved, 16)
            pool.wait_ge(xT_tr, 4)
            pool.wait_ge(silu_c_ready, 1)
            ada_sum(ADA_FIRST)
            pool.wait_ge(score_raw, 2 * HEADS)
            behind(score, MASKED, score_masked)
            pool.wait_ge(sel_raw, 1)
            behind(sel_bias, NEG, sel_ready)
            for ch in range(ADA_FIRST + 1, ADA_N):
                ada_sum(ch)
            pool.wait_ge(mo_taken, KT)
            pool.memset(xsT[:, :, PAIRS:COLS], 0.0).then_inc(pad_ready, 1)
            pool.memset(y_sb, 0.0).then_inc(pad_ready, 1)
            pool.memset(turned[:, 1, :], 0.0).then_inc(pad_ready, 1)
            pool.memset(rank, 0.0).then_inc(pad_ready, 1)
            pool.memset(w_all, 0.0).then_inc(pad_ready, 1)
            pool.memset(gate_w[:], 0.0).then_inc(pool_step, 1)
            pool.wait_ge(pool_step, step.up())
            for g, w in enumerate((lru_wa_2, lru_wx_2)):
                for odd in range(2):
                    q = slice(64 * odd, 64 * odd + 64)
                    pool.dma_start(gate_w[q, g, :, q], w[0].rearrange("(j o) d e -> o d j e", o=2)[odd]
                                   ).then_inc(lru_there, 16)

        @block.tensor
        def _(pe):
            def chunk_there(kind, c):
                n = NUMBER[kind, c]
                pe.wait_ge(arrived[n % SLOTS], ARRIVED[n])

            def sum_squares(i, bank, col=0, tiles=range(KT), n=L):
                for k in tiles:
                    last = pe.matmul(ps[:, bank, col:col + n], lhsT=ones[:], rhs=sq[:, k, :],
                                     start=k == tiles[0], stop=k == tiles[-1])
                last.then_inc(ssq_ready[i], 1)

            def product(o, w_of, rhs_of, k_n=KT):
                for k in range(k_n):
                    last = pe.matmul(o, lhsT=w_of(k), rhs=rhs_of(k), start=k == 0, stop=k == k_n - 1)
                return last

            pe.wait_ge(consts_ready, N_CONST)
            pe.wait_ge(par_there, 16 * N_PAR)
            pe.transpose(ps[:, 2, 0:PA_N], hT[0:PA_N, 0, 0:P], ident[0:PA_N, 0:PA_N]).then_inc(par_tr, 1)
            pe.transpose(ps[:, 3, 0:PB_N], hT[0:PB_N, 1, 0:P], ident[0:PB_N, 0:PB_N]).then_inc(par_tr, 1)
            pe.wait_ge(x_there, 16)
            for q, bank in enumerate((0, 1, 4, 5)):
                for k in (2 * q, 2 * q + 1):
                    for b in range(BLK):
                        at = (k % 2) * L + b * P
                        last = pe.transpose(ps[:, bank, at:at + P], tok[:, b, k * P:(k + 1) * P], ident[:])
                last.then_inc(xT_tr, 1)

            def ada(ch):
                pe.wait_ge(ada_used, ch + 1)
                for i in range(ADA_W // P):
                    m = ch * (ADA_W // P) + i
                    last = pe.matmul(ps[:, 7, m:m + 1], lhsT=ada_part(ch)[:, i * P:(i + 1) * P], rhs=ones[:, 0:1],
                                     start=True, stop=True)
                last.then_inc(ada_done, 1)

            pe.wait_ge(sq_ready[0], 2)
            sum_squares(0, 6)
            for ch in range(ADA_FIRST):
                ada(ch)

            unit = Count()

            def bank_of_unit():
                u = unit.up() - 1
                if u >= 2:
                    pe.wait_ge(tile_taken, u - 1)
                return ps[:, u % 2, :]

            def features(ch, cols):
                w = weights("in", ch, KT, IN_CHUNKS[ch][1] - IN_CHUNKS[ch][0])
                o = bank_of_unit()
                return product(o[:, 0:L], lambda k: cols(w[:, k, :]), lambda k: hT[:, k, :])

            def tokens(ch, lo, hi, blocks, bias=None):
                w = weights("in", ch, KT, IN_CHUNKS[ch][1] - IN_CHUNKS[ch][0])
                o, n = bank_of_unit(), hi - lo
                for i, b in enumerate(blocks):
                    for k in range(KT):
                        last = pe.matmul(o[:, i * n:(i + 1) * n], lhsT=hT[:, k, b * P:(b + 1) * P],
                                         rhs=w[:, k, lo:hi], start=k == 0, stop=k == KT - 1 and bias is None)
                    if bias is not None:
                        last = pe.matmul(o[:, i * n:(i + 1) * n], lhsT=ones[0:1, :], rhs=bias,
                                         start=False, stop=True)
                return last

            pe.wait_ge(h_ready[0], KT)
            chunk_there("in", 0)
            tokens(0, IW - IQ, BQ - IQ, (0, 1)).then_inc(tile_ready, 1)
            ik = IK - IQ
            w = weights("in", 0, KT, BQ - IQ)
            product(bank_of_unit()[0:64, 0:L], lambda k: w[:, k, ik:ik + 64], lambda k: hT[:, k, :]
                    ).then_inc(tile_ready, 1)
            for j in range(4):
                last = features(0, lambda w: w[:, j * P:(j + 1) * P]).then_inc(tile_ready, 1)
            pe.wait_ge(tile_taken, 6)
            pe.sem_inc(chunk_used, 1)

            def dots(h):
                bank, q = 2 + h % 2, slice(64 * (h % 2), 64 * (h % 2) + 64)
                if h >= 2:
                    pe.wait_ge(dots_taken, h - 1)
                pe.matmul(ps[:, bank, 0:P], lhsT=qI[q, h // 2, 0:P], rhs=kI[q, 0:P], start=True, stop=True)
                pe.matmul(ps[:, bank, P:NK], lhsT=qI[q, h // 2, P:L], rhs=kI[q, :],
                          start=True, stop=True).then_inc(dots_ready, 1)

            pe.wait_ge(par_taken, 2)
            pe.wait_ge(k_moved, 16)
            chunk_there("in", 1)
            dots(0)
            dots(1)
            features(1, lambda w: w[:, AK:AV]).then_inc(tile_ready, 1)
            dots(2)
            dots(3)
            tokens(1, AV, IQ, (0, 1)).then_inc(tile_ready, 1)
            for j in range(4):
                if j < 2:
                    dots(4 + 2 * j)
                    dots(5 + 2 * j)
                features(1, lambda w: w[:, j * P:(j + 1) * P]).then_inc(tile_ready, 1)
            pe.wait_ge(tile_ready, 12)
            pe.sem_inc(chunk_used, 1)

            def head(n):
                if n < HEADS:
                    kv, half = n // 4, n % 2
                    q = slice(64 * half, 64 * half + 64)
                    return q, qA[q, n // 2, :], (kA if kv == half else kA_swap)[q, :], vA[:, :, 64 * kv:64 * kv + 64]
                h = n - HEADS
                q = slice(64 * (h % 2), 64 * (h % 2) + 64)
                return q, qB[q, h // 2, :], kB[q, h // 2, :], vB[:, :, h * 64:(h + 1) * 64]

            def attend(n):
                if n < 2 * HEADS:
                    _, q, k, _ = head(n)
                    bank, more = 2 + n % 2, n >= HEADS
                    if n >= 2:
                        pe.wait_ge(logits_taken, n - 1)
                    else:
                        pe.wait_ge(dots_taken, HEADS)
                    for o, qb, keys in ((ps[:, bank, 0:P], 0, slice(0, P)), (ps[:, bank, P:NK], 1, slice(0, L))):
                        last = pe.matmul(o, lhsT=q[:, qb * P:(qb + 1) * P], rhs=k[:, keys], start=True,
                                         stop=not more)
                        if more:
                            last = pe.matmul(o, lhsT=head_row[:, n - HEADS, :], rhs=ncumT[:, keys],
                                             start=False, stop=True)
                    last.then_inc(logits_done, 1)
                if 1 <= n <= 2 * HEADS:
                    m = n - 1
                    bank = 4 + m % 2
                    pe.wait_ge(diag_ready, m + 1)
                    if m >= 2:
                        pe.wait_ge(pt_taken, m - 1)
                    for s in range(3):
                        last = pe.matmul(ps[:, bank, s * P:(s + 1) * P], lhsT=prob[:, m % 2, s * P:(s + 1) * P],
                                         rhs=diag[:, m % 2, min(s, 1), :], start=True, stop=True)
                    last.then_inc(pt_done, 1)
                if 2 <= n:
                    m = n - 2
                    q, _, _, v = head(m)
                    pe.wait_ge(pt_taken, m + 1)
                    if m % 2 == 0 and m:
                        pe.wait_ge(pv_taken, m // 2)
                    pe.matmul(ps[q, 6, 0:L], lhsT=v[:, 0, :], rhs=probT[:, m % 2, 0:L], start=True, stop=False)
                    pe.matmul(ps[q, 6, P:L], lhsT=v[:, 1, :], rhs=probT[:, m % 2, L:NK], start=False,
                              stop=True).then_inc(pv_done, 1)

            def bq(j):
                features(3, lambda w: w[:, j * P:(j + 1) * P]).then_inc(tile_ready, 1)

            pe.wait_ge(k_moved, 48)
            attend(0)
            chunk_there("in", 2)
            tokens(2, BF - BK - 256, BF - BK - 256 + 8, (0, 1), bias=brow[0:1, 0:8]).then_inc(tile_ready, 1)
            features(2, lambda w: w[:, 0:P]).then_inc(tile_ready, 1)
            attend(1)
            features(2, lambda w: w[:, P:2 * P]).then_inc(tile_ready, 1)
            attend(2)
            tokens(2, BV - BK - 256, BF - BK - 256, (0,)).then_inc(tile_ready, 1)
            attend(3)
            tokens(2, BV - BK - 256, BF - BK - 256, (1,)).then_inc(tile_ready, 1)
            pe.wait_ge(tile_ready, 17)
            pe.sem_inc(chunk_used, 1)
            attend(4)
            chunk_there("in", 3)
            bq(0)
            bq(1)
            attend(5)
            bq(2)
            bq(3)
            pe.wait_ge(log_f_ready, 1)
            pe.wait_ge(mod_ready, 1)
            lf = forget[:, 2, :].rearrange("p (b h) -> p b h", b=BLK)
            pe.matmul(ps[:, 7, 64:72], lhsT=tri[:, 0:P], rhs=lf[:, 0, :], start=True, stop=True)
            pe.matmul(ps[:, 7, 72:80], lhsT=ones[:], rhs=lf[:, 0, :], start=True, stop=False)
            pe.matmul(ps[:, 7, 72:80], lhsT=tri[:, 0:P], rhs=lf[:, 1, :], start=False, stop=True)
            pe.matmul(ps[0:HEADS, 7, 128:384], lhsT=lf[:, 0, :], rhs=tri[:], start=True, stop=False)
            pe.matmul(ps[0:HEADS, 7, 256:384], lhsT=lf[:, 1, :], rhs=tri[:, 0:P], start=False,
                      stop=True).then_inc(cum_done, 1)
            attend(6)
            bq(4)
            attend(7)
            bq(5)
            pe.wait_ge(tile_taken, 23)
            pe.sem_inc(chunk_used, 1)
            pe.wait_ge(cum_taken, 2)
            for n in range(HEADS, 2 * HEADS + 2):
                attend(n)
                if n % 2 == 0:
                    ada(ADA_FIRST + (n - HEADS) // 2)

            pe.wait_ge(sq_ready[5], 2)
            sum_squares(5, 6, 0, range(4))
            sum_squares(5, 6, L, range(4, 8))
            pe.wait_ge(mix_ready, KT)
            for m in range(KT):
                ch, i = divmod(m, 4)
                if i == 0:
                    chunk_there("out", ch)
                w = weights("out", ch, KT, 512)
                if m >= 4:
                    pe.wait_ge(mo_taken, m - 3)
                product(ps[:, m % 4, 0:L], lambda k: w[:, k, i * P:(i + 1) * P],
                        lambda k: mixT[:, k, :]).then_inc(mo_done, 1)
                if i == 3:
                    pe.wait_ge(mo_done, m + 1)
                    pe.sem_inc(chunk_used, 1)

            pe.wait_ge(sq_ready[1], 2)
            sum_squares(1, 6)
            pe.wait_ge(wr_there, 16 * N_WR)
            pe.wait_ge(h_ready[1], KT)
            nr = GROUPS + EXPERTS
            for b in range(BLK):
                for k in range(KT):
                    pe.matmul(ps[:, 4, b * nr:(b + 1) * nr], lhsT=hT[:, k, b * P:(b + 1) * P], rhs=wr[:, k, :],
                              start=k == 0, stop=False)
                last = pe.matmul(ps[:, 4, b * nr:(b + 1) * nr], lhsT=ones[0:1, :], rhs=brow[0:1, 8:8 + nr],
                                 start=False, stop=True)
            last.then_inc(route_done, 1)
            pe.wait_ge(mo_taken, KT)
            for i in range(4):
                b, half = divmod(i, 2)
                for k in range(4):
                    last = pe.transpose(ps[:, i, k * P:(k + 1) * P], hT[:, 4 * half + k, b * P:(b + 1) * P], ident[:])
                last.then_inc(htr_done, 1)
            pe.wait_ge(choice_ready, 1)
            pe.matmul(ps[:, 5, 0:32], lhsT=strict[:], rhs=R_chosen[:, 0, :], start=True, stop=True)
            pe.matmul(ps[:, 5, 32:64], lhsT=ones[:], rhs=R_chosen[:, 0, :], start=True, stop=False)
            pe.matmul(ps[:, 5, 32:64], lhsT=strict[:], rhs=R_chosen[:, 1, :], start=False, stop=True)
            pe.matmul(ps[:, 5, 64:96], lhsT=ones[:], rhs=R_chosen[:, 0, :], start=True, stop=False)
            pe.matmul(ps[:, 5, 64:96], lhsT=ones[:], rhs=R_chosen[:, 1, :], start=False,
                      stop=True).then_inc(rank_done, 1)
            pe.wait_ge(pick_ready, BLK)
            pe.wait_ge(htr_taken_a, 4)
            for j in range(KT):
                if j >= 4:
                    if j % 2 == 0:
                        pe.wait_ge(gather_taken_a, (j - 4) // 2 + 1)
                    else:
                        pe.wait_ge(gather_taken_v, (j - 4) // 2 + 1)
                for b in range(BLK):
                    last = pe.matmul(ps[:, j % 4, :], lhsT=tok[:, b, j * P:(j + 1) * P], rhs=pick[:, b, :],
                                     start=b == 0, stop=b == BLK - 1)
                last.then_inc(gather_done, 1)

            def gate_up(e0, u):
                for h in range(2):
                    gu_w, _ = expert_weights((e0 + h) % SLOTS)
                    for k in range(KT):
                        last = pe.matmul(ps[WIN * h:WIN * (h + 1), 0, :].rearrange("p (g n) -> p g n", g=2),
                                         lhsT=xw[:, u, k, WIN * h:WIN * (h + 1)], rhs=gu_w[:, :, k, :],
                                         start=k == 0, stop=k == KT - 1)
                return last

            def turn(u):
                for b in range(BLK):
                    pe.transpose(ps[:, 1, FE + b * P:FE + (b + 1) * P], put[:, u, b].rearrange("p h r -> p (h r)"),
                                 ident[:])
                for f in range(2):
                    last = pe.transpose(ps[:, 1, f * P:(f + 1) * P], act_e[:, f * P:(f + 1) * P], ident[:])
                return last

            def down(e0, u):
                for h in range(2):
                    _, dn = expert_weights((e0 + h) % SLOTS)
                    for half in range(2):
                        for k in range(2):
                            at = k * P + WIN * h
                            last = pe.matmul(ps[WIN * h:WIN * (h + 1), 2 + half, :], lhsT=turned[:, u, at:at + WIN],
                                             rhs=dn[:, k, half * 512:(half + 1) * 512], start=k == 0, stop=k == 1)
                return last

            def combine(u, tiles):
                for j in tiles:
                    last = pe.matmul(ps[:, 4 + j // 2, (j % 2) * L:(j % 2 + 1) * L], lhsT=y_sb[:, j * P:(j + 1) * P],
                                     rhs=turned[:, u, FE:FE + L], start=False, stop=False, skip_group_check=True)
                return last

            pe.wait_ge(gather_taken_a, 4)
            pe.wait_ge(gather_taken_v, 4)
            pe.wait_ge(pad_ready, 5)
            pe.wait_ge(windows_ready, 2)
            for j in range(4):
                pe.matmul(ps[:, 4 + j, :], lhsT=ones[:], rhs=turned[:, 1, :], start=True, stop=False,
                          skip_group_check=True)
            too_many = pe.value_load(flag_i[0:1, 0:1], min_val=0, max_val=1)
            with pe.If(too_many < 1):
                with pe.Fori(0, EXPERTS // SLOTS) as i:
                    for u in range(2):
                        e0, n = EXPERT0 + 2 * u, i * 2 + u
                        pe.wait_ge(windows_copied, n + 1)
                        for h in range(2):
                            s = (e0 + h) % SLOTS
                            pe.wait_ge(arrived[s], i * 48 + ARRIVED[e0 + h])
                        gate_up(e0, u).then_inc(gu_done, 1)
                        pe.wait_ge(y_taken_a, n + 1)
                        pe.wait_ge(y_taken_v, n + 1)
                        combine(1 - u, range(0, 5))
                        pe.wait_ge(act_ready, n + 2)
                        turn(u).then_inc(turn_done, 1)
                        combine(1 - u, range(5, KT))
                        pe.wait_ge(turn_taken, n + 1)
                        down(e0, u).then_inc(chunk_used, 2)
                pe.wait_ge(y_taken_a, EXPERTS // 2 + 1)
                pe.wait_ge(y_taken_v, EXPERTS // 2 + 1)
                combine(1, range(KT)).then_inc(comb_done, 1)
            with pe.Else():
                with pe.Fori(0, EXPERTS // SLOTS) as i:
                    for u in range(2):
                        e0 = EXPERT0 + 2 * u
                        with pe.Fori(0, WINDOWS) as w:
                            n = i * (2 * WINDOWS) + w + u * WINDOWS
                            for h in range(2):
                                s = (e0 + h) % SLOTS
                                pe.wait_ge(arrived[s], i * 48 + ARRIVED[e0 + h])
                            pe.wait_ge(windows_copied, n + 1)
                            gate_up(e0, 0).then_inc(gu_done, 1)
                            pe.wait_ge(act_ready, n + 2)
                            turn(0).then_inc(turn_done, 1)
                            pe.wait_ge(turn_taken, n + 1)
                            down(e0, 0).then_inc(w_y_done, 1)
                            pe.wait_ge(y_taken_a, n + 2)
                            pe.wait_ge(y_taken_v, n + 2)
                            combine(0, range(KT)).then_inc(w_comb_done, 1)
                        pe.wait_ge(w_comb_done, i * (2 * WINDOWS) + (u + 1) * WINDOWS)
                        pe.sem_inc(chunk_used, 2)
                pe.wait_ge(w_comb_done, EXPERTS // 2 * WINDOWS)
                pe.sem_inc(comb_done, 1)

            pe.wait_ge(sq_ready[2], 2)
            sum_squares(2, 6)
            pe.wait_ge(sq_ready[3], 2)
            sum_squares(3, 6)
            unit2 = Count()

            def bank2():
                u = unit2.up() - 1
                if u >= 4:
                    pe.wait_ge(u2_taken, u - 3)
                return ps[:, u % 4, :]

            def features2(ch, lo):
                w = weights("in2", ch, KT, 768)
                product(bank2()[:, 0:L], lambda k: w[:, k, lo:lo + P], lambda k: hT[:, k, :]).then_inc(u2_done, 1)

            def chunk2_used(units):
                pe.wait_ge(u2_done, units)
                pe.sem_inc(chunk_used, 1)

            pe.wait_ge(scaled[3], KT)
            chunk_there("in2", 0)
            for i in range(6):
                features2(0, i * P)
            chunk2_used(6)
            chunk_there("in2", 1)
            features2(1, 0)
            features2(1, P)
            w = weights("in2", 1, KT, 768)
            for b in range(BLK):
                product(bank2(), lambda k: hT[:, k, b * P:(b + 1) * P], lambda k: w[:, k, 256:768]).then_inc(u2_done, 1)
            chunk2_used(10)
            chunk_there("in2", 2)
            for i in range(6):
                features2(2, i * P)
            chunk2_used(16)

            pe.wait_ge(ks_ready, 1)
            for b in range(BLK):
                for h in range(HG):
                    last = pe.transpose(ps[:, 4 + b, h * P:(h + 1) * P], ks[:, h, b * P:(b + 1) * P], ident[:])
                last.then_inc(kst_done, 1)
            pe.wait_ge(kd_ready, 1)
            pe.wait_ge(qd_ready, 1)
            for b in range(BLK):
                t = slice(b * P, (b + 1) * P)
                for h in range(HG):
                    last = pe.matmul(ps[:, 6 + b, h * P:(h + 1) * P], lhsT=kd[:, h, t], rhs=raw_q[:, h, t],
                                     start=True, stop=True)
                last.then_inc(hsc_done, 1)
            chunk_there("in2", 3)
            features2(3, 0)
            features2(3, P)
            pe.wait_ge(kst_taken, 2)
            pe.wait_ge(hsc_ready, 2)
            for ch in range(CHUNKS - 1):
                b, r = divmod(ch, P // CHUNK)
                rows = slice(CHUNK * r, CHUNK * (r + 1))
                if ch >= 4:
                    pe.wait_ge(state_ready, ch - 3)
                for h in range(HG):
                    n = slice(h * P, (h + 1) * P)
                    last = pe.matmul(ps[:, 4 + ch % 4, n], lhsT=ksT[rows, b, n], rhs=v_[rows, b, n],
                                     start=True, stop=True)
                last.then_inc(kv_done, 1)
            pe.wait_ge(state_ready, CHUNKS - 1)
            pe.wait_ge(xc_ready, 4)
            pe.wait_ge(lru_there, 16 * 4)
            for g in range(2):
                for j in range(4):
                    last = pe.matmul(ps[:, 4 + 2 * g + j // 2, (j % 2) * L:(j % 2 + 1) * L],
                                     lhsT=gate_w[:, g, j, :], rhs=xc[:, j, :], start=True, stop=True)
                last.then_inc(gates_done, 1)
            for i in range(4):
                features2(3, 256 + i * P)
            chunk2_used(22)
            pe.wait_ge(gates_ready, 8)
            for h in range(HG):
                n = slice(h * P, (h + 1) * P)
                o = ps[:, 4 + h // 2, (h % 2) * L:(h % 2 + 1) * L]
                for b in range(BLK):
                    pe.matmul(o[:, b * P:(b + 1) * P], lhsT=v_[:, b, n], rhs=sc_[:, b, h, :],
                              start=h % 2 == 0 and b == 0, stop=False, skip_group_check=True)
                for ch in range(1, CHUNKS):
                    t = slice(ch * CHUNK, (ch + 1) * CHUNK)
                    last = pe.matmul(o[:, t], lhsT=state(ch)[:, n], rhs=raw_q[:, h, t], start=False,
                                     stop=ch == CHUNKS - 1, skip_group_check=True)
                if h % 2:
                    last.then_inc(o_done, 1)
            pe.wait_ge(o_sq, 2)
            for i in range(2):
                pe.matmul(ps[:, 6 + i, :], lhsT=ones[:], rhs=sqf[:, i * 512:(i + 1) * 512], start=True,
                          stop=True).then_inc(o_ssq, 1)

            pe.wait_ge(mix2_ready, 8)
            for m in range(KT):
                ch, i = divmod(m, 4)
                if i == 0:
                    chunk_there("out2", ch)
                w = weights("out2", ch, KT, 512)
                if m >= 4:
                    pe.wait_ge(mo_taken, KT + m - 3)
                else:
                    pe.wait_ge(u2_taken, 22)
                product(ps[:, m % 4, 0:L], lambda k: w[:, k, i * P:(i + 1) * P],
                        lambda k: mixT[:, k, :]).then_inc(mo_done, 1)
                if i == 3:
                    pe.wait_ge(mo_done, KT + m + 1)
                    pe.sem_inc(chunk_used, 1)

            pe.wait_ge(sq_ready[4], 2)
            sum_squares(4, 6)
            pe.wait_ge(scaled[4], KT)
            for t in range(FT):
                ch, i = divmod(t, FFN_STEP)
                n = min(FFN_STEP, FT - ch * FFN_STEP)
                if i == 0:
                    chunk_there("ffn", ch)
                w = weights("ffn", ch, KT, 2 * n * P)
                if t >= 4:
                    pe.wait_ge(ffn_taken, t - 3)
                else:
                    pe.wait_ge(mo_taken, 2 * KT)
                for half in range(2):
                    at = (half * n + i) * P
                    last = product(ps[:, t % 4, half * L:(half + 1) * L], lambda k: w[:, k, at:at + P],
                                   lambda k: hT[:, k, :])
                last.then_inc(ffn_done, 1)
                if i == n - 1:
                    pe.wait_ge(ffn_done, t + 1)
                    pe.sem_inc(chunk_used, 1)
            for t in range(FT):
                ch, i = divmod(t, DOWN_STEP)
                n = min(DOWN_STEP, FT - ch * DOWN_STEP)
                if i == 0:
                    chunk_there("down", ch)
                w = weights("down", ch, n, D)
                pe.wait_ge(ffn_taken, t + 1)
                for j in range(KT):
                    last = pe.matmul(ps[:, 4 + j // 2, (j % 2) * L:(j % 2 + 1) * L], lhsT=w[:, i, j * P:(j + 1) * P],
                                     rhs=ffn[:, t, :], start=t == 0 and j % 2 == 0, stop=t == FT - 1,
                                     skip_group_check=True)
                    if t == FT - 1 and j % 2:
                        last.then_inc(down_done, 1)
                if i == n - 1 and t < FT - 1:
                    last.then_inc(chunk_used, 1)

            pe.wait_ge(sq_ready[6], 2)
            sum_squares(6, 4)
            pe.wait_ge(scaled[5], KT)
            for i in range(4):
                b, half = divmod(i, 2)
                for k in range(4):
                    last = pe.transpose(ps[:, i, k * P:(k + 1) * P], hT[:, 4 * half + k, b * P:(b + 1) * P], ident[:])
                last.then_inc(otr_done, 1)

        @block.scalar
        def _(act):
            def rows(tile, names, name):
                lo, hi = names[name]
                return hT[lo:hi, tile, 0:P]

            for name, v in (("c", c[0]), ("b_ada", b_ada[0]), ("g_mix", g_mix[0]), ("g_ffn", g_ffn[0]),
                            ("g_final", g_final)):
                act.dma_start(rows(0, PA_ROWS, name), v.rearrange("(k p) -> k p", p=P)).then_inc(par_there, 16)
            for name, v in (("g_out_a", g_out_a[0]), ("g_out_b", g_out_b[0]), ("mix2", mix_norm_w_2[0]), ("ffn2", ffn_norm_w_2[0]),
                            ("final2", final_norm_w_2), ("lb0", hg_lb_2[0]), ("lb1", hg_lb_2[1]),
                            ("hg_norm", hg_norm_w_2[0]),
                            ("conv_w", conv_w_2[0].rearrange("w n -> (w n)")), ("conv_b", conv_b_2[0]),
                            ("lru_ba", lru_ba_2[0]), ("lru_bx", lru_bx_2[0]), ("lru_a", lru_a_2[0])):
                act.dma_start(rows(1, PB_ROWS, name), v.rearrange("(k p) -> k p", p=P)).then_inc(par_there, 16)
            act.dma_start(brow[0:1, 0:8], b_forget).then_inc(par_there, 16)
            act.dma_start(brow[0:1, 8:8 + GROUPS], b_group).then_inc(par_there, 16)
            act.dma_start(brow[0:1, 8 + GROUPS:8 + GROUPS + EXPERTS], b_router.rearrange("o g e -> o (g e)")
                          ).then_inc(par_there, 16)

            def squares(i, src, ready, first, second):
                for half, n in ((0, first), (1, second)):
                    act.wait_ge(ready, n)
                    act.activation(sq[:, 4 * half:4 * half + 4, :], src[:, 4 * half:4 * half + 4, :], ACT.Square
                                   ).then_inc(sq_ready[i], 1)

            def std_of(i, n, bank=6, parts=1):
                act.wait_ge(ssq_ready[i], parts)
                act.activation(rstd[:].rearrange("p a t -> p (a t)")[:, 0:parts * L], ps[:, bank, 0:parts * L],
                               ACT.Sqrt, scale=1.0 / n, bias=EPS).then_inc(std_ready[i], 1)

            def add_shift(i, shift):
                for k in range(KT):
                    act.wait_ge(scaled[i], k + 1)
                    act.activation(hT[:, k, :], hT[:, k, :], ACT.Identity, bias=mod[:, shift + k:shift + k + 1]
                                   ).then_inc(h_ready[i], 1)

            act.wait_ge(par_taken, 1)
            act.activation(silu_c[:], parA[:, 0:KT], ACT.Silu).then_inc(silu_c_ready, 1)
            for q, bank in enumerate((0, 1, 4, 5)):
                act.wait_ge(xT_tr, q + 1)
                act.activation(xT[:, 2 * q:2 * q + 2, :], ps[:, bank, :].rearrange("p (k t) -> p k t", k=2),
                               ACT.Copy).then_inc(xT_ready, 1)
            squares(0, xT, xT_ready, 2, 4)
            std_of(0, D)
            act.dma_start(wr[:, :, 0:GROUPS], w_group[0].rearrange("(k p) g -> p k g", p=P)).then_inc(wr_there, 16)
            for g in range(GROUPS):
                act.dma_start(wr[:, :, GROUPS + PER_GROUP * g:GROUPS + PER_GROUP * (g + 1)],
                              w_router[0, g].rearrange("(k p) e -> p k e", p=P)).then_inc(wr_there, 16)
            act.wait_ge(mod_ready, 1)
            add_shift(0, 0)

            unit = Count()

            def take(dst, src, scale=1.0):
                u = unit.up() - 1
                act.wait_ge(tile_ready, u + 1)
                act.activation(dst, src(ps[:, u % 2, :]), ACT.Copy, scale=scale).then_inc(tile_taken, 1)

            def whole(o):
                return o[:, 0:L]

            def relu_dots(h):
                act.wait_ge(dots_ready, h + 1)
                if h >= 2:
                    act.wait_ge(score_raw, 2 * (h - 1))
                act.activation(relu[:, h % 2, :], ps[:, 2 + h % 2, 0:NK], ACT.Relu).then_inc(dots_taken, 1)

            take(iwT, lambda o: o[:, 0:16].rearrange("p (b h) -> p b h", b=BLK))
            take(kI[0:64, :], lambda o: o[0:64, 0:L])
            for j in range(4):
                take(qI[:, j, :], whole)
            relu_dots(0)
            relu_dots(1)
            take(kA, whole)
            relu_dots(2)
            relu_dots(3)
            take(vA, lambda o: o[:, 0:256].rearrange("p (b n) -> p b n", b=BLK))
            for j in range(4):
                if j < 2:
                    relu_dots(4 + 2 * j)
                    relu_dots(5 + 2 * j)
                take(qA[:, j, :], whole, SCALE)

            def attend(n):
                if n < 2 * HEADS:
                    act.wait_ge(logits_ready, 2 * (n + 1))
                    if n >= 2:
                        act.wait_ge(pt_done, n - 1)
                    act.activation(prob[:, n % 2, 0:P], logit[:, n % 2, 0:P], ACT.Exp,
                                   bias=neg_max[:, n, 0:1], accum_out=p_sum[:, n, 0:1]).then_inc(act_step, 1)
                    act.activation(prob[:, n % 2, P:NK], logit[:, n % 2, P:NK], ACT.Exp,
                                   bias=neg_max[:, n, 1:2], accum_out=p_sum[:, n, 1:2]).then_inc(probs_ready, 1)
                if 1 <= n <= 2 * HEADS:
                    m = n - 1
                    act.wait_ge(pt_done, m + 1)
                    if m >= 2:
                        act.wait_ge(pv_done, m - 1)
                    act.activation(probT[:, m % 2, :], ps[:, 4 + m % 2, 0:NK], ACT.Copy).then_inc(pt_taken, 1)
                if n >= 3 and n % 2:
                    act.wait_ge(pv_done, n - 1)
                    act.activation(mixT[:, (n - 3) // 2, :], ps[:, 6, 0:L], ACT.Copy).then_inc(pv_taken, 1)

            attend(0)
            take(forget[:, 0, :], lambda o: o[:, 0:16])
            take(kB[:, 2, :], whole)
            attend(1)
            take(kB[:, 3, :], whole)
            act.wait_ge(forget_abs, 1)
            act.activation(forget[:, 1, :], forget[:, 1, :], ACT.Exp).then_inc(forget_ln, 1)
            act.wait_ge(forget_ln, 1)
            act.activation(forget[:, 1, :], forget[:, 1, :], ACT.Ln, bias=1.0).then_inc(forget_ln, 1)
            attend(2)
            take(vB[:, 0, :], lambda o: o)
            attend(3)
            take(vB[:, 1, :], lambda o: o)
            attend(4)
            take(qB[:, 0, :], whole, SCALE)
            take(qB[:, 1, :], whole, SCALE)
            attend(5)
            take(qB[:, 2, :], whole, SCALE)
            take(qB[:, 3, :], whole, SCALE)
            attend(6)
            take(kB[:, 0, :], whole)
            attend(7)
            take(kB[:, 1, :], whole)
            for n in range(HEADS, 2 * HEADS + 2):
                attend(n)
            squares(5, mixT, pv_taken, 4, 8)
            std_of(5, 512, parts=2)
            squares(1, xT, mo_taken, 4, 8)
            std_of(1, D)
            act.wait_ge(mod_ready, 2)
            add_shift(1, 24)

            for i in range(4):
                b, half = divmod(i, 2)
                act.wait_ge(htr_done, i + 1)
                act.activation(tok[:, b, :].rearrange("t (j p) -> t j p", j=KT)[:, :, 64 * half:64 * half + 64],
                               ps[:, i, :].rearrange("t (p j) -> t j p", j=KT), ACT.Copy).then_inc(htr_taken_a, 1)
            act.wait_ge(gate_max, 1)
            for b in range(BLK):
                act.activation(g_pen[:, b, :], g8[:, b, 0:GROUPS], ACT.Exp, bias=w_top[:, 0, b:b + 1],
                               accum_out=g_sum[:, b:b + 1]).then_inc(gate_exp, 1)
            act.wait_ge(top_diff, 1)
            act.activation(e_diff, e_diff, ACT.Exp).then_inc(top_exp, 1)
            for j in range(0, KT, 2):
                act.wait_ge(gather_done, j + 1)
                act.activation(xsT[:, j, 0:PAIRS], ps[:, j % 4, :], ACT.Copy).then_inc(gather_taken_a, 1)
            act.wait_ge(lru_par, 2)
            act.activation(t8, t8, ACT.Exp).then_inc(lru_par_a, 1)
            act.activation(t4, t4, ACT.Exp).then_inc(lru_par_a, 1)
            act.wait_ge(lru_par_a, 2)
            act.activation(t4, t4, ACT.Ln, bias=1.0).then_inc(lru_par_a, 1)
            act.wait_ge(windows_ready, 2)
            too_many = act.value_load(flag_i[0:1, 0:1], min_val=0, max_val=1)

            def pair_act(n, u, y_sem, y_count):
                act.wait_ge(gu_done, n + 1)
                act.wait_ge(act_ready, n + 1)
                act.activation(act_g, ps[:, 0, 0:FE], ACT.Silu).then_inc(silu_done, 1)
                act.wait_ge(turn_done, n + 1)
                act.activation(turned[:, u, :], ps[:, 1, :], ACT.Copy).then_inc(turn_taken, 1)
                act.wait_ge(y_sem, y_count)
                act.activation(y_sb[:, 0:512], ps[:, 2, :], ACT.Copy).then_inc(y_taken_a, 1)

            act.sem_inc(y_taken_a, 1)
            with act.If(too_many < 1):
                with act.Fori(0, EXPERTS // SLOTS) as i:
                    for u in range(2):
                        pair_act(i * 2 + u, u, chunk_used, i * SLOTS + (USED0 + 2 * u + 2))
            with act.Else():
                with act.Fori(0, EXPERTS // 2 * WINDOWS) as i:
                    pair_act(i, 0, w_y_done, i + 1)
            squares(2, xT, comb_taken, 4, 8)
            std_of(2, D)
            squares(3, xT, scaled[2], 4, 8)
            std_of(3, D)

            unit2 = Count()

            def take2(dst, n=L):
                u = unit2.up() - 1
                act.wait_ge(u2_done, u + 1)
                act.activation(dst, ps[:, u % 4, 0:n], ACT.Copy).then_inc(u2_taken, 1)

            take2(raw_q[:, 2, :])
            take2(raw_q[:, 3, :])
            for h in range(HG):
                take2(f_[:, h, :])
            act.wait_ge(u2_taken, 6)
            act.activation(f_, f_, ACT.Sigmoid).then_inc(f_sig, 1)
            take2(raw_q[:, 0, :])
            take2(raw_q[:, 1, :])
            act.wait_ge(u2_taken, 8)
            act.activation(a_, raw_q, ACT.Sigmoid).then_inc(q_sig, 1)
            take2(v_[:, 0, :], 512)
            act.wait_ge(f_ready, 1)
            act.activation(f_, f_, ACT.Ln).then_inc(f_ln, 1)
            take2(v_[:, 1, :], 512)
            take2(lx[:, 0, 4:260])
            act.wait_ge(b_ready, HG)
            act.activation(eb, b_, ACT.Exp).then_inc(decay_ready, 1)
            act.activation(kd, b_, ACT.Exp, scale=-1.0).then_inc(decay_ready, 1)
            take2(lx[:, 1, 4:260])
            act.wait_ge(last_diff, 1)
            act.activation(ks, ks, ACT.Exp).then_inc(last_exp, 1)
            take2(lx[:, 2, 4:260])
            take2(lx[:, 3, 4:260])
            take2(lg[:, 0, :])
            take2(lg[:, 1, :])
            for b in range(BLK):
                act.wait_ge(kst_done, b + 1)
                act.activation(ksT[:, b, :], ps[:, 4 + b, :], ACT.Copy).then_inc(kst_taken, 1)
            take2(lg[:, 2, :])
            take2(lg[:, 3, :])
            for g in range(2):
                act.wait_ge(gates_done, g + 1)
                for j in range(4):
                    bias = parB[:, PB_ROWS["lru_bx" if g else "lru_ba"][0] + j:][:, 0:1]
                    act.activation((ig if g else r_)[:, j, :],
                                   ps[:, 4 + 2 * g + j // 2, (j % 2) * L:(j % 2 + 1) * L], ACT.Sigmoid,
                                   bias=bias).then_inc(gates_ready, 1)
            take2(g_[:, 0, :])
            take2(g_[:, 1, :])
            act.wait_ge(gates_ready, 8)
            act.wait_ge(lru_par, 3)
            for j in range(4):
                act.activation(th[:, j, :], r_[:, j, :], ACT.Tanh, scale=lru_c[:, j:j + 1]).then_inc(decays_ready, 1)
                act.activation(a_[:, j, :], r_[:, j, :], ACT.Exp, scale=lru_nc[:, j:j + 1]).then_inc(decays_ready, 1)
            take2(g_[:, 2, :])
            take2(g_[:, 3, :])
            act.wait_ge(half_power, 1)
            act.activation(th, th, ACT.Sqrt, scale=2.0).then_inc(power_root, 1)
            act.wait_ge(gelu_in, 1)
            act.activation(k_, k_, ACT.Sigmoid, scale=1.5957691216057308).then_inc(gelu_sig, 1)
            act.wait_ge(u2_taken, 22)
            act.activation(ks, g_, ACT.Sigmoid).then_inc(g_sig, 1)
            for i in range(2):
                act.wait_ge(o_done, i + 1)
                act.activation(o_[:, 2 * i:2 * i + 2, :], ps[:, 4 + i, :].rearrange("p (h t) -> p h t", h=2), ACT.Copy
                               ).then_inc(o_taken, 1)
            act.wait_ge(o_taken, 2)
            for i in range(2):
                act.activation(sq[:, 2 * i:2 * i + 2, :], o_[:, 2 * i:2 * i + 2, :], ACT.Square).then_inc(o_sq, 1)
            act.wait_ge(o_ssq, 2)
            act.activation(b_, ps[:, 6:8, :].rearrange("p a (h t) -> p (a h) t", h=2), ACT.Sqrt, scale=1.0 / P,
                           bias=EPS).then_inc(o_std, 1)
            squares(4, xT, mo_taken, KT + 4, KT + 8)
            std_of(4, D)

            for t in range(FT):
                act.wait_ge(ffn_done, t + 1)
                if t >= 2:
                    act.wait_ge(ffn_taken, t - 1)
                act.activation(silu_t[:, t % 2, :], ps[:, t % 4, 0:L], ACT.Silu).then_inc(ffn_silu, 1)
            squares(6, xT, down_taken, 2, 4)
            std_of(6, D, bank=4)
            for b in range(BLK):
                act.wait_ge(otr_done, 2 * b + 1)
                act.activation(tok[:, b, 0:512], ps[:, 2 * b, :], ACT.Copy).then_inc(otr_taken_a, 1)

        @block.vector
        def _(ve):
            step = Count()

            def own(k=1):
                ve.wait_ge(dve_step, step.up(k))

            def rstd_of(i, parts=1):
                ve.wait_ge(std_ready[i], 1)
                r = rstd[:].rearrange("p a t -> p (a t)")[:, 0:parts * L]
                ve.reciprocal(r, r).then_inc(dve_step, 1)
                own()

            def scale(i, dst, gain):
                for k in range(KT):
                    ve.scalar_tensor_tensor(dst[:, k, :], xT[:, k, :], gain[:, k:k + 1], rstd[:, 0, :],
                                            ALU.mult, ALU.mult).then_inc(scaled[i], 1)

            def par(tile, names, name, k=None):
                lo, hi = names[name]
                return tile[:, lo:hi] if k is None else tile[:, lo + k:lo + k + 1]

            ve.wait_ge(par_tr, 1)
            ve.tensor_copy(parA[:], ps[:, 2, 0:PA_N]).then_inc(par_taken, 1)
            ve.wait_ge(par_tr, 2)
            ve.tensor_copy(parB[:], ps[:, 3, 0:PB_N]).then_inc(par_taken, 1)
            ve.wait_ge(par_taken, 2)
            lb0, lb1, lru = par(parB, PB_ROWS, "lb0"), par(parB, PB_ROWS, "lb1"), par(parB, PB_ROWS, "lru_a")
            ve.tensor_tensor(m4, lb0, lb1, ALU.max).then_inc(dve_step, 1)
            ve.tensor_scalar(u4, lru, -1.0, 0.0, ALU.mult, ALU.max).then_inc(dve_step, 1)
            own(2)
            ve.tensor_tensor(t8[:, 0:4], lb0, m4, ALU.subtract).then_inc(dve_step, 1)
            ve.tensor_tensor(t8[:, 4:8], lb1, m4, ALU.subtract).then_inc(lru_par, 1)
            ve.scalar_tensor_tensor(t4, lru, -1.0, lru, ALU.mult, ALU.min).then_inc(lru_par, 1)
            own()
            ve.wait_ge(silu_c_ready, 1)
            for ch in range(ADA_FIRST):
                w, part = ada_arrived(ve, ch), ada_part(ch)
                ve.tensor_scalar(part, w[:, 0, :], silu_c[:, 0:1], None, ALU.mult).then_inc(dve_step, 1)
                for k in range(1, KT):
                    own()
                    ve.scalar_tensor_tensor(part, w[:, k, :], silu_c[:, k:k + 1], part, ALU.mult, ALU.add
                                            ).then_inc(ada_used if k == KT - 1 else dve_step, 1)
            rstd_of(0)
            m0 = ADA_FIRST * ADA_W // P
            b_lo = PA_ROWS["b_ada"][0]
            ve.wait_ge(par_taken, 2)
            ve.wait_ge(ada_done, ADA_FIRST)
            ve.tensor_tensor(mod[:, 0:m0], ps[:, 7, 0:m0], parA[:, b_lo:b_lo + m0], ALU.add).then_inc(mod_ready, 1)
            ve.wait_ge(mod_ready, 1)
            ve.scalar_tensor_tensor(gains[:, 0, :], mod[:, 8:16], 1.0, par(parA, PA_ROWS, "g_mix"), ALU.add,
                                    ALU.mult).then_inc(dve_step, 1)
            own()
            scale(0, hT, gains[:, 0, :])

            keys = (slice(0, P), slice(P, NK))
            for h in range(HEADS):
                ve.wait_ge(dots_taken, h + 1)
                if h:
                    ve.wait_ge(score_raw, 2 * h)
                for b in range(BLK):
                    if h == 0:
                        ve.tensor_scalar(score[:, keys[b]], relu[:, 0, keys[b]], iwT[:, b, 0:1], None, ALU.mult
                                         ).then_inc(score_raw, 1)
                    else:
                        ve.scalar_tensor_tensor(score[:, keys[b]], relu[:, h % 2, keys[b]], iwT[:, b, h:h + 1],
                                                score[:, keys[b]], ALU.mult, ALU.add).then_inc(score_raw, 1)
            ve.wait_ge(score_masked, 2)
            for r in range(TOPK // 8):
                src = score if r == 0 else left
                for b in range(BLK):
                    ve.max(top8[:, b, :], src[:, keys[b]]).then_inc(dve_step, 1)
                own(2)
                for b in range(BLK):
                    ve.match_replace(left[:, keys[b]], top8[:, b, :], src[:, keys[b]], TAKEN).then_inc(dve_step, 1)
                own(2)
            ve.tensor_scalar(sel_bias, left, -3.2e38, NEG, ALU.is_gt, ALU.mult).then_inc(sel_raw, 1)

            def logits(n):
                ve.wait_ge(logits_done, n + 1)
                bank = 2 + n % 2
                if n < HEADS:
                    slope = 2.0 ** (-8.0 * (n + 1) / HEADS)
                    ve.scalar_tensor_tensor(with_alibi, neg_dist, slope, ps[:, bank, 0:NK], ALU.mult, ALU.add
                                            ).then_inc(logits_taken, 1)
                    ve.wait_ge(sel_ready, 2)
                    ve.wait_ge(logits_taken, n + 1)
                    ve.tensor_tensor(logit[:, n % 2, :], with_alibi, sel_bias, ALU.add).then_inc(dve_step, 1)
                    own()
                else:
                    h = n - HEADS
                    ve.scalar_tensor_tensor(logit[:, n % 2, 0:P], ps[:, bank, 0:P], cum[:, 0, h:h + 1],
                                            causal[:, P:L], ALU.add, ALU.add).then_inc(dve_step, 1)
                    ve.scalar_tensor_tensor(logit[:, n % 2, P:NK], ps[:, bank, P:NK], cum[:, 1, h:h + 1],
                                            causal[:], ALU.add, ALU.add).then_inc(logits_taken, 1)
                    own()
                    ve.wait_ge(logits_taken, n + 1)
                for b in range(BLK):
                    ve.tensor_reduce(neg_max[:, n, b:b + 1], logit[:, n % 2, keys[b]], AX.X, ALU.max, negate=True
                                     ).then_inc(logits_ready, 1)

            def diagonals(m):
                ve.wait_ge(probs_ready, m + 1)
                ve.reciprocal(p_rsum[:, m, :], p_sum[:, m, :]).then_inc(dve_step, 1)
                own()
                if m >= 2:
                    ve.wait_ge(pt_done, m - 1)
                for b in range(BLK):
                    i = ve.tensor_scalar(diag[:, m % 2, b, :], ident[:], p_rsum[:, m, b:b + 1], None, ALU.mult)
                i.then_inc(diag_ready, 1)

            for n in range(2 * HEADS + 1):
                if n < 2 * HEADS:
                    logits(n)
                if n:
                    diagonals(n - 1)
                if n == 0:
                    ve.wait_ge(tile_taken, 13)
                    ve.scalar_tensor_tensor(forget[:, 1, :], forget[:, 0, :], -1.0, forget[:, 0, :], ALU.mult,
                                            ALU.min).then_inc(forget_abs, 1)
                if n == 2:
                    ve.wait_ge(forget_ln, 2)
                    ve.scalar_tensor_tensor(forget[:, 2, :], forget[:, 0, :], 0.0, forget[:, 1, :], ALU.min,
                                            ALU.subtract).then_inc(log_f_ready, 1)
                if n == 5:
                    ve.wait_ge(cum_done, 1)
                    ve.tensor_copy(cum, ps[:, 7, 64:80].rearrange("p (b h) -> p b h", b=BLK)).then_inc(cum_taken, 1)
                    ve.tensor_scalar(ncumT[0:HEADS, :], ps[0:HEADS, 7, 128:384], -1.0, None, ALU.mult
                                     ).then_inc(cum_taken, 1)
                    ve.wait_ge(cum_taken, 2)
            ve.wait_ge(ada_done, ADA_N)
            ve.tensor_tensor(mod[:, m0:48], ps[:, 7, m0:48], parA[:, b_lo + m0:b_lo + 48], ALU.add).then_inc(mod_ready, 1)
            ve.wait_ge(mod_ready, 2)
            ve.scalar_tensor_tensor(gains[:, 1, :], mod[:, 32:40], 1.0, par(parA, PA_ROWS, "g_ffn"), ALU.add,
                                    ALU.mult).then_inc(dve_step, 1)
            own()
            rstd_of(5, parts=2)
            for k in range(KT):
                ve.scalar_tensor_tensor(mixT[:, k, :], mixT[:, k, :], parB[:, k:k + 1], rstd[:, k // 4, :],
                                        ALU.mult, ALU.mult).then_inc(mix_ready, 1)
            for m in range(KT):
                ve.wait_ge(mo_done, m + 1)
                ve.scalar_tensor_tensor(xT[:, m, :], ps[:, m % 4, 0:L], mod[:, 16 + m:17 + m], xT[:, m, :], ALU.mult,
                                        ALU.add).then_inc(mo_taken, 1)

            rstd_of(1)
            scale(1, hT, gains[:, 1, :])
            nr = GROUPS + EXPERTS
            ve.memset(g8, -BIG).then_inc(dve_step, 1)
            own()
            ve.wait_ge(route_done, 1)
            logit_r = ps[:, 4, 0:BLK * nr].rearrange("p (b n) -> p b n", b=BLK)
            ve.tensor_copy(g8[:, :, 0:GROUPS], logit_r[:, :, 0:GROUPS]).then_inc(dve_step, 1)
            ve.tensor_copy(e_log, logit_r[:, :, GROUPS:nr]).then_inc(dve_step, 1)
            own(2)
            for b in range(BLK):
                ve.max(g_top[:, b, :], g8[:, b, :]).then_inc(dve_step, 1)
            own(2)
            ve.tensor_scalar(w_top[:, 0, :], g_top[:, :, 0], -1.0, None, ALU.mult).then_inc(gate_max, 1)
            for b in range(BLK):
                ve.max_index(idx_u[:, 0, b, :], g_top[:, b, :], g8[:, b, :]).then_inc(dve_step, 1)
            own(2)
            ve.tensor_copy(g_idx, idx_u[:, 0, :, 0]).then_inc(dve_step, 1)
            own()
            for b in range(BLK):
                ve.tensor_scalar(g_one[:, b, :], col_no[:, 0:GROUPS], g_idx[:, b:b + 1], None, ALU.is_equal
                                 ).then_inc(dve_step, 1)
            own(2)
            ve.wait_ge(gate_exp, 2)
            ve.tensor_scalar(g_pen, g_one, -1.0, BIG, ALU.add, ALU.mult).then_inc(dve_step, 1)
            one = g_one.rearrange("p b g -> p (b g)").unsqueeze(2).broadcast_to([P, BLK * GROUPS, PER_GROUP])
            pen = g_pen.rearrange("p b g -> p (b g)").unsqueeze(2).broadcast_to([P, BLK * GROUPS, PER_GROUP])
            e_3d = e_log.rearrange("p b (g e) -> p (b g) e", g=GROUPS)
            ve.tensor_tensor(e_3d, e_3d, one, ALU.mult).then_inc(dve_step, 1)
            own(2)
            ve.tensor_tensor(e_3d, e_3d, pen, ALU.add).then_inc(dve_step, 1)
            own()
            for b in range(BLK):
                ve.max(e_top[:, b, :], e_log[:, b, :]).then_inc(dve_step, 1)
            own(2)
            ve.tensor_tensor(e_diff, e_top[:, :, 1], e_top[:, :, 0], ALU.subtract).then_inc(top_diff, 1)
            for b in range(BLK):
                ve.max_index(idx_u[:, 1, b, :], e_top[:, b, :], e_log[:, b, :]).then_inc(dve_step, 1)
            own(2)
            ve.tensor_copy(e_idx, idx_u[:, 1, :, 0:2]).then_inc(dve_step, 1)
            own()
            for ch in range(2):
                for b in range(BLK):
                    ve.tensor_scalar(R_one[:, ch, b * EXPERTS:(b + 1) * EXPERTS], col_no[:, 0:EXPERTS],
                                     e_idx[:, b, ch:ch + 1], None, ALU.is_equal).then_inc(dve_step, 1)
            own(4)
            ve.tensor_tensor(R_chosen.rearrange("p b e -> p (b e)"), R_one[:, 0, :], R_one[:, 1, :], ALU.add
                             ).then_inc(choice_ready, 1)
            ve.wait_ge(rank_done, 1)
            ve.wait_ge(pad_ready, 5)
            ve.tensor_copy(rank[:, :, 0:EXPERTS], ps[:, 5, 0:64].rearrange("p (b e) -> p b e", b=BLK)
                           ).then_inc(dve_step, 1)
            ve.tensor_copy(counts, ps[:, 5, 64:96]).then_inc(dve_step, 1)
            own(2)
            ve.tensor_tensor_scan(upto, ones[:, 0:EXPERTS], counts, 0.0, ALU.mult, ALU.add).then_inc(dve_step, 1)
            own()
            ve.tensor_tensor(starts_f, upto, counts, ALU.subtract).then_inc(dve_step, 1)
            own()
            ve.tensor_tensor(place, ps[:, 5, 0:64].rearrange("p (b e) -> p b e", b=BLK),
                             starts_f.unsqueeze(1).broadcast_to([P, BLK, EXPERTS]), ALU.add).then_inc(dve_step, 1)
            own()
            prod = tmp_cols[:, 0:2 * BLK * EXPERTS].rearrange("p (c n) -> p c n", c=2)
            ve.tensor_tensor(prod, R_one, place.rearrange("p b e -> p (b e)").unsqueeze(1).broadcast_to(
                [P, 2, BLK * EXPERTS]), ALU.mult).then_inc(dve_step, 1)
            own()
            ve.tensor_reduce(cols.rearrange("p c b -> p (c b)"), prod.rearrange("p c (b e) -> p (c b) e", b=BLK),
                             AX.X, ALU.add).then_inc(dve_step, 1)
            own()
            for b in range(BLK):
                if b:
                    ve.wait_ge(pick_ready, b)
                ve.tensor_scalar(tmp_cols, col_no, cols[:, 1, b:b + 1], None, ALU.is_equal).then_inc(dve_step, 1)
                own()
                ve.scalar_tensor_tensor(pick[:, b, :], col_no, cols[:, 0, b:b + 1], tmp_cols, ALU.is_equal, ALU.add
                                        ).then_inc(pick_ready, 1)
            for w in range(WINDOWS):
                ve.tensor_scalar(wins_i[0:1, w, 0:EXPERTS], starts_f[0:1, :], float(w * WIN), float(PAIRS), ALU.add, ALU.min
                                 ).then_inc(dve_step, 1)
            ve.memset(wins_i[0:1, :, EXPERTS:], 0).then_inc(dve_step, 1)
            ve.tensor_reduce(most, counts, AX.X, ALU.max).then_inc(dve_step, 1)
            own(WINDOWS + 2)
            ve.tensor_scalar(flag_i[0:1, 0:1], most[0:1, :], float(WIN), None, ALU.is_gt).then_inc(windows_ready, 2)
            ve.wait_ge(top_exp, 1)
            ve.scalar_tensor_tensor(w_top[:, 0, :], e_diff, 1.0, g_sum, ALU.add, ALU.mult).then_inc(dve_step, 1)
            own()
            ve.reciprocal(w_top[:, 0, :], w_top[:, 0, :]).then_inc(dve_step, 1)
            own()
            ve.tensor_tensor(w_top[:, 1, :], w_top[:, 0, :], e_diff, ALU.mult).then_inc(dve_step, 1)
            own()
            ve.tensor_scalar(w_all[:, :, 0:EXPERTS], R_one[:, 0, :].rearrange("p (b e) -> p b e", b=BLK), 0.0, None,
                             ALU.mult).then_inc(dve_step, 1)
            own()
            for ch in range(2):
                for b in range(BLK):
                    ve.scalar_tensor_tensor(w_all[:, b, 0:EXPERTS], R_one[:, ch, b * EXPERTS:(b + 1) * EXPERTS],
                                            w_top[:, ch, b:b + 1], w_all[:, b, 0:EXPERTS], ALU.mult, ALU.add
                                            ).then_inc(dve_step, 1)
                own(2)
            for j in range(1, KT, 2):
                ve.wait_ge(gather_done, j + 1)
                ve.tensor_copy(xsT[:, j, 0:PAIRS], ps[:, j % 4, :]).then_inc(gather_taken_v, 1)

            def windows(n, u, starts, e, w):
                for h in range(2):
                    ve.tensor_copy(xw[:, u, :, h * WIN:(h + 1) * WIN], xsT[:, :, bass.ds(starts[h], WIN)])
                shape = [P, BLK, 2, WIN]
                rows = (col_no[:, 0:WIN] if w is None else col_no[:, bass.ds(w * WIN, WIN)])
                ve.tensor_tensor(put[:, u], rows.unsqueeze(1).unsqueeze(1).broadcast_to(shape),
                                 rank[:, :, bass.ds(e, 2)].unsqueeze(3).broadcast_to(shape), ALU.is_equal
                                 ).then_inc(rows_found, 1)
                ve.wait_ge(rows_found, n + 1)
                ve.tensor_tensor(put[:, u], put[:, u], w_all[:, :, bass.ds(e, 2)].unsqueeze(3).broadcast_to(shape),
                                 ALU.mult).then_inc(windows_copied, 1)

            def gated(n):
                ve.wait_ge(silu_done, n + 1)
                ve.tensor_tensor(act_e, act_g, ps[:, 0, FE:2 * FE], ALU.mult).then_inc(act_ready, 1)

            def result():
                ve.tensor_copy(y_sb[:, 512:1024], ps[:, 3, :]).then_inc(y_taken_v, 1)

            def load(lo, n):
                return nc.values_load_multi_w_load_instructions(
                    wins_i[:].rearrange("o w e -> o (w e)")[0:1, bass.ds(lo, n)], engines=(ENG.DVE,), min_val=0,
                    max_val=PAIRS)[1]

            ve.wait_ge(gather_taken_v, 4)
            ve.wait_ge(gather_taken_a, 4)
            too_many = ve.value_load(flag_i[0:1, 0:1], min_val=0, max_val=1)
            ve.sem_inc(y_taken_v, 1)
            ve.sem_inc(act_ready, 1)
            with ve.If(too_many < 1):
                windows(0, 0, load(0, 2), 0, None)
                with ve.Fori(0, EXPERTS // SLOTS) as i:
                    starts = load(i * SLOTS + 2, SLOTS)
                    for u in range(2):
                        gated(i * 2 + u)
                        windows(i * 2 + (u + 1), 1 - u, starts[2 * u:2 * u + 2], i * SLOTS + (2 * u + 2), None)
                        ve.wait_ge(chunk_used, i * SLOTS + (USED0 + 2 * u + 2))
                        result()
            with ve.Else():
                with ve.Fori(0, EXPERTS // 2) as i:
                    with ve.Fori(0, WINDOWS) as w:
                        n = i * WINDOWS + w
                        windows(n, 0, load(w * (EXPERTS + SLOTS) + i * 2, 2), i * 2, w)
                        gated(n)
                        ve.wait_ge(w_y_done, n + 1)
                        result()
            for j in range(KT):
                ve.wait_ge(comb_done, 1)
                ve.scalar_tensor_tensor(xT[:, j, :], ps[:, 4 + j // 2, (j % 2) * L:(j % 2 + 1) * L], mod[:, 40 + j:41 + j], xT[:, j, :], ALU.mult,
                                        ALU.add).then_inc(comb_taken, 1)
            rstd_of(2)
            scale(2, xT, par(parA, PA_ROWS, "g_final"))
            rstd_of(3)
            scale(3, hT, par(parB, PB_ROWS, "mix2"))

            ve.wait_ge(lru_par_a, 3)
            ve.tensor_tensor(m4, t8[:, 0:4], t8[:, 4:8], ALU.add).then_inc(dve_step, 1)
            ve.tensor_tensor(u4, u4, t4, ALU.add).then_inc(dve_step, 1)
            own(2)
            ve.reciprocal(m4, m4).then_inc(dve_step, 1)
            ve.tensor_scalar(lru_c, u4, LRU_C, None, ALU.mult).then_inc(dve_step, 1)
            ve.tensor_scalar(lru_nc, u4, -LRU_C, None, ALU.mult).then_inc(lru_par, 1)
            own(2)
            ve.tensor_tensor(lb, t8[:, 0:4], m4, ALU.mult).then_inc(dve_step, 1)
            own()
            ve.tensor_scalar(one_lb, lb, -1.0, 1.0, ALU.mult, ALU.add).then_inc(dve_step, 1)
            ve.memset(lx[:, :, 1:4], 0.0).then_inc(dve_step, 1)
            own(2)
            ve.wait_ge(f_sig, 1)
            for h in range(HG):
                ve.tensor_scalar(f_[:, h, :], f_[:, h, :], one_lb[:, h:h + 1], lb[:, h:h + 1], ALU.mult, ALU.add
                                 ).then_inc(dve_step, 1)
            own(HG)
            ve.tensor_scalar(k_, f_, -1.0, 1.0, ALU.mult, ALU.add).then_inc(f_ready, 1)
            ve.wait_ge(q_sig, 1)
            ve.tensor_tensor(raw_q, raw_q, a_, ALU.mult).then_inc(dve_step, 1)
            own()
            ve.wait_ge(f_ln, 1)
            for h in range(HG):
                ve.tensor_tensor_scan(b_[:, h, :], reset, f_[:, h, :], 0.0, ALU.mult, ALU.add).then_inc(b_ready, 1)
            ve.wait_ge(b_ready, HG)
            ve.wait_ge(f_ready, 1)
            flat = "p h (c j) -> p (h c) j"
            bc = b_.rearrange(flat, j=CHUNK)
            ve.tensor_tensor(ks.rearrange(flat, j=CHUNK),
                             bc[:, :, CHUNK - 1:CHUNK].broadcast_to([P, HG * CHUNKS, CHUNK]), bc, ALU.subtract
                             ).then_inc(last_diff, 1)
            ve.wait_ge(decay_ready, 1)
            ve.tensor_tensor(raw_q, raw_q, eb, ALU.mult).then_inc(qd_ready, 1)
            ve.wait_ge(decay_ready, 2)
            ve.tensor_tensor(kd, kd, k_, ALU.mult).then_inc(kd_ready, 1)
            ve.wait_ge(last_exp, 1)
            ve.tensor_tensor(ks, ks, k_, ALU.mult).then_inc(ks_ready, 1)
            ve.wait_ge(u2_taken, 14)
            cw, cb = PB_ROWS["conv_w"][0], PB_ROWS["conv_b"][0]
            for tap in range(CONV):
                for j in range(4):
                    w_tap = parB[:, cw + 4 * tap + j:cw + 4 * tap + j + 1]
                    if tap == 0:
                        ve.tensor_scalar(xc[:, j, :], lx[:, j, 1:1 + L], w_tap, parB[:, cb + j:cb + j + 1], ALU.mult,
                                         ALU.add).then_inc(dve_step, 1)
                    else:
                        ve.scalar_tensor_tensor(xc[:, j, :], lx[:, j, 1 + tap:1 + tap + L], w_tap, xc[:, j, :],
                                                ALU.mult, ALU.add
                                                ).then_inc(xc_ready if tap == CONV - 1 else dve_step, 1)
                if tap < CONV - 1:
                    own(4)
            for b in range(BLK):
                ve.wait_ge(hsc_done, b + 1)
                ve.scalar_tensor_tensor(sc_[:, b], ps[:, 6 + b, :].rearrange("p (h t) -> p h t", h=HG), BIG,
                                        in_chunk.unsqueeze(1).broadcast_to([P, HG, P]), ALU.min, ALU.mult
                                        ).then_inc(hsc_ready, 1)
            for ch in range(CHUNKS - 1):
                ve.wait_ge(kv_done, ch + 1)
                if ch == 0:
                    ve.tensor_copy(state(1), ps[:, 4, :]).then_inc(state_ready, 1)
                    continue
                ve.wait_ge(state_ready, ch)
                for h in range(HG):
                    n = slice(h * P, (h + 1) * P)
                    last = ch * CHUNK + CHUNK - 1
                    i = ve.scalar_tensor_tensor(state(ch + 1)[:, n], state(ch)[:, n], eb[:, h, last:last + 1],
                                                ps[:, 4 + ch % 4, n], ALU.mult, ALU.add)
                i.then_inc(state_ready, 1)
            ve.wait_ge(u2_taken, 18)
            ve.wait_ge(ks_ready, 1)
            ve.tensor_tensor(k_, lg, lg, ALU.mult).then_inc(dve_step, 1)
            own()
            ve.tensor_scalar(k_, k_, 0.044715, 1.0, ALU.mult, ALU.add).then_inc(dve_step, 1)
            own()
            ve.tensor_tensor(k_, k_, lg, ALU.mult).then_inc(gelu_in, 1)
            ve.wait_ge(decays_ready, 8)
            ve.tensor_scalar(r_, th, 1.0, None, ALU.add).then_inc(dve_step, 1)
            ve.tensor_tensor(ig, ig, xc, ALU.mult).then_inc(dve_step, 1)
            own(2)
            ve.reciprocal(r_, r_).then_inc(dve_step, 1)
            own()
            ve.tensor_tensor(th, th, r_, ALU.mult).then_inc(half_power, 1)
            ve.wait_ge(power_root, 1)
            ve.tensor_tensor(ig, ig, th, ALU.mult).then_inc(dve_step, 1)
            own()
            for j in range(4):
                ve.tensor_tensor_scan(xc[:, j, :], a_[:, j, :], ig[:, j, :], 0.0, ALU.mult, ALU.add
                                      ).then_inc(dve_step, 1)
            own(4)
            ve.wait_ge(gelu_sig, 1)
            ve.tensor_tensor(lg, lg, k_, ALU.mult).then_inc(dve_step, 1)
            own()
            ve.tensor_tensor(mixT[:, 4:8, :], xc, lg, ALU.mult).then_inc(mix2_ready, 4)
            ve.wait_ge(g_sig, 1)
            ve.scalar_tensor_tensor(g_, g_, par(parB, PB_ROWS, "hg_norm"), ks, ALU.mult, ALU.mult).then_inc(dve_step, 1)
            ve.wait_ge(o_std, 1)
            ve.reciprocal(b_, b_).then_inc(dve_step, 1)
            own(2)
            ve.tensor_tensor(o_, o_, b_, ALU.mult).then_inc(dve_step, 1)
            own()
            ve.tensor_tensor(mixT[:, 0:4, :], o_, g_, ALU.mult).then_inc(mix2_ready, 4)
            for m in range(KT):
                ve.wait_ge(mo_done, KT + m + 1)
                ve.tensor_tensor(xT[:, m, :], ps[:, m % 4, 0:L], xT[:, m, :], ALU.add).then_inc(mo_taken, 1)

            rstd_of(4)
            scale(4, hT, par(parB, PB_ROWS, "ffn2"))
            for t in range(FT):
                ve.wait_ge(ffn_silu, t + 1)
                ve.tensor_tensor(ffn[:, t, :], silu_t[:, t % 2, :], ps[:, t % 4, L:2 * L], ALU.mult
                                 ).then_inc(ffn_taken, 1)
            for i in range(4):
                ve.wait_ge(down_done, i + 1)
                ve.tensor_tensor(xT[:, 2 * i:2 * i + 2, :], ps[:, 4 + i, :].rearrange("p (k t) -> p k t", k=2),
                                 xT[:, 2 * i:2 * i + 2, :], ALU.add).then_inc(down_taken, 1)
            rstd_of(6)
            scale(5, hT, par(parB, PB_ROWS, "final2"))
            for b in range(BLK):
                ve.wait_ge(otr_done, 2 * b + 2)
                ve.tensor_copy(tok[:, b, 512:1024], ps[:, 2 * b + 1, :]).then_inc(otr_taken_v, 1)


_INS = ['x', 'c', 'w_ada', 'b_ada', 'g_mix', 'w_in', 'b_forget', 'g_out_a', 'g_out_b', 'w_out', 'g_ffn',
        'w_group', 'b_group', 'w_router', 'b_router', 'w_gate', 'w_up', 'w_down', 'g_final',
        'mix_norm_w_2', 'w_in_2', 'hg_lb_2', 'hg_norm_w_2', 'conv_w_2', 'conv_b_2', 'lru_wa_2', 'lru_ba_2',
        'lru_wx_2', 'lru_bx_2', 'lru_a_2', 'w_out_2', 'ffn_norm_w_2', 'w_gate_up_2', 'w_down_2',
        'final_norm_w_2']


def kernel(**inputs):
    import numpy as np
    import concourse.bacc as bacc
    from concourse.bass_utils import run_bass_kernel_spmd

    nc = bacc.Bacc("TRN2", target_bir_lowering=False, num_devices=1)
    arrays, args = {}, []
    for name in _INS:
        a = np.ascontiguousarray(inputs[name])
        arrays[f"in_{name}"] = a
        args.append(nc.dram_tensor(f"in_{name}", a.shape, mybir.dt.from_np(a.dtype), kind="ExternalInput").ap())
    args.append(nc.dram_tensor("out_y", (1, L, D), F32, kind="ExternalOutput").ap())
    build(nc, *args)
    r = run_bass_kernel_spmd(nc, [arrays], core_ids=[0])
    return r.results[0]["out_y"]
```

```python
from contextlib import ExitStack

import concourse.bass as bass
from concourse import mybir

F32 = mybir.dt.float32
I32 = mybir.dt.int32
U32 = mybir.dt.uint32
ALU = mybir.AluOpType
ACT = mybir.ActivationFunctionType
AX = mybir.AxisListType
ENG = mybir.EngineType

P = 128
L = 256
BLK = L // P
D = 1024
KT = D // P
EPS = 1e-6

HEADS = 8
HD = 64
SCALE = HD ** -0.5
TOPK = min(256, L // 4)
IN_COLS = 2896
AQ, AK, AV, IQ, IK, IW, BQ, BK, BV, BF = 0, 512, 640, 768, 1280, 1344, 1352, 1864, 2376, 2888
GROUPS, PER_GROUP = 4, 8
EXPERTS = GROUPS * PER_GROUP
FE = 256
PAIRS = 2 * L
WIN = 64
WINDOWS = L // WIN
COLS = PAIRS + WIN

HG = 4
CHUNK = 32
CHUNKS = L // CHUNK
CONV = 4
LRU_C = 8.0
D_FF = 2816
FT = D_FF // P

TAKEN = -3.4e38
NEG = -1.0e30
BIG = 3.0e38

SLOTS = 4
SLOT_F = KT * 776
ADA_W = 768
ADA_N = 6 * D // ADA_W
IN_CHUNKS = [(IQ, BQ), (AQ, IQ), (BK + 256, IN_COLS), (BQ, BK + 256)]
ADA_FIRST = 3
FFN_STEP = 3
FFN_N = -(-FT // FFN_STEP)
DOWN_STEP = 6
DOWN_N = -(-FT // DOWN_STEP)

ORDER = ([("ada", c, 1) for c in range(ADA_FIRST)]
         + [(kind, c + (ADA_FIRST if kind == "ada" else 0), 1) for c in range(4) for kind in ("in", "ada")]
         + [("ada", ADA_N - 1, 1)] + [("out", c, 1) for c in range(2)]
         + [("expert", e, 3) for e in range(EXPERTS)]
         + [("in2", 0, 1), ("in2", 1, 2), ("in2", 2, 1), ("in2", 3, 2)]
         + [("out2", c, 1) for c in range(2)] + [("ffn", c, 2) for c in range(FFN_N)]
         + [("down", c, 1) for c in range(DOWN_N)])
NUMBER = {(kind, c): n for n, (kind, c, _) in enumerate(ORDER)}
ARRIVED = []
_counts = [0] * SLOTS
for _n, (_, _, _dmas) in enumerate(ORDER):
    _counts[_n % SLOTS] += 16 * _dmas
    ARRIVED.append(_counts[_n % SLOTS])
EXPERT0 = NUMBER["expert", 0]
PE_USED = [sum(kind != "ada" for kind, _, _ in ORDER[:n + 1]) for n in range(len(ORDER))]
USED0 = PE_USED[EXPERT0] - 1
assert EXPERTS % SLOTS == 0

PA_ROWS = {}
PB_ROWS = {}
for _rows, _list in ((PA_ROWS, [("c", 8), ("b_ada", 48), ("g_mix", 8), ("g_ffn", 8), ("g_final", 8)]),
                     (PB_ROWS, [("g_out_a", 4), ("g_out_b", 4), ("mix2", 8), ("ffn2", 8), ("final2", 8),
                                ("lb0", 4), ("lb1", 4), ("hg_norm", 1), ("conv_w", 16), ("conv_b", 4),
                                ("lru_ba", 4), ("lru_bx", 4), ("lru_a", 4)])):
    _at = 0
    for _name, _k in _list:
        _rows[_name] = (_at, _at + _k)
        _at += _k
PA_N = 80
N_CONST, N_PAR_A, N_PAR, N_WR = 12, 5, 16, 5
PB_N = 73



class Count:

    def __init__(self):
        self.n = 0

    def up(self, k=1):
        self.n += k
        return self.n


def build(nc, x, c, w_ada, b_ada, g_mix, w_in, b_forget, g_out_a, g_out_b, w_out, g_ffn, w_group,
          b_group, w_router, b_router, w_gate, w_up, w_down, g_final, mix_norm_w_2, w_in_2, hg_lb_2,
          hg_norm_w_2, conv_w_2, conv_b_2, lru_wa_2, lru_ba_2, lru_wx_2, lru_bx_2, lru_a_2, w_out_2,
          ffn_norm_w_2, w_gate_up_2, w_down_2, final_norm_w_2, out):
    with ExitStack() as ctx:
        def sb(name, shape, dt=F32):
            return ctx.enter_context(nc.sbuf_tensor(name, shape, dt))

        def sem(name):
            return ctx.enter_context(nc.semaphore(name))

        ring = sb("ring", [P, SLOTS, SLOT_F])
        xT = sb("xT", [P, KT, L])
        hT = sb("hT", [P, KT, L])
        sq = sb("sq", [P, KT, L])
        mixT = sb("mixT", [P, KT, L])
        tok = sb("tok", [P, BLK, D])
        ident = sb("ident", [P, P])
        ones = sb("ones", [P, P])
        tri = sb("tri", [P, L])
        parA = sb("parA", [P, PA_N])
        parB = sb("parB", [P, PB_N])
        mod = sb("mod", [P, 48])
        gains = sb("gains", [P, 2, KT])
        silu_c = sb("silu_c", [P, KT])
        rstd = sb("rstd", [P, 2, L])
        small = sb("small", [P, 64])
        arena = sb("arena", [P, 15760])
        wins_i = sb("wins_i", [1, WINDOWS, EXPERTS + SLOTS], I32)
        flag_i = sb("flag_i", [1, 1], I32)
        idx_u = sb("idx_u", [P, 2, BLK, 8], U32)

        def cut(at, *shape):
            n = 1
            for s in shape:
                n *= s
            v = arena[:, at:at + n]
            if len(shape) == 2:
                v = v.rearrange("p (a b) -> p a b", b=shape[1])
            if len(shape) == 3:
                v = v.rearrange("p (a b c) -> p a b c", b=shape[1], c=shape[2])
            return v

        qA = cut(0, 4, L)
        qI = cut(1024, 4, L)
        qB = cut(2048, 4, L)
        kB = cut(3072, 4, L)
        kA = cut(4096, L)
        kI = cut(4352, L)
        kA_swap = cut(14240, L)
        vA = cut(4608, BLK, 128)
        vB = cut(4864, BLK, 512)
        NK = P + L
        score = cut(5888, NK)
        left = cut(6272, NK)
        relu = cut(6656, 2, NK)
        sel_bias = cut(7424, NK)
        with_alibi = cut(7808, NK)
        logit = cut(8192, 2, NK)
        prob = cut(8960, 2, NK)
        probT = cut(9728, 2, NK)
        diag = cut(10496, 2, BLK, P)
        causal = cut(11008, L)
        neg_dist = cut(11264, NK)
        head_row = cut(11648, HEADS, P)
        ncumT = cut(12672, L)
        iwT = cut(12928, BLK, 8)
        cum = cut(12944, BLK, 8)
        forget = cut(12960, 3, BLK * 8)
        att_small = cut(13008, 512)
        top8 = att_small[:, 0:16].rearrange("p (b k) -> p b k", b=BLK)
        neg_max = att_small[:, 16:48].rearrange("p (n b) -> p n b", b=BLK)
        p_sum = att_small[:, 48:80].rearrange("p (n b) -> p n b", b=BLK)
        p_rsum = att_small[:, 80:112].rearrange("p (n b) -> p n b", b=BLK)

        xsT = cut(0, KT, COLS)
        xw = cut(4608, 2 * KT, 2 * WIN).rearrange("p (u k) n -> p u k n", u=2)
        y_sb = cut(6656, D)
        act_g = cut(7680, FE)
        act_e = cut(7936, FE)
        put = cut(8192, 2 * BLK, 2, WIN).rearrange("p (u b) h r -> p u b h r", u=2)
        turned = cut(10240, 2, 512)
        rank = cut(11264, BLK, EXPERTS + 2)
        w_all = cut(11332, BLK, EXPERTS + 2)
        pick = cut(9216, BLK, PAIRS)
        col_no = cut(13600, PAIRS)
        strict = cut(14112, P)
        tmp_cols = cut(14240, PAIRS)
        route = cut(14752, 624)
        wr = sb("wr", [P, KT, GROUPS + EXPERTS])
        brow = sb("brow", [1, 8 + GROUPS + EXPERTS])

        n1k = HG * L
        raw_q = cut(0, HG, L)
        f_ = cut(1024, HG, L)
        k_ = cut(2048, HG, L)
        b_ = cut(3072, HG, L)
        eb = cut(4096, HG, L)
        kd = cut(5120, HG, L)
        ks = cut(6144, HG, L)
        v_ = cut(7168, BLK, 512)
        g_ = cut(8192, HG, L)
        lx = cut(9216, 4, 260)
        lg = cut(10256, 4, L)
        xc = cut(11280, 4, L)
        r_ = cut(12304, 4, L)
        ig = cut(13328, 4, L)
        a_ = cut(14352, 4, L)
        th = cut(9216, 4, L)
        reset = cut(15376, L)
        in_chunk = cut(15632, P)
        ksT = b_.rearrange("p h t -> p (h t)").rearrange("p (b n) -> p b n", b=BLK)
        sc_ = f_.rearrange("p h t -> p (h t)").rearrange("p (b h t) -> p b h t", b=BLK, h=HG)
        o_ = kd
        gate_w = mixT[:, 0:4, :].rearrange("p a b -> p (a b)").rearrange("p (g j n) -> p g j n", g=2, j=4)
        ffn = cut(0, FT, L)
        silu_t = cut(5632, 2, L)

        sqf = sq[:].rearrange("p k t -> p (k t)")
        tokf = tok[:].rearrange("p b d -> p (b d)")

        def o_sqs(i):
            return sqf[:, 1536:2048] if i == 0 else sqf[:, 0:512]

        def state(ch):
            return tokf[:, (ch - 1) * 512:ch * 512] if ch <= 4 else sqf[:, (ch - 5) * 512:(ch - 4) * 512]

        def piece(at, *shape):
            n = 1
            for v in shape:
                n *= v
            v = route[:, at:at + n]
            return v.rearrange("p (a b) -> p a b", b=shape[1]) if len(shape) == 2 else (
                v.rearrange("p (a b c) -> p a b c", b=shape[1], c=shape[2]) if len(shape) == 3 else v)

        g8 = piece(0, BLK, 8)
        g_top = piece(16, BLK, 8)
        e_log = piece(32, BLK, EXPERTS)
        e_top = piece(96, BLK, 8)
        R_one = piece(112, 2, BLK * EXPERTS)
        R_chosen = piece(240, BLK, EXPERTS)
        counts = piece(304, EXPERTS)
        upto = piece(336, EXPERTS)
        starts_f = piece(368, EXPERTS)
        place = piece(400, BLK, EXPERTS)
        g_one = piece(464, BLK, GROUPS)
        g_pen = piece(472, BLK, GROUPS)
        cols = piece(480, 2, BLK)
        e_idx = piece(484, BLK, 2)
        g_idx = piece(488, BLK)
        g_sum = piece(490, BLK)
        e_diff = piece(492, BLK)
        w_top = piece(494, 2, BLK)
        wins_f = piece(498, EXPERTS)
        most = piece(530, 1)
        lb = small[:, 0:4]
        one_lb = small[:, 4:8]
        lru_c = small[:, 8:12]
        lru_nc = small[:, 12:16]
        t4 = small[:, 16:20]
        u4 = small[:, 20:24]
        t8 = small[:, 24:32]
        m4 = small[:, 32:36]

        ps = ctx.enter_context(nc.psum_tensor("ps", [P, 8, 512], F32))

        arrived = [sem(f"arrived{i}") for i in range(SLOTS)]
        chunk_used = sem("chunk_used")
        ada_used_v, ada_used_g = sem("ada_used_v"), sem("ada_used_g")
        x_there, par_a_there, par_there, wr_there, lru_there = sem("x_there"), sem("par_a_there"), sem("par_there"), sem("wr_there"), sem("lru_there")
        consts_ready = sem("consts_ready")
        pool_step, dve_step, act_step = sem("pool_step"), sem("dve_step"), sem("act_step")
        par_tr, par_taken = sem("par_tr"), sem("par_taken")
        xT_tr, xT_ready = sem("xT_tr"), sem("xT_ready")
        silu_c_ready, ada_done, mod_ready = sem("silu_c_ready"), sem("ada_done"), sem("mod_ready")
        sq_ready = [sem(f"sq_ready{i}") for i in range(7)]
        ssq_ready = [sem(f"ssq_ready{i}") for i in range(7)]
        std_ready = [sem(f"std_ready{i}") for i in range(7)]
        scaled = [sem(f"scaled{i}") for i in range(6)]
        h_ready = [sem(f"h_ready{i}") for i in range(2)]
        tile_ready, tile_taken = sem("tile_ready"), sem("tile_taken")
        dots_ready, dots_taken = sem("dots_ready"), sem("dots_taken")
        score_raw, sel_ready = sem("score_raw"), sem("sel_ready")
        forget_abs, forget_ln, log_f_ready = sem("forget_abs"), sem("forget_ln"), sem("log_f_ready")
        cum_done, cum_taken = sem("cum_done"), sem("cum_taken")
        logits_done, logits_taken, logits_ready = sem("logits_done"), sem("logits_taken"), sem("logits_ready")
        probs_ready, diag_ready = sem("probs_ready"), sem("diag_ready")
        pt_done, pt_taken, pv_done, pv_taken = sem("pt_done"), sem("pt_taken"), sem("pv_done"), sem("pv_taken")
        mix_ready = sem("mix_ready")
        mo_done, mo_taken = sem("mo_done"), sem("mo_taken")
        route_done, gate_max, gate_exp = sem("route_done"), sem("gate_max"), sem("gate_exp")
        top_diff, top_exp = sem("top_diff"), sem("top_exp")
        htr_done, htr_taken_a = sem("htr_done"), sem("htr_taken_a")
        choice_ready, rank_done, pick_ready, windows_ready = sem("choice_ready"), sem("rank_done"), sem("pick_ready"), sem("windows_ready")
        gather_done, gather_taken_a, gather_taken_v = sem("gather_done"), sem("gather_taken_a"), sem("gather_taken_v")
        ki_moved, k_moved = sem("ki_moved"), sem("k_moved")
        pad_ready = sem("pad_ready")
        windows_copied, rows_found = sem("windows_copied"), sem("rows_found")
        gate_up_used = sem("gate_up_used")
        gu_done, silu_done, act_ready = sem("gu_done"), sem("silu_done"), sem("act_ready")
        turn_done, turn_taken, y_taken_a, y_taken_v = sem("turn_done"), sem("turn_taken"), sem("y_taken_a"), sem("y_taken_v")
        w_y_done, w_comb_done = sem("w_y_done"), sem("w_comb_done")
        comb_done, comb_taken = sem("comb_done"), sem("comb_taken")
        both_ssq, gate_scaled, up_scaled = sem("both_ssq"), sem("gate_scaled"), sem("up_scaled")
        u2_done, u2_taken = sem("u2_done"), sem("u2_taken")
        f_sig, f_ready, f_ln, b_ready = sem("f_sig"), sem("f_ready"), sem("f_ln"), sem("b_ready")
        decay_ready, last_diff, last_exp = sem("decay_ready"), sem("last_diff"), sem("last_exp")
        q_sig, kd_ready, ks_ready, qd_ready = sem("q_sig"), sem("kd_ready"), sem("ks_ready"), sem("qd_ready")
        kst_done, kst_taken, hsc_done, hsc_ready = sem("kst_done"), sem("kst_taken"), sem("hsc_done"), sem("hsc_ready")
        kv_done, o_done, o_taken, o_sq = sem("kv_done"), sem("o_done"), sem("o_taken"), sem("o_sq")
        o_ssq, g_sig = sem("o_ssq"), sem("g_sig")
        xc_ready, gates_done, gates_ready, decays_ready = sem("xc_ready"), sem("gates_done"), sem("gates_ready"), sem("decays_ready")
        o_std, half_power, power_root = sem("o_std"), sem("half_power"), sem("power_root")
        gelu_in, gelu_sig, lru_par = sem("gelu_in"), sem("gelu_sig"), sem("lru_par")
        lru_par_a = sem("lru_par_a")
        state_ready = sem("state_ready")
        mix2_ready = sem("mix2_ready")
        ffn_done, ffn_silu, ffn_taken = sem("ffn_done"), sem("ffn_silu"), sem("ffn_taken")
        down_done, down_taken = sem("down_done"), sem("down_taken")
        otr_done, otr_taken_a, otr_taken_v, stored = sem("otr_done"), sem("otr_taken_a"), sem("otr_taken_v"), sem("stored")

        block = ctx.enter_context(nc.Block())

        def ada_part(ch):
            if ch < ADA_FIRST:
                return cut(5888 + ch * ADA_W, ADA_W)
            if ch == ADA_N - 1:
                return cut(14500, ADA_W)
            part = tokf if ch < ADA_FIRST + 2 else sqf
            return part[:, (ch - ADA_FIRST) % 2 * ADA_W:][:, 0:ADA_W]

        def ada_wait(eng, ch):
            if ch < ADA_FIRST:
                eng.wait_ge(ada_used_v, ch + 1)
            else:
                eng.wait_ge(ada_used_g, ch - ADA_FIRST + 1)

        def ada_arrived(eng, ch):
            n = NUMBER["ada", ch]
            eng.wait_ge(arrived[n % SLOTS], ARRIVED[n])
            return weights("ada", ch, KT, ADA_W)

        def slot(n):
            return ring[:, n % SLOTS, :]

        def weights(kind, c, k, n):
            return slot(NUMBER[kind, c])[:, 0:k * n].rearrange("p (k n) -> p k n", n=n)

        def expert_weights(s):
            v = ring[:, s, :]
            return (v[:, 0:2 * KT * FE].rearrange("p (h k n) -> p h k n", h=2, k=KT),
                    v[:, 2 * KT * FE:3 * KT * FE].rearrange("p (k n) -> p k n", n=D))

        @block.sync
        def _(sp):
            def free(n):
                if n >= SLOTS:
                    kind, c, _ = ORDER[n - SLOTS]
                    if kind == "ada":
                        ada_wait(sp, c)
                    else:
                        sp.wait_ge(chunk_used, PE_USED[n - SLOTS])

            def load_ada(c):
                n = NUMBER["ada", c]
                free(n)
                sp.dma_start(weights("ada", c, KT, ADA_W),
                             w_ada[0].rearrange("(k p) n -> p k n", p=P)[:, :, c * ADA_W:(c + 1) * ADA_W]
                             ).then_inc(arrived[n % SLOTS], 16)

            sp.dma_start(tok[:], x[0].rearrange("(b p) d -> p b d", p=P)).then_inc(x_there, 16)
            sp.wait_ge(par_a_there, 16 * N_PAR_A)
            for ch in range(ADA_FIRST):
                load_ada(ch)
            assert ADA_N == ADA_FIRST + len(IN_CHUNKS) + 1
            for ch, (lo, hi) in enumerate(IN_CHUNKS):
                n = NUMBER["in", ch]
                free(n)
                sp.dma_start(weights("in", ch, KT, hi - lo),
                             w_in[0].rearrange("(k p) n -> p k n", p=P)[:, :, lo:hi]
                             ).then_inc(arrived[n % SLOTS], 16)
                load_ada(ADA_FIRST + ch)
            load_ada(ADA_N - 1)
            for ch in range(2):
                n = NUMBER["out", ch]
                free(n)
                sp.dma_start(weights("out", ch, KT, 512),
                             w_out[0].rearrange("(k p) n -> p k n", p=P)[:, :, ch * 512:ch * 512 + 512]
                             ).then_inc(arrived[n % SLOTS], 16)
            gate_d = w_gate[0].rearrange("e (p k) f -> p e (k f)", k=KT)
            up_d = w_up[0].rearrange("e (p k) f -> p e (k f)", k=KT)
            down_d = w_down[0].rearrange("e (k p) d -> p e k d", p=P)

            def load_gate_up(u, e):
                s = (EXPERT0 + u) % SLOTS
                gu_w, _ = expert_weights(s)
                for g, src in enumerate((gate_d, up_d)):
                    sp.dma_start(gu_w[:, g].rearrange("p k n -> p (k n)"), src[:, e, :].rearrange("p e f -> p (e f)")
                                 ).then_inc(arrived[s], 16)

            def load_down(u, e):
                s = (EXPERT0 + u) % SLOTS
                sp.dma_start(expert_weights(s)[1], down_d[:, e, :, :].rearrange("p e k d -> p (e k) d")
                             ).then_inc(arrived[s], 16)

            for u in range(SLOTS):
                free(EXPERT0 + u)
                load_gate_up(u, slice(u, u + 1))
                load_down(u, slice(u, u + 1))
            with sp.Fori(0, EXPERTS // SLOTS - 1) as i:
                for pair in range(2):
                    us = (2 * pair, 2 * pair + 1)
                    sp.wait_ge(gate_up_used, i * 2 + pair + 1)
                    for u in us:
                        load_gate_up(u, bass.ds(i * SLOTS + (SLOTS + u), 1))
                    sp.wait_ge(chunk_used, i * SLOTS + (USED0 + us[1] + 1))
                    for u in us:
                        load_down(u, bass.ds(i * SLOTS + (SLOTS + u), 1))
            in2 = w_in_2[0].rearrange("(k p) n -> p k n", p=P)
            for ch, parts in enumerate([[(256, 1024)], [(0, 256), (1024, 1536)], [(2048, 2816)],
                                        [(2816, 3072), (1536, 2048)]]):
                n = NUMBER["in2", ch]
                free(n)
                w, at = weights("in2", ch, KT, 768), 0
                for lo, hi in parts:
                    sp.dma_start(w[:, :, at:at + hi - lo], in2[:, :, lo:hi]).then_inc(arrived[n % SLOTS], 16)
                    at += hi - lo
            for ch in range(2):
                n = NUMBER["out2", ch]
                free(n)
                sp.dma_start(weights("out2", ch, KT, 512),
                             w_out_2[0].rearrange("(k p) n -> p k n", p=P)[:, :, ch * 512:ch * 512 + 512]
                             ).then_inc(arrived[n % SLOTS], 16)
            gu = w_gate_up_2[0].rearrange("(k p) n -> p k n", p=P)
            for ch in range(FFN_N):
                n = NUMBER["ffn", ch]
                free(n)
                k = min(FFN_STEP, FT - ch * FFN_STEP) * P
                w = weights("ffn", ch, KT, 2 * k)
                for half in range(2):
                    lo = half * D_FF + ch * FFN_STEP * P
                    sp.dma_start(w[:, :, half * k:(half + 1) * k], gu[:, :, lo:lo + k]
                                 ).then_inc(arrived[n % SLOTS], 16)
            for ch in range(DOWN_N):
                n = NUMBER["down", ch]
                free(n)
                k = min(DOWN_STEP, FT - ch * DOWN_STEP)
                sp.dma_start(weights("down", ch, k, D),
                             w_down_2[0, ch * DOWN_STEP * P:(ch * DOWN_STEP + k) * P].rearrange(
                                 "(k p) n -> p k n", p=P)).then_inc(arrived[n % SLOTS], 16)
            for b in range(BLK):
                sp.wait_ge(otr_taken_a, b + 1)
                sp.wait_ge(otr_taken_v, b + 1)
                sp.dma_start(out[0, b * P:(b + 1) * P, :], tok[:, b, :]).then_inc(stored, 16)
            sp.wait_ge(stored, 16 * BLK)

        @block.gpsimd
        def _(pool):
            step = Count()
            pool.memset(ident[:], 0.0).then_inc(pool_step, 1)
            pool.memset(ones[:], 1.0).then_inc(consts_ready, 1)
            pool.memset(tri[:], 1.0).then_inc(pool_step, 1)
            pool.memset(causal[:], 0.0).then_inc(pool_step, 1)
            pool.memset(head_row[:], 1.0).then_inc(pool_step, 1)
            pool.memset(strict[:], 1.0).then_inc(pool_step, 1)
            pool.memset(reset[:], 1.0).then_inc(pool_step, 1)
            pool.memset(ncumT[:], 0.0).then_inc(consts_ready, 1)
            pool.memset(in_chunk[:], 1.0).then_inc(pool_step, 1)
            pool.wait_ge(pool_step, step.up(7))
            pool.affine_select(out=ident[:], in_=ident[:], compare_op=ALU.not_equal, fill=1.0, base=0,
                               pattern=[[-1, P]], channel_multiplier=1).then_inc(consts_ready, 1)
            pool.affine_select(out=tri[:], in_=tri[:], compare_op=ALU.is_ge, fill=0.0, base=0,
                               pattern=[[1, L]], channel_multiplier=-1).then_inc(consts_ready, 1)
            pool.affine_select(out=causal[:, P:L], in_=causal[:, P:L], compare_op=ALU.is_ge, fill=NEG, base=0,
                               pattern=[[-1, P]], channel_multiplier=1).then_inc(consts_ready, 1)
            pool.affine_select(out=head_row[:], in_=head_row[:], compare_op=ALU.is_equal, fill=0.0,
                               base=0, pattern=[[1, HEADS], [0, P]], channel_multiplier=-1
                               ).then_inc(consts_ready, 1)
            pool.affine_select(out=strict[:], in_=strict[:], compare_op=ALU.is_gt, fill=0.0, base=0,
                               pattern=[[1, P]], channel_multiplier=-1).then_inc(consts_ready, 1)
            pool.affine_select(out=in_chunk[:], in_=in_chunk[:], compare_op=ALU.is_ge, fill=0.0, base=0,
                               pattern=[[1, P]], channel_multiplier=-1).then_inc(pool_step, 1)
            pool.wait_ge(pool_step, step.up())
            pool.affine_select(out=in_chunk[:], in_=in_chunk[:], compare_op=ALU.is_ge, fill=0.0, base=0,
                               pattern=[[-CHUNK, P // CHUNK], [0, CHUNK]], channel_multiplier=1
                               ).then_inc(consts_ready, 1)
            pool.memset(reset[:, 0:L:CHUNK], 0.0).then_inc(consts_ready, 1)
            pool.iota(neg_dist[:, 0:P], [[1, P]], base=0, channel_multiplier=-1,
                      allow_small_or_imprecise_dtypes=True).then_inc(consts_ready, 1)
            pool.iota(neg_dist[:, P:NK], [[1, L]], base=-P, channel_multiplier=-1,
                      allow_small_or_imprecise_dtypes=True).then_inc(consts_ready, 1)
            pool.iota(col_no[:], [[1, PAIRS]], base=0, channel_multiplier=0,
                      allow_small_or_imprecise_dtypes=True).then_inc(consts_ready, 1)

            def ada_sum(ch):
                w = ada_arrived(pool, ch)
                pool.tensor_tensor(w, w, silu_c[:].unsqueeze(2).broadcast_to([P, KT, ADA_W]), ALU.mult
                                   ).then_inc(pool_step, 1)
                for half in (4, 2):
                    pool.wait_ge(pool_step, step.up())
                    pool.tensor_tensor(w[:, 0:half, :], w[:, 0:half, :], w[:, half:2 * half, :], ALU.add
                                       ).then_inc(pool_step, 1)
                pool.wait_ge(pool_step, step.up())
                if ch == ADA_FIRST + 2:
                    pool.wait_ge(ssq_ready[0], 1)
                pool.tensor_tensor(ada_part(ch), w[:, 0, :], w[:, 1, :], ALU.add).then_inc(ada_used_g, 1)

            pool.wait_ge(xT_tr, 4)
            pool.wait_ge(silu_c_ready, 1)
            for ch in range(ADA_FIRST, ADA_N):
                ada_sum(ch)
            pool.wait_ge(mo_taken, KT)
            pool.memset(xsT[:, :, PAIRS:COLS], 0.0).then_inc(pad_ready, 1)
            pool.memset(y_sb, 0.0).then_inc(pad_ready, 1)
            pool.memset(turned[:, 1, :], 0.0).then_inc(pad_ready, 1)
            pool.memset(rank, 0.0).then_inc(pad_ready, 1)
            pool.memset(w_all, 0.0).then_inc(pad_ready, 1)
            pool.memset(gate_w[:], 0.0).then_inc(pool_step, 1)
            pool.wait_ge(pool_step, step.up())
            for g, w in enumerate((lru_wa_2, lru_wx_2)):
                for odd in range(2):
                    q = slice(64 * odd, 64 * odd + 64)
                    pool.dma_start(gate_w[q, g, :, q], w[0].rearrange("(j o) d e -> o d j e", o=2)[odd]
                                   ).then_inc(lru_there, 16)

        @block.tensor
        def _(pe):
            def chunk_there(kind, c):
                n = NUMBER[kind, c]
                pe.wait_ge(arrived[n % SLOTS], ARRIVED[n])

            def sum_squares(i, bank, col=0, tiles=range(KT), n=L):
                for k in tiles:
                    last = pe.matmul(ps[:, bank, col:col + n], lhsT=ones[:], rhs=sq[:, k, :],
                                     start=k == tiles[0], stop=k == tiles[-1])
                last.then_inc(ssq_ready[i], 1)

            def product(o, w_of, rhs_of, k_n=KT):
                for k in range(k_n):
                    last = pe.matmul(o, lhsT=w_of(k), rhs=rhs_of(k), start=k == 0, stop=k == k_n - 1)
                return last

            pe.wait_ge(consts_ready, N_CONST)
            pe.wait_ge(par_a_there, 16 * N_PAR_A)
            pe.transpose(ps[:, 2, 0:PA_N], hT[0:PA_N, 0, 0:P], ident[0:PA_N, 0:PA_N]).then_inc(par_tr, 1)
            pe.wait_ge(x_there, 16)
            for q, bank in enumerate((0, 1, 4, 5)):
                for k in (2 * q, 2 * q + 1):
                    for b in range(BLK):
                        at = (k % 2) * L + b * P
                        last = pe.transpose(ps[:, bank, at:at + P], tok[:, b, k * P:(k + 1) * P], ident[:])
                last.then_inc(xT_tr, 1)

            def ada(ch):
                ada_wait(pe, ch)
                for i in range(ADA_W // P):
                    m = ch * (ADA_W // P) + i
                    last = pe.matmul(ps[:, 7, m:m + 1], lhsT=ada_part(ch)[:, i * P:(i + 1) * P], rhs=ones[:, 0:1],
                                     start=True, stop=True)
                last.then_inc(ada_done, 1)

            pe.wait_ge(sq_ready[0], 2)
            sum_squares(0, 6)
            ada(0)
            ada(1)
            pe.wait_ge(par_there, 16 * N_PAR)
            pe.transpose(ps[:, 3, 0:PB_N], hT[0:PB_N, 1, 0:P], ident[0:PB_N, 0:PB_N]).then_inc(par_tr, 1)
            ada(2)

            unit = Count()

            def bank_of_unit():
                u = unit.up() - 1
                if u >= 2:
                    pe.wait_ge(tile_taken, u - 1)
                return ps[:, u % 2, :]

            def features(ch, cols):
                w = weights("in", ch, KT, IN_CHUNKS[ch][1] - IN_CHUNKS[ch][0])
                o = bank_of_unit()
                return product(o[:, 0:L], lambda k: cols(w[:, k, :]), lambda k: hT[:, k, :])

            def tokens(ch, lo, hi, blocks, bias=None):
                w = weights("in", ch, KT, IN_CHUNKS[ch][1] - IN_CHUNKS[ch][0])
                o, n = bank_of_unit(), hi - lo
                for i, b in enumerate(blocks):
                    for k in range(KT):
                        last = pe.matmul(o[:, i * n:(i + 1) * n], lhsT=hT[:, k, b * P:(b + 1) * P],
                                         rhs=w[:, k, lo:hi], start=k == 0, stop=k == KT - 1 and bias is None)
                    if bias is not None:
                        last = pe.matmul(o[:, i * n:(i + 1) * n], lhsT=ones[0:1, :], rhs=bias,
                                         start=False, stop=True)
                return last

            pe.wait_ge(h_ready[0], KT)
            chunk_there("in", 0)
            tokens(0, IW - IQ, BQ - IQ, (0, 1)).then_inc(tile_ready, 1)
            ik = IK - IQ
            w = weights("in", 0, KT, BQ - IQ)
            product(bank_of_unit()[0:64, 0:L], lambda k: w[:, k, ik:ik + 64], lambda k: hT[:, k, :]
                    ).then_inc(tile_ready, 1)
            for j in range(4):
                last = features(0, lambda w: w[:, j * P:(j + 1) * P]).then_inc(tile_ready, 1)
            pe.wait_ge(tile_taken, 6)
            pe.sem_inc(chunk_used, 1)

            def dots(h):
                bank, q = 2 + h % 2, slice(64 * (h % 2), 64 * (h % 2) + 64)
                if h >= 2:
                    pe.wait_ge(dots_taken, h - 1)
                pe.matmul(ps[:, bank, 0:P], lhsT=qI[q, h // 2, 0:P], rhs=kI[q, 0:P], start=True, stop=True)
                pe.matmul(ps[:, bank, P:NK], lhsT=qI[q, h // 2, P:L], rhs=kI[q, :],
                          start=True, stop=True).then_inc(dots_ready, 1)

            pe.wait_ge(par_taken, 2)
            pe.wait_ge(ki_moved, 16)
            chunk_there("in", 1)
            dots(0)
            dots(1)
            features(1, lambda w: w[:, AK:AV]).then_inc(tile_ready, 1)
            dots(2)
            dots(3)
            tokens(1, AV, IQ, (0, 1)).then_inc(tile_ready, 1)
            for j in range(4):
                if j < 2:
                    dots(4 + 2 * j)
                    dots(5 + 2 * j)
                features(1, lambda w: w[:, j * P:(j + 1) * P]).then_inc(tile_ready, 1)
            pe.wait_ge(tile_ready, 12)
            pe.sem_inc(chunk_used, 1)

            def head(n):
                if n < HEADS:
                    kv, half = n // 4, n % 2
                    q = slice(64 * half, 64 * half + 64)
                    return q, qA[q, n // 2, :], (kA if kv == half else kA_swap)[q, :], vA[:, :, 64 * kv:64 * kv + 64]
                h = n - HEADS
                q = slice(64 * (h % 2), 64 * (h % 2) + 64)
                return q, qB[q, h // 2, :], kB[q, h // 2, :], vB[:, :, h * 64:(h + 1) * 64]

            def attend(n):
                if n < 2 * HEADS:
                    _, q, k, _ = head(n)
                    bank, more = 2 + n % 2, n >= HEADS
                    if n >= 2:
                        pe.wait_ge(logits_taken, n - 1)
                    else:
                        pe.wait_ge(dots_taken, HEADS)
                    for o, qb, keys in ((ps[:, bank, 0:P], 0, slice(0, P)), (ps[:, bank, P:NK], 1, slice(0, L))):
                        last = pe.matmul(o, lhsT=q[:, qb * P:(qb + 1) * P], rhs=k[:, keys], start=True,
                                         stop=not more)
                        if more:
                            last = pe.matmul(o, lhsT=head_row[:, n - HEADS, :], rhs=ncumT[:, keys],
                                             start=False, stop=True)
                    last.then_inc(logits_done, 1)
                if 2 <= n <= 2 * HEADS + 1:
                    m = n - 2
                    bank = 4 + m % 2
                    pe.wait_ge(diag_ready, m + 1)
                    if m >= 2:
                        pe.wait_ge(pt_taken, m - 1)
                    for s in range(3):
                        last = pe.matmul(ps[:, bank, s * P:(s + 1) * P], lhsT=prob[:, m % 2, s * P:(s + 1) * P],
                                         rhs=diag[:, m % 2, min(s, 1), :], start=True, stop=True)
                    last.then_inc(pt_done, 1)
                if 3 <= n:
                    m = n - 3
                    q, _, _, v = head(m)
                    pe.wait_ge(pt_taken, m + 1)
                    if m % 2 == 0 and m:
                        pe.wait_ge(pv_taken, m // 2)
                    pe.matmul(ps[q, 6, 0:L], lhsT=v[:, 0, :], rhs=probT[:, m % 2, 0:L], start=True, stop=False)
                    pe.matmul(ps[q, 6, P:L], lhsT=v[:, 1, :], rhs=probT[:, m % 2, L:NK], start=False,
                              stop=True).then_inc(pv_done, 1)

            def bq(j):
                features(3, lambda w: w[:, j * P:(j + 1) * P]).then_inc(tile_ready, 1)

            chunk_there("in", 2)
            tokens(2, BF - BK - 256, BF - BK - 256 + 8, (0, 1), bias=brow[0:1, 0:8]).then_inc(tile_ready, 1)
            features(2, lambda w: w[:, 0:P]).then_inc(tile_ready, 1)
            features(2, lambda w: w[:, P:2 * P]).then_inc(tile_ready, 1)
            tokens(2, BV - BK - 256, BF - BK - 256, (0,)).then_inc(tile_ready, 1)
            tokens(2, BV - BK - 256, BF - BK - 256, (1,)).then_inc(tile_ready, 1)
            pe.wait_ge(tile_ready, 17)
            pe.sem_inc(chunk_used, 1)
            pe.wait_ge(k_moved, 32)
            chunk_there("in", 3)
            for n in range(6):
                attend(n)
                bq(n)
            pe.wait_ge(log_f_ready, 1)
            pe.wait_ge(mod_ready, 1)
            lf = forget[:, 2, :].rearrange("p (b h) -> p b h", b=BLK)
            pe.matmul(ps[:, 7, 64:72], lhsT=tri[:, 0:P], rhs=lf[:, 0, :], start=True, stop=True)
            pe.matmul(ps[:, 7, 72:80], lhsT=ones[:], rhs=lf[:, 0, :], start=True, stop=False)
            pe.matmul(ps[:, 7, 72:80], lhsT=tri[:, 0:P], rhs=lf[:, 1, :], start=False, stop=True)
            pe.matmul(ps[0:HEADS, 7, 128:384], lhsT=lf[:, 0, :], rhs=tri[:], start=True, stop=False)
            pe.matmul(ps[0:HEADS, 7, 256:384], lhsT=lf[:, 1, :], rhs=tri[:, 0:P], start=False,
                      stop=True).then_inc(cum_done, 1)
            pe.wait_ge(tile_taken, 23)
            pe.sem_inc(chunk_used, 1)
            attend(6)
            attend(7)
            pe.wait_ge(cum_taken, 2)
            for n in range(HEADS, 2 * HEADS + 3):
                attend(n)
                if n < HEADS + ADA_N - ADA_FIRST:
                    ada(ADA_FIRST + n - HEADS)
                if n == HEADS + 6:
                    pe.wait_ge(sq_ready[5], 1)
                    pe.wait_ge(tile_taken, 23)
                    sum_squares(5, 0, 0, range(4))

            def out_part(kind, ch, half, tiles, last_of=None):
                w = weights(kind, ch, KT, 512)
                for m in tiles:
                    o = ps[:, m // 2, (m % 2) * L:(m % 2 + 1) * L]
                    for k in range(4 * half, 4 * half + 4):
                        last = pe.matmul(o, lhsT=w[:, k, (m % 4) * P:(m % 4 + 1) * P], rhs=mixT[:, k, :],
                                         start=last_of is None and m % 2 == 0 and k % 4 == 0,
                                         stop=last_of is not None and k % 4 == 3, skip_group_check=True)
                    if last_of is not None:
                        last.then_inc(mo_done, 1)
                        if m == tiles[-1]:
                            pe.wait_ge(mo_done, last_of)
                            pe.sem_inc(chunk_used, 1)

            pe.wait_ge(mix_ready, 4)
            pe.wait_ge(logits_taken, 2 * HEADS)
            chunk_there("out", 0)
            out_part("out", 0, 0, range(4))
            pe.wait_ge(sq_ready[5], 2)
            sum_squares(5, 6, L, range(4, 8))
            chunk_there("out", 1)
            out_part("out", 1, 0, range(4, 8))
            pe.wait_ge(mix_ready, KT)
            out_part("out", 0, 1, range(4), 4)
            out_part("out", 1, 1, range(4, 8), 8)

            pe.wait_ge(sq_ready[1], 2)
            sum_squares(1, 6)
            pe.wait_ge(wr_there, 16 * N_WR)
            pe.wait_ge(h_ready[1], KT)
            nr = GROUPS + EXPERTS
            for b in range(BLK):
                for k in range(KT):
                    pe.matmul(ps[:, 4, b * nr:(b + 1) * nr], lhsT=hT[:, k, b * P:(b + 1) * P], rhs=wr[:, k, :],
                              start=k == 0, stop=False)
                last = pe.matmul(ps[:, 4, b * nr:(b + 1) * nr], lhsT=ones[0:1, :], rhs=brow[0:1, 8:8 + nr],
                                 start=False, stop=True)
            last.then_inc(route_done, 1)
            pe.wait_ge(mo_taken, KT)
            for i in range(4):
                b, half = divmod(i, 2)
                for k in range(4):
                    last = pe.transpose(ps[:, i, k * P:(k + 1) * P], hT[:, 4 * half + k, b * P:(b + 1) * P], ident[:])
                last.then_inc(htr_done, 1)
            pe.wait_ge(choice_ready, 1)
            pe.matmul(ps[:, 5, 0:32], lhsT=strict[:], rhs=R_chosen[:, 0, :], start=True, stop=True)
            pe.matmul(ps[:, 5, 32:64], lhsT=ones[:], rhs=R_chosen[:, 0, :], start=True, stop=False)
            pe.matmul(ps[:, 5, 32:64], lhsT=strict[:], rhs=R_chosen[:, 1, :], start=False, stop=True)
            pe.matmul(ps[:, 5, 64:96], lhsT=ones[:], rhs=R_chosen[:, 0, :], start=True, stop=False)
            pe.matmul(ps[:, 5, 64:96], lhsT=ones[:], rhs=R_chosen[:, 1, :], start=False,
                      stop=True).then_inc(rank_done, 1)
            pe.wait_ge(pick_ready, BLK)
            pe.wait_ge(htr_taken_a, 4)
            for j in range(KT):
                if j >= 4:
                    if j % 2 == 0:
                        pe.wait_ge(gather_taken_a, (j - 4) // 2 + 1)
                    else:
                        pe.wait_ge(gather_taken_v, (j - 4) // 2 + 1)
                for b in range(BLK):
                    last = pe.matmul(ps[:, j % 4, :], lhsT=tok[:, b, j * P:(j + 1) * P], rhs=pick[:, b, :],
                                     start=b == 0, stop=b == BLK - 1)
                last.then_inc(gather_done, 1)

            def gate_up(e0, u):
                for h in range(2):
                    gu_w, _ = expert_weights((e0 + h) % SLOTS)
                    for k in range(KT):
                        last = pe.matmul(ps[WIN * h:WIN * (h + 1), 0, :].rearrange("p (g n) -> p g n", g=2),
                                         lhsT=xw[:, u, k, WIN * h:WIN * (h + 1)], rhs=gu_w[:, :, k, :],
                                         start=k == 0, stop=k == KT - 1)
                return last

            def turn(u):
                for b in range(BLK):
                    pe.transpose(ps[:, 1, FE + b * P:FE + (b + 1) * P], put[:, u, b].rearrange("p h r -> p (h r)"),
                                 ident[:])
                for f in range(2):
                    last = pe.transpose(ps[:, 1, f * P:(f + 1) * P], act_e[:, f * P:(f + 1) * P], ident[:])
                return last

            def down(e0, u):
                for h in range(2):
                    _, dn = expert_weights((e0 + h) % SLOTS)
                    for half in range(2):
                        for k in range(2):
                            at = k * P + WIN * h
                            last = pe.matmul(ps[WIN * h:WIN * (h + 1), 2 + half, :], lhsT=turned[:, u, at:at + WIN],
                                             rhs=dn[:, k, half * 512:(half + 1) * 512], start=k == 0, stop=k == 1)
                return last

            def combine(u, tiles):
                for j in tiles:
                    last = pe.matmul(ps[:, 4 + j // 2, (j % 2) * L:(j % 2 + 1) * L], lhsT=y_sb[:, j * P:(j + 1) * P],
                                     rhs=turned[:, u, FE:FE + L], start=False, stop=False, skip_group_check=True)
                return last

            pe.wait_ge(gather_taken_a, 4)
            pe.wait_ge(gather_taken_v, 4)
            pe.wait_ge(pad_ready, 5)
            pe.wait_ge(windows_ready, 2)
            for j in range(4):
                pe.matmul(ps[:, 4 + j, :], lhsT=ones[:], rhs=turned[:, 1, :], start=True, stop=False,
                          skip_group_check=True)
            too_many = pe.value_load(flag_i[0:1, 0:1], min_val=0, max_val=1)
            with pe.If(too_many < 1):
                with pe.Fori(0, EXPERTS // SLOTS) as i:
                    for u in range(2):
                        e0, n = EXPERT0 + 2 * u, i * 2 + u
                        pe.wait_ge(windows_copied, n + 1)
                        for h in range(2):
                            s = (e0 + h) % SLOTS
                            pe.wait_ge(arrived[s], i * 48 + ARRIVED[e0 + h])
                        gate_up(e0, u).then_inc(gu_done, 1)
                        pe.wait_ge(y_taken_a, n + 1)
                        pe.wait_ge(y_taken_v, n + 1)
                        combine(1 - u, range(0, 5))
                        pe.wait_ge(act_ready, n + 2)
                        turn(u).then_inc(turn_done, 1)
                        combine(1 - u, range(5, KT))
                        pe.wait_ge(turn_taken, n + 1)
                        down(e0, u).then_inc(chunk_used, 2)
                pe.wait_ge(y_taken_a, EXPERTS // 2 + 1)
                pe.wait_ge(y_taken_v, EXPERTS // 2 + 1)
                combine(1, range(KT)).then_inc(comb_done, 1)
            with pe.Else():
                with pe.Fori(0, EXPERTS // SLOTS) as i:
                    for u in range(2):
                        e0 = EXPERT0 + 2 * u
                        with pe.Fori(0, WINDOWS) as w:
                            n = i * (2 * WINDOWS) + w + u * WINDOWS
                            for h in range(2):
                                s = (e0 + h) % SLOTS
                                pe.wait_ge(arrived[s], i * 48 + ARRIVED[e0 + h])
                            pe.wait_ge(windows_copied, n + 1)
                            gate_up(e0, 0).then_inc(gu_done, 1)
                            pe.wait_ge(act_ready, n + 2)
                            turn(0).then_inc(turn_done, 1)
                            pe.wait_ge(turn_taken, n + 1)
                            down(e0, 0).then_inc(w_y_done, 1)
                            pe.wait_ge(y_taken_a, n + 2)
                            pe.wait_ge(y_taken_v, n + 2)
                            combine(0, range(KT)).then_inc(w_comb_done, 1)
                        pe.wait_ge(w_comb_done, i * (2 * WINDOWS) + (u + 1) * WINDOWS)
                        pe.sem_inc(gate_up_used, 1)
                        pe.sem_inc(chunk_used, 2)
                pe.wait_ge(w_comb_done, EXPERTS // 2 * WINDOWS)
                pe.sem_inc(comb_done, 1)

            pe.wait_ge(sq_ready[2], 2)
            sum_squares(2, 6)
            pe.wait_ge(sq_ready[3], KT)
            product(ps[:, 5, 0:L], lambda k: ones[:], lambda k: hT[:, k, :]).then_inc(ssq_ready[3], 1)
            unit2 = Count()

            def bank2():
                u = unit2.up() - 1
                if u >= 4:
                    pe.wait_ge(u2_taken, u - 3)
                return ps[:, u % 4, :]

            def features2(ch, lo):
                w = weights("in2", ch, KT, 768)
                product(bank2()[:, 0:L], lambda k: w[:, k, lo:lo + P], lambda k: hT[:, k, :]).then_inc(u2_done, 1)

            def chunk2_used(units):
                pe.wait_ge(u2_done, units)
                pe.sem_inc(chunk_used, 1)

            pe.wait_ge(scaled[3], KT)
            chunk_there("in2", 0)
            for i in range(6):
                features2(0, i * P)
            chunk2_used(6)
            chunk_there("in2", 1)
            features2(1, 0)
            features2(1, P)
            w = weights("in2", 1, KT, 768)
            for b in range(BLK):
                product(bank2(), lambda k: hT[:, k, b * P:(b + 1) * P], lambda k: w[:, k, 256:768]).then_inc(u2_done, 1)
            chunk2_used(10)
            chunk_there("in2", 2)
            for i in range(6):
                features2(2, i * P)
            chunk2_used(16)

            pe.wait_ge(ks_ready, 1)
            for b in range(BLK):
                for h in range(HG):
                    last = pe.transpose(ps[:, 4 + b, h * P:(h + 1) * P], ks[:, h, b * P:(b + 1) * P], ident[:])
                last.then_inc(kst_done, 1)
            pe.wait_ge(kd_ready, 1)
            pe.wait_ge(qd_ready, 1)
            for b in range(BLK):
                t = slice(b * P, (b + 1) * P)
                for h in range(HG):
                    last = pe.matmul(ps[:, 6 + b, h * P:(h + 1) * P], lhsT=kd[:, h, t], rhs=raw_q[:, h, t],
                                     start=True, stop=True)
                last.then_inc(hsc_done, 1)
            chunk_there("in2", 3)
            features2(3, 0)
            features2(3, P)
            pe.wait_ge(kst_taken, 2)
            pe.wait_ge(hsc_ready, 2)
            for ch in range(CHUNKS - 1):
                b, r = divmod(ch, P // CHUNK)
                rows = slice(CHUNK * r, CHUNK * (r + 1))
                if ch >= 4:
                    pe.wait_ge(state_ready, ch - 3)
                for h in range(HG):
                    n = slice(h * P, (h + 1) * P)
                    last = pe.matmul(ps[:, 4 + ch % 4, n], lhsT=ksT[rows, b, n], rhs=v_[rows, b, n],
                                     start=True, stop=True)
                last.then_inc(kv_done, 1)
            pe.wait_ge(state_ready, CHUNKS - 1)
            pe.wait_ge(xc_ready, 4)
            pe.wait_ge(lru_there, 16 * 4)
            for g in range(2):
                for j in range(4):
                    last = pe.matmul(ps[:, 4 + 2 * g + j // 2, (j % 2) * L:(j % 2 + 1) * L],
                                     lhsT=gate_w[:, g, j, :], rhs=xc[:, j, :], start=True, stop=True)
                last.then_inc(gates_done, 1)
            for i in range(4):
                features2(3, 256 + i * P)
            chunk2_used(22)
            pe.wait_ge(gates_ready, 8)
            for h in range(HG):
                n = slice(h * P, (h + 1) * P)
                o = ps[:, 4 + h // 2, (h % 2) * L:(h % 2 + 1) * L]
                for b in range(BLK):
                    pe.matmul(o[:, b * P:(b + 1) * P], lhsT=v_[:, b, n], rhs=sc_[:, b, h, :],
                              start=h % 2 == 0 and b == 0, stop=False, skip_group_check=True)
                for ch in range(1, CHUNKS):
                    t = slice(ch * CHUNK, (ch + 1) * CHUNK)
                    last = pe.matmul(o[:, t], lhsT=state(ch)[:, n], rhs=raw_q[:, h, t], start=False,
                                     stop=ch == CHUNKS - 1, skip_group_check=True)
                if h % 2:
                    last.then_inc(o_done, 1)
            def outputs_ssq(i):
                pe.wait_ge(o_sq, i + 1)
                pe.matmul(ps[:, 6 + i, :], lhsT=ones[:], rhs=o_sqs(i), start=True,
                          stop=True).then_inc(o_ssq, 1)

            outputs_ssq(0)
            pe.wait_ge(mix2_ready, 4)
            pe.wait_ge(u2_taken, 22)
            chunk_there("out2", 0)
            chunk_there("out2", 1)
            out_part("out2", 0, 1, (0, 1))
            outputs_ssq(1)
            out_part("out2", 0, 1, (2, 3))
            out_part("out2", 1, 1, range(4, 8))
            pe.wait_ge(mix2_ready, 8)
            out_part("out2", 0, 0, range(4), KT + 4)
            out_part("out2", 1, 0, range(4, 8), KT + 8)

            for t in range(FT):
                ch, i = divmod(t, FFN_STEP)
                n = min(FFN_STEP, FT - ch * FFN_STEP)
                if i == 0:
                    chunk_there("ffn", ch)
                w = weights("ffn", ch, KT, 2 * n * P)
                if t >= 4:
                    pe.wait_ge(up_scaled, t - 3)
                else:
                    pe.wait_ge(mo_taken, 2 * KT)
                for half in range(2):
                    at = (half * n + i) * P
                    for k in range(KT):
                        if t == 0 and half == 0:
                            pe.wait_ge(scaled[4], k + 1)
                        last = pe.matmul(ps[:, t % 4, half * L:(half + 1) * L], lhsT=w[:, k, at:at + P],
                                         rhs=hT[:, k, :], start=k == 0, stop=k == KT - 1)
                last.then_inc(ffn_done, 1)
                if t == 0:
                    pe.wait_ge(sq_ready[4], 2)
                    sum_squares(4, 6)
                if i == 0 and t:
                    pe.wait_ge(ffn_done, t)
                    pe.sem_inc(chunk_used, 1)
                if t == FT - 1:
                    pe.wait_ge(ffn_done, FT)
                    pe.sem_inc(chunk_used, 1)
            for t in range(FT):
                ch, i = divmod(t, DOWN_STEP)
                n = min(DOWN_STEP, FT - ch * DOWN_STEP)
                if i == 0:
                    chunk_there("down", ch)
                w = weights("down", ch, n, D)
                pe.wait_ge(ffn_taken, t + 1)
                for j in range(KT):
                    last = pe.matmul(ps[:, 4 + j // 2, (j % 2) * L:(j % 2 + 1) * L], lhsT=w[:, i, j * P:(j + 1) * P],
                                     rhs=ffn[:, t, :], start=t == 0 and j % 2 == 0, stop=t == FT - 1,
                                     skip_group_check=True)
                    if t == FT - 1 and j % 2:
                        last.then_inc(down_done, 1)
                if i == n - 1 and t < FT - 1:
                    last.then_inc(chunk_used, 1)

            pe.wait_ge(sq_ready[6], 2)
            sum_squares(6, 4)
            pe.wait_ge(scaled[5], KT)
            for i in range(4):
                b, half = divmod(i, 2)
                for k in range(4):
                    last = pe.transpose(ps[:, i, k * P:(k + 1) * P], hT[:, 4 * half + k, b * P:(b + 1) * P], ident[:])
                last.then_inc(otr_done, 1)

        @block.scalar
        def _(act):
            def rows(tile, names, name):
                lo, hi = names[name]
                return hT[lo:hi, tile, 0:P]

            for name, v in (("c", c[0]), ("b_ada", b_ada[0]), ("g_mix", g_mix[0]), ("g_ffn", g_ffn[0]),
                            ("g_final", g_final)):
                act.dma_start(rows(0, PA_ROWS, name), v.rearrange("(k p) -> k p", p=P)).then_inc(par_a_there, 16)
            for name, v in (("g_out_a", g_out_a[0]), ("g_out_b", g_out_b[0]), ("mix2", mix_norm_w_2[0]), ("ffn2", ffn_norm_w_2[0]),
                            ("final2", final_norm_w_2), ("lb0", hg_lb_2[0]), ("lb1", hg_lb_2[1]),
                            ("hg_norm", hg_norm_w_2[0]),
                            ("conv_w", conv_w_2[0].rearrange("w n -> (w n)")), ("conv_b", conv_b_2[0]),
                            ("lru_ba", lru_ba_2[0]), ("lru_bx", lru_bx_2[0]), ("lru_a", lru_a_2[0])):
                act.dma_start(rows(1, PB_ROWS, name), v.rearrange("(k p) -> k p", p=P)).then_inc(par_there, 16)
            act.dma_start(brow[0:1, 0:8], b_forget).then_inc(par_there, 16)
            act.dma_start(brow[0:1, 8:8 + GROUPS], b_group).then_inc(par_there, 16)
            act.dma_start(brow[0:1, 8 + GROUPS:8 + GROUPS + EXPERTS], b_router.rearrange("o g e -> o (g e)")
                          ).then_inc(par_there, 16)

            def squares(i, src, ready, first, second):
                for half, n in ((0, first), (1, second)):
                    act.wait_ge(ready, n)
                    act.activation(sq[:, 4 * half:4 * half + 4, :], src[:, 4 * half:4 * half + 4, :], ACT.Square
                                   ).then_inc(sq_ready[i], 1)

            def std_of(i, n, bank=6, parts=1):
                act.wait_ge(ssq_ready[i], parts)
                act.activation(rstd[:].rearrange("p a t -> p (a t)")[:, 0:parts * L], ps[:, bank, 0:parts * L],
                               ACT.Sqrt, scale=1.0 / n, bias=EPS).then_inc(std_ready[i], 1)

            def add_shift(i, shift):
                for k in range(KT):
                    act.wait_ge(scaled[i], k + 1)
                    act.activation(hT[:, k, :], hT[:, k, :], ACT.Identity, bias=mod[:, shift + k:shift + k + 1]
                                   ).then_inc(h_ready[i], 1)

            act.wait_ge(par_taken, 1)
            act.activation(silu_c[:], parA[:, 0:KT], ACT.Silu).then_inc(silu_c_ready, 1)
            for q, bank in enumerate((0, 1, 4, 5)):
                act.wait_ge(xT_tr, q + 1)
                act.activation(xT[:, 2 * q:2 * q + 2, :], ps[:, bank, :].rearrange("p (k t) -> p k t", k=2),
                               ACT.Copy).then_inc(xT_ready, 1)
            squares(0, xT, xT_ready, 2, 4)
            std_of(0, D)
            act.wait_ge(mod_ready, 1)
            add_shift(0, 0)

            unit = Count()

            def take(dst, src, scale=1.0):
                u = unit.up() - 1
                act.wait_ge(tile_ready, u + 1)
                act.activation(dst, src(ps[:, u % 2, :]), ACT.Copy, scale=scale).then_inc(tile_taken, 1)

            def whole(o):
                return o[:, 0:L]

            def relu_dots(h):
                act.wait_ge(dots_ready, h + 1)
                if h >= 2:
                    act.wait_ge(score_raw, 2 * (h - 1))
                act.activation(relu[:, h % 2, :], ps[:, 2 + h % 2, 0:NK], ACT.Relu).then_inc(dots_taken, 1)

            take(iwT, lambda o: o[:, 0:16].rearrange("p (b h) -> p b h", b=BLK))
            take(kI[0:64, :], lambda o: o[0:64, 0:L])
            act.wait_ge(tile_taken, 2)
            act.dma_start(kI[64:128, :], kI[0:64, :]).then_inc(ki_moved, 16)
            for j in range(4):
                take(qI[:, j, :], whole)
            relu_dots(0)
            relu_dots(1)
            take(kA, whole)
            act.wait_ge(tile_taken, 7)
            act.dma_start(kA_swap[64:128, :], kA[0:64, :]).then_inc(k_moved, 16)
            act.dma_start(kA_swap[0:64, :], kA[64:128, :]).then_inc(k_moved, 16)
            relu_dots(2)
            relu_dots(3)
            take(vA, lambda o: o[:, 0:256].rearrange("p (b n) -> p b n", b=BLK))
            for j in range(4):
                if j < 2:
                    relu_dots(4 + 2 * j)
                    relu_dots(5 + 2 * j)
                take(qA[:, j, :], whole, SCALE)

            def attend(n):
                if n >= 5 and n % 2:
                    act.wait_ge(pv_done, n - 3)
                    act.activation(mixT[:, (n - 5) // 2, :], ps[:, 6, 0:L], ACT.Copy).then_inc(pv_taken, 1)
                if n < 2 * HEADS:
                    act.wait_ge(logits_ready, 2 * (n + 1))
                    if n >= 2:
                        act.wait_ge(pt_done, n - 1)
                    act.activation(prob[:, n % 2, 0:P], logit[:, n % 2, 0:P], ACT.Exp,
                                   bias=neg_max[:, n, 0:1], accum_out=p_sum[:, n, 0:1]).then_inc(act_step, 1)
                    act.activation(prob[:, n % 2, P:NK], logit[:, n % 2, P:NK], ACT.Exp,
                                   bias=neg_max[:, n, 1:2], accum_out=p_sum[:, n, 1:2]).then_inc(probs_ready, 1)
                if 2 <= n <= 2 * HEADS + 1:
                    m = n - 2
                    act.wait_ge(pt_done, m + 1)
                    if m >= 2:
                        act.wait_ge(pv_done, m - 1)
                    act.activation(probT[:, m % 2, :], ps[:, 4 + m % 2, 0:NK], ACT.Copy).then_inc(pt_taken, 1)

            take(forget[:, 0, :], lambda o: o[:, 0:16])
            take(kB[:, 2, :], whole)
            take(kB[:, 3, :], whole)
            take(vB[:, 0, :], lambda o: o)
            take(vB[:, 1, :], lambda o: o)
            for n in range(6):
                attend(n)
                if n < 4:
                    take(qB[:, n, :], whole, SCALE)
                else:
                    take(kB[:, n - 4, :], whole)
                if n == 1:
                    act.wait_ge(forget_abs, 1)
                    act.activation(forget[:, 1, :], forget[:, 1, :], ACT.Exp).then_inc(forget_ln, 1)
                    act.wait_ge(forget_ln, 1)
                    act.activation(forget[:, 1, :], forget[:, 1, :], ACT.Ln, bias=1.0).then_inc(forget_ln, 1)
            for n in range(6, 2 * HEADS):
                attend(n)
                if n == HEADS + 5:
                    act.wait_ge(ada_done, ADA_N)
                    act.wait_ge(pv_taken, 4)
                    act.activation(sq[:, 0:4, :], mixT[:, 0:4, :], ACT.Square).then_inc(sq_ready[5], 1)
                if n == HEADS:
                    act.dma_start(wr[:, :, 0:GROUPS], w_group[0].rearrange("(k p) g -> p k g", p=P)
                                  ).then_inc(wr_there, 16)
                    for g in range(GROUPS):
                        act.dma_start(wr[:, :, GROUPS + PER_GROUP * g:GROUPS + PER_GROUP * (g + 1)],
                                      w_router[0, g].rearrange("(k p) e -> p k e", p=P)).then_inc(wr_there, 16)
            def group_std(half, bank):
                act.wait_ge(ssq_ready[5], half + 1)
                act.activation(rstd[:, half, :], ps[:, bank, half * L:(half + 1) * L], ACT.Sqrt, scale=1.0 / 512,
                               bias=EPS).then_inc(std_ready[5], 1)

            for n in range(2 * HEADS, 2 * HEADS + 4):
                attend(n)
                if n == 2 * HEADS:
                    group_std(0, 0)
            act.wait_ge(pv_taken, 8)
            act.activation(sq[:, 4:8, :], mixT[:, 4:8, :], ACT.Square).then_inc(sq_ready[5], 1)
            group_std(1, 6)
            squares(1, xT, mo_taken, 4, 8)
            std_of(1, D)
            act.wait_ge(mod_ready, 2)
            add_shift(1, 24)

            for i in range(4):
                b, half = divmod(i, 2)
                act.wait_ge(htr_done, i + 1)
                act.activation(tok[:, b, :].rearrange("t (j p) -> t j p", j=KT)[:, :, 64 * half:64 * half + 64],
                               ps[:, i, :].rearrange("t (p j) -> t j p", j=KT), ACT.Copy).then_inc(htr_taken_a, 1)
            act.wait_ge(gate_max, 1)
            for b in range(BLK):
                act.activation(g_pen[:, b, :], g8[:, b, 0:GROUPS], ACT.Exp, bias=w_top[:, 0, b:b + 1],
                               accum_out=g_sum[:, b:b + 1]).then_inc(gate_exp, 1)
            act.wait_ge(top_diff, 1)
            act.activation(e_diff, e_diff, ACT.Exp).then_inc(top_exp, 1)
            for j in range(0, KT, 2):
                act.wait_ge(gather_done, j + 1)
                act.activation(xsT[:, j, 0:PAIRS], ps[:, j % 4, :], ACT.Copy).then_inc(gather_taken_a, 1)
            act.wait_ge(lru_par, 2)
            act.activation(t8, t8, ACT.Exp).then_inc(lru_par_a, 1)
            act.activation(t4, t4, ACT.Exp).then_inc(lru_par_a, 1)
            act.wait_ge(lru_par_a, 2)
            act.activation(t4, t4, ACT.Ln, bias=1.0).then_inc(lru_par_a, 1)
            act.wait_ge(windows_ready, 2)
            too_many = act.value_load(flag_i[0:1, 0:1], min_val=0, max_val=1)

            def pair_act(n, u, y_sem, y_count):
                act.wait_ge(gu_done, n + 1)
                if y_sem is chunk_used:
                    act.sem_inc(gate_up_used, 1)
                act.wait_ge(act_ready, n + 1)
                act.activation(act_g, ps[:, 0, 0:FE], ACT.Silu).then_inc(silu_done, 1)
                act.wait_ge(turn_done, n + 1)
                act.activation(turned[:, u, :], ps[:, 1, :], ACT.Copy).then_inc(turn_taken, 1)
                act.wait_ge(y_sem, y_count)
                act.activation(y_sb[:, 0:512], ps[:, 2, :], ACT.Copy).then_inc(y_taken_a, 1)

            act.sem_inc(y_taken_a, 1)
            with act.If(too_many < 1):
                with act.Fori(0, EXPERTS // SLOTS) as i:
                    for u in range(2):
                        pair_act(i * 2 + u, u, chunk_used, i * SLOTS + (USED0 + 2 * u + 2))
            with act.Else():
                with act.Fori(0, EXPERTS // 2 * WINDOWS) as i:
                    pair_act(i, 0, w_y_done, i + 1)
            for half in range(2):
                tiles = slice(4 * half, 4 * half + 4)
                act.wait_ge(comb_taken, 4 * half + 4)
                act.activation(sq[:, tiles, :], xT[:, tiles, :], ACT.Square).then_inc(sq_ready[2], 1)
                for k in range(4 * half, 4 * half + 4):
                    g = PA_ROWS["g_final"][0] + k
                    act.activation(hT[:, k, :], xT[:, k, :], ACT.Square, scale=parA[:, g:g + 1]
                                   ).then_inc(sq_ready[3], 1)
            act.wait_ge(both_ssq, 1)
            act.activation(rstd[:, 1, :], rstd[:, 1, :], ACT.Sqrt, scale=1.0 / D).then_inc(std_ready[3], 1)
            std_of(2, D)

            unit2 = Count()

            def take2(dst, n=L):
                u = unit2.up() - 1
                act.wait_ge(u2_done, u + 1)
                act.activation(dst, ps[:, u % 4, 0:n], ACT.Copy).then_inc(u2_taken, 1)

            take2(raw_q[:, 2, :])
            take2(raw_q[:, 3, :])
            for h in range(HG):
                take2(f_[:, h, :])
            act.wait_ge(u2_taken, 6)
            act.activation(f_, f_, ACT.Sigmoid).then_inc(f_sig, 1)
            take2(raw_q[:, 0, :])
            take2(raw_q[:, 1, :])
            act.wait_ge(u2_taken, 8)
            act.activation(a_, raw_q, ACT.Sigmoid).then_inc(q_sig, 1)
            take2(v_[:, 0, :], 512)
            act.wait_ge(f_ready, 1)
            act.activation(f_, f_, ACT.Ln).then_inc(f_ln, 1)
            take2(v_[:, 1, :], 512)
            take2(lx[:, 0, 4:260])
            act.wait_ge(b_ready, HG)
            act.activation(eb, b_, ACT.Exp).then_inc(decay_ready, 1)
            act.activation(kd, b_, ACT.Exp, scale=-1.0).then_inc(decay_ready, 1)
            take2(lx[:, 1, 4:260])
            act.wait_ge(last_diff, 1)
            act.activation(ks, ks, ACT.Exp).then_inc(last_exp, 1)
            take2(lx[:, 2, 4:260])
            take2(lx[:, 3, 4:260])
            take2(lg[:, 0, :])
            take2(lg[:, 1, :])
            for b in range(BLK):
                act.wait_ge(kst_done, b + 1)
                act.activation(ksT[:, b, :], ps[:, 4 + b, :], ACT.Copy).then_inc(kst_taken, 1)
            take2(lg[:, 2, :])
            take2(lg[:, 3, :])
            for g in range(2):
                act.wait_ge(gates_done, g + 1)
                for j in range(4):
                    bias = parB[:, PB_ROWS["lru_bx" if g else "lru_ba"][0] + j:][:, 0:1]
                    act.activation((ig if g else r_)[:, j, :],
                                   ps[:, 4 + 2 * g + j // 2, (j % 2) * L:(j % 2 + 1) * L], ACT.Sigmoid,
                                   bias=bias).then_inc(gates_ready, 1)
            take2(g_[:, 0, :])
            take2(g_[:, 1, :])
            act.wait_ge(gates_ready, 8)
            act.wait_ge(lru_par, 3)
            for j in range(4):
                act.activation(th[:, j, :], r_[:, j, :], ACT.Tanh, scale=lru_c[:, j:j + 1]).then_inc(decays_ready, 1)
                act.activation(a_[:, j, :], r_[:, j, :], ACT.Exp, scale=lru_nc[:, j:j + 1]).then_inc(decays_ready, 1)
            take2(g_[:, 2, :])
            take2(g_[:, 3, :])
            act.wait_ge(half_power, 1)
            act.activation(th, th, ACT.Sqrt, scale=2.0).then_inc(power_root, 1)
            act.wait_ge(gelu_in, 1)
            act.activation(k_, k_, ACT.Sigmoid, scale=1.5957691216057308).then_inc(gelu_sig, 1)
            act.wait_ge(u2_taken, 22)
            act.activation(ks, g_, ACT.Sigmoid).then_inc(g_sig, 1)
            o_f, b_f = o_.rearrange("p h t -> p (h t)"), b_.rearrange("p h t -> p (h t)")

            def o_squares(i):
                act.wait_ge(o_done, i + 1)
                act.activation(o_f[:, i * 512:(i + 1) * 512], ps[:, 4 + i, :], ACT.Copy).then_inc(o_taken, 1)
                act.wait_ge(o_taken, i + 1)
                act.activation(o_sqs(i), o_f[:, i * 512:(i + 1) * 512], ACT.Square).then_inc(o_sq, 1)

            def o_stds(i):
                act.wait_ge(o_ssq, i + 1)
                act.activation(b_f[:, i * 512:(i + 1) * 512], ps[:, 6 + i, :], ACT.Sqrt, scale=1.0 / P, bias=EPS
                               ).then_inc(o_std, 1)

            o_squares(0)
            o_squares(1)
            o_stds(0)
            o_stds(1)
            for half in range(2):
                for k in range(4 * half, 4 * half + 4):
                    g = PB_ROWS["ffn2"][0] + k
                    act.wait_ge(mo_taken, KT + k + 1)
                    act.activation(hT[:, k, :], xT[:, k, :], ACT.Copy, scale=parB[:, g:g + 1]).then_inc(scaled[4], 1)
            for half in range(2):
                tiles = slice(4 * half, 4 * half + 4)
                act.activation(sq[:, tiles, :], xT[:, tiles, :], ACT.Square).then_inc(sq_ready[4], 1)
            std_of(4, D)

            for t in range(FT):
                act.wait_ge(gate_scaled, t + 1)
                act.activation(silu_t[:, t % 2, :], silu_t[:, t % 2, :], ACT.Silu).then_inc(ffn_silu, 1)
            squares(6, xT, down_taken, 2, 4)
            std_of(6, D, bank=4)
            for b in range(BLK):
                act.wait_ge(otr_done, 2 * b + 1)
                act.activation(tok[:, b, 0:512], ps[:, 2 * b, :], ACT.Copy).then_inc(otr_taken_a, 1)

        @block.vector
        def _(ve):
            step = Count()

            def own(k=1):
                ve.wait_ge(dve_step, step.up(k))

            def rstd_of(i, parts=1):
                ve.wait_ge(std_ready[i], 1)
                r = rstd[:].rearrange("p a t -> p (a t)")[:, 0:parts * L]
                ve.reciprocal(r, r).then_inc(dve_step, 1)
                own()

            def scale(i, dst, gain):
                for k in range(KT):
                    ve.scalar_tensor_tensor(dst[:, k, :], xT[:, k, :], gain[:, k:k + 1], rstd[:, 0, :],
                                            ALU.mult, ALU.mult).then_inc(scaled[i], 1)

            def par(tile, names, name, k=None):
                lo, hi = names[name]
                return tile[:, lo:hi] if k is None else tile[:, lo + k:lo + k + 1]

            ve.wait_ge(par_tr, 1)
            ve.tensor_copy(parA[:], ps[:, 2, 0:PA_N]).then_inc(par_taken, 1)
            ve.wait_ge(silu_c_ready, 1)
            for ch in range(ADA_FIRST):
                w, part = ada_arrived(ve, ch), ada_part(ch)
                ve.tensor_scalar(part, w[:, 0, :], silu_c[:, 0:1], None, ALU.mult).then_inc(dve_step, 1)
                for k in range(1, KT):
                    own()
                    ve.scalar_tensor_tensor(part, w[:, k, :], silu_c[:, k:k + 1], part, ALU.mult, ALU.add
                                            ).then_inc(ada_used_v if k == KT - 1 else dve_step, 1)
                if ch == 0:
                    rstd_of(0)
            ve.wait_ge(par_tr, 2)
            ve.tensor_copy(parB[:], ps[:, 3, 0:PB_N]).then_inc(par_taken, 1)
            m0 = ADA_FIRST * ADA_W // P
            b_lo = PA_ROWS["b_ada"][0]
            ve.wait_ge(par_taken, 2)
            ve.wait_ge(ada_done, ADA_FIRST)
            ve.tensor_tensor(mod[:, 0:m0], ps[:, 7, 0:m0], parA[:, b_lo:b_lo + m0], ALU.add).then_inc(mod_ready, 1)
            ve.wait_ge(mod_ready, 1)
            ve.scalar_tensor_tensor(gains[:, 0, :], mod[:, 8:16], 1.0, par(parA, PA_ROWS, "g_mix"), ALU.add,
                                    ALU.mult).then_inc(dve_step, 1)
            own()
            scale(0, hT, gains[:, 0, :])

            ve.wait_ge(par_taken, 2)
            lb0, lb1, lru = par(parB, PB_ROWS, "lb0"), par(parB, PB_ROWS, "lb1"), par(parB, PB_ROWS, "lru_a")
            ve.tensor_tensor(m4, lb0, lb1, ALU.max).then_inc(dve_step, 1)
            ve.tensor_scalar(u4, lru, -1.0, 0.0, ALU.mult, ALU.max).then_inc(dve_step, 1)
            own(2)
            ve.tensor_tensor(t8[:, 0:4], lb0, m4, ALU.subtract).then_inc(dve_step, 1)
            ve.tensor_tensor(t8[:, 4:8], lb1, m4, ALU.subtract).then_inc(lru_par, 1)
            ve.scalar_tensor_tensor(t4, lru, -1.0, lru, ALU.mult, ALU.min).then_inc(lru_par, 1)
            own()

            keys = (slice(0, P), slice(P, NK))
            for h in range(HEADS):
                ve.wait_ge(dots_taken, h + 1)
                if h:
                    ve.wait_ge(score_raw, 2 * h)
                for b in range(BLK):
                    if h == 0:
                        ve.tensor_scalar(score[:, keys[b]], relu[:, 0, keys[b]], iwT[:, b, 0:1], None, ALU.mult
                                         ).then_inc(score_raw, 1)
                    else:
                        ve.scalar_tensor_tensor(score[:, keys[b]], relu[:, h % 2, keys[b]], iwT[:, b, h:h + 1],
                                                score[:, keys[b]], ALU.mult, ALU.add).then_inc(score_raw, 1)
            ve.wait_ge(score_raw, 2 * HEADS)
            for b in range(BLK):
                ve.tensor_tensor(score[:, keys[b]], score[:, keys[b]], causal[:, P:L] if b == 0 else causal, ALU.add
                                 ).then_inc(dve_step, 1)
            own(2)
            for r in range(TOPK // 8):
                src = score if r == 0 else left
                for b in range(BLK):
                    ve.max(top8[:, b, :], src[:, keys[b]]).then_inc(dve_step, 1)
                own(2)
                for b in range(BLK):
                    ve.match_replace(left[:, keys[b]], top8[:, b, :], src[:, keys[b]], TAKEN).then_inc(dve_step, 1)
                own(2)
            ve.tensor_scalar(sel_bias, left, -3.2e38, NEG, ALU.is_gt, ALU.mult).then_inc(dve_step, 1)
            own()
            for b in range(BLK):
                ve.tensor_tensor(sel_bias[:, keys[b]], sel_bias[:, keys[b]], causal[:, P:L] if b == 0 else causal,
                                 ALU.add).then_inc(sel_ready, 1)

            def logits(n):
                ve.wait_ge(logits_done, n + 1)
                bank = 2 + n % 2
                if n < HEADS:
                    slope = 2.0 ** (-8.0 * (n + 1) / HEADS)
                    ve.scalar_tensor_tensor(with_alibi, neg_dist, slope, ps[:, bank, 0:NK], ALU.mult, ALU.add
                                            ).then_inc(logits_taken, 1)
                    ve.wait_ge(sel_ready, 2)
                    ve.wait_ge(logits_taken, n + 1)
                    ve.tensor_tensor(logit[:, n % 2, :], with_alibi, sel_bias, ALU.add).then_inc(dve_step, 1)
                    own()
                else:
                    h = n - HEADS
                    ve.scalar_tensor_tensor(logit[:, n % 2, 0:P], ps[:, bank, 0:P], cum[:, 0, h:h + 1],
                                            causal[:, P:L], ALU.add, ALU.add).then_inc(dve_step, 1)
                    ve.scalar_tensor_tensor(logit[:, n % 2, P:NK], ps[:, bank, P:NK], cum[:, 1, h:h + 1],
                                            causal[:], ALU.add, ALU.add).then_inc(logits_taken, 1)
                    own()
                    ve.wait_ge(logits_taken, n + 1)
                for b in range(BLK):
                    ve.tensor_reduce(neg_max[:, n, b:b + 1], logit[:, n % 2, keys[b]], AX.X, ALU.max, negate=True
                                     ).then_inc(logits_ready, 1)

            def diagonals(m):
                ve.wait_ge(probs_ready, m + 1)
                ve.reciprocal(p_rsum[:, m, :], p_sum[:, m, :]).then_inc(dve_step, 1)
                own()
                if m >= 2:
                    ve.wait_ge(pt_done, m - 1)
                for b in range(BLK):
                    i = ve.tensor_scalar(diag[:, m % 2, b, :], ident[:], p_rsum[:, m, b:b + 1], None, ALU.mult)
                i.then_inc(diag_ready, 1)

            for n in range(2 * HEADS + 1):
                if n < 2 * HEADS:
                    logits(n)
                if n:
                    diagonals(n - 1)
                if n == 0:
                    ve.wait_ge(tile_taken, 13)
                    ve.scalar_tensor_tensor(forget[:, 1, :], forget[:, 0, :], -1.0, forget[:, 0, :], ALU.mult,
                                            ALU.min).then_inc(forget_abs, 1)
                if n == 2:
                    ve.wait_ge(forget_ln, 2)
                    ve.scalar_tensor_tensor(forget[:, 2, :], forget[:, 0, :], 0.0, forget[:, 1, :], ALU.min,
                                            ALU.subtract).then_inc(log_f_ready, 1)
                if n == 5:
                    ve.wait_ge(cum_done, 1)
                    ve.tensor_copy(cum, ps[:, 7, 64:80].rearrange("p (b h) -> p b h", b=BLK)).then_inc(cum_taken, 1)
                    ve.tensor_scalar(ncumT[0:HEADS, :], ps[0:HEADS, 7, 128:384], -1.0, None, ALU.mult
                                     ).then_inc(cum_taken, 1)
                    ve.wait_ge(cum_taken, 2)
            ve.wait_ge(ada_done, ADA_N)
            ve.tensor_tensor(mod[:, m0:48], ps[:, 7, m0:48], parA[:, b_lo + m0:b_lo + 48], ALU.add).then_inc(mod_ready, 1)
            ve.wait_ge(mod_ready, 2)
            ve.scalar_tensor_tensor(gains[:, 1, :], mod[:, 32:40], 1.0, par(parA, PA_ROWS, "g_ffn"), ALU.add,
                                    ALU.mult).then_inc(dve_step, 1)
            own()
            ve.tensor_tensor(gains[:, 0, :], par(parA, PA_ROWS, "g_final"), par(parB, PB_ROWS, "mix2"), ALU.mult
                             ).then_inc(dve_step, 1)
            own()
            for half in range(2):
                ve.wait_ge(std_ready[5], half + 1)
                ve.reciprocal(rstd[:, half, :], rstd[:, half, :]).then_inc(dve_step, 1)
                own()
                for k in range(4 * half, 4 * half + 4):
                    ve.scalar_tensor_tensor(mixT[:, k, :], mixT[:, k, :], parB[:, k:k + 1], rstd[:, half, :],
                                            ALU.mult, ALU.mult).then_inc(mix_ready, 1)
            for m in range(KT):
                ve.wait_ge(mo_done, m // 2 * 2 + 2)
                ve.scalar_tensor_tensor(xT[:, m, :], ps[:, m // 2, (m % 2) * L:(m % 2 + 1) * L], mod[:, 16 + m:17 + m], xT[:, m, :], ALU.mult,
                                        ALU.add).then_inc(mo_taken, 1)

            rstd_of(1)
            scale(1, hT, gains[:, 1, :])
            nr = GROUPS + EXPERTS
            ve.memset(g8, -BIG).then_inc(dve_step, 1)
            own()
            ve.wait_ge(route_done, 1)
            logit_r = ps[:, 4, 0:BLK * nr].rearrange("p (b n) -> p b n", b=BLK)
            ve.tensor_copy(g8[:, :, 0:GROUPS], logit_r[:, :, 0:GROUPS]).then_inc(dve_step, 1)
            ve.tensor_copy(e_log, logit_r[:, :, GROUPS:nr]).then_inc(dve_step, 1)
            own(2)
            for b in range(BLK):
                ve.max(g_top[:, b, :], g8[:, b, :]).then_inc(dve_step, 1)
            own(2)
            ve.tensor_scalar(w_top[:, 0, :], g_top[:, :, 0], -1.0, None, ALU.mult).then_inc(gate_max, 1)
            for b in range(BLK):
                ve.max_index(idx_u[:, 0, b, :], g_top[:, b, :], g8[:, b, :]).then_inc(dve_step, 1)
            own(2)
            ve.tensor_copy(g_idx, idx_u[:, 0, :, 0]).then_inc(dve_step, 1)
            own()
            for b in range(BLK):
                ve.tensor_scalar(g_one[:, b, :], col_no[:, 0:GROUPS], g_idx[:, b:b + 1], None, ALU.is_equal
                                 ).then_inc(dve_step, 1)
            own(2)
            ve.wait_ge(gate_exp, 2)
            ve.tensor_scalar(g_pen, g_one, -1.0, BIG, ALU.add, ALU.mult).then_inc(dve_step, 1)
            one = g_one.rearrange("p b g -> p (b g)").unsqueeze(2).broadcast_to([P, BLK * GROUPS, PER_GROUP])
            pen = g_pen.rearrange("p b g -> p (b g)").unsqueeze(2).broadcast_to([P, BLK * GROUPS, PER_GROUP])
            e_3d = e_log.rearrange("p b (g e) -> p (b g) e", g=GROUPS)
            ve.tensor_tensor(e_3d, e_3d, one, ALU.mult).then_inc(dve_step, 1)
            own(2)
            ve.tensor_tensor(e_3d, e_3d, pen, ALU.add).then_inc(dve_step, 1)
            own()
            for b in range(BLK):
                ve.max(e_top[:, b, :], e_log[:, b, :]).then_inc(dve_step, 1)
            own(2)
            ve.tensor_tensor(e_diff, e_top[:, :, 1], e_top[:, :, 0], ALU.subtract).then_inc(top_diff, 1)
            for b in range(BLK):
                ve.max_index(idx_u[:, 1, b, :], e_top[:, b, :], e_log[:, b, :]).then_inc(dve_step, 1)
            own(2)
            ve.tensor_copy(e_idx, idx_u[:, 1, :, 0:2]).then_inc(dve_step, 1)
            own()
            for ch in range(2):
                for b in range(BLK):
                    ve.tensor_scalar(R_one[:, ch, b * EXPERTS:(b + 1) * EXPERTS], col_no[:, 0:EXPERTS],
                                     e_idx[:, b, ch:ch + 1], None, ALU.is_equal).then_inc(dve_step, 1)
            own(4)
            ve.tensor_tensor(R_chosen.rearrange("p b e -> p (b e)"), R_one[:, 0, :], R_one[:, 1, :], ALU.add
                             ).then_inc(choice_ready, 1)
            ve.wait_ge(rank_done, 1)
            ve.wait_ge(pad_ready, 5)
            ve.tensor_copy(rank[:, :, 0:EXPERTS], ps[:, 5, 0:64].rearrange("p (b e) -> p b e", b=BLK)
                           ).then_inc(dve_step, 1)
            ve.tensor_copy(counts, ps[:, 5, 64:96]).then_inc(dve_step, 1)
            own(2)
            ve.tensor_tensor_scan(upto, ones[:, 0:EXPERTS], counts, 0.0, ALU.mult, ALU.add).then_inc(dve_step, 1)
            own()
            ve.tensor_tensor(starts_f, upto, counts, ALU.subtract).then_inc(dve_step, 1)
            own()
            ve.tensor_tensor(place, ps[:, 5, 0:64].rearrange("p (b e) -> p b e", b=BLK),
                             starts_f.unsqueeze(1).broadcast_to([P, BLK, EXPERTS]), ALU.add).then_inc(dve_step, 1)
            own()
            prod = tmp_cols[:, 0:2 * BLK * EXPERTS].rearrange("p (c n) -> p c n", c=2)
            ve.tensor_tensor(prod, R_one, place.rearrange("p b e -> p (b e)").unsqueeze(1).broadcast_to(
                [P, 2, BLK * EXPERTS]), ALU.mult).then_inc(dve_step, 1)
            own()
            ve.tensor_reduce(cols.rearrange("p c b -> p (c b)"), prod.rearrange("p c (b e) -> p (c b) e", b=BLK),
                             AX.X, ALU.add).then_inc(dve_step, 1)
            own()
            for b in range(BLK):
                if b:
                    ve.wait_ge(pick_ready, b)
                ve.tensor_scalar(tmp_cols, col_no, cols[:, 1, b:b + 1], None, ALU.is_equal).then_inc(dve_step, 1)
                own()
                ve.scalar_tensor_tensor(pick[:, b, :], col_no, cols[:, 0, b:b + 1], tmp_cols, ALU.is_equal, ALU.add
                                        ).then_inc(pick_ready, 1)
            for w in range(WINDOWS):
                ve.tensor_scalar(wins_i[0:1, w, 0:EXPERTS], starts_f[0:1, :], float(w * WIN), float(PAIRS), ALU.add, ALU.min
                                 ).then_inc(dve_step, 1)
            ve.memset(wins_i[0:1, :, EXPERTS:], 0).then_inc(dve_step, 1)
            ve.tensor_reduce(most, counts, AX.X, ALU.max).then_inc(dve_step, 1)
            own(WINDOWS + 2)
            ve.tensor_scalar(flag_i[0:1, 0:1], most[0:1, :], float(WIN), None, ALU.is_gt).then_inc(windows_ready, 2)
            ve.wait_ge(top_exp, 1)
            ve.scalar_tensor_tensor(w_top[:, 0, :], e_diff, 1.0, g_sum, ALU.add, ALU.mult).then_inc(dve_step, 1)
            own()
            ve.reciprocal(w_top[:, 0, :], w_top[:, 0, :]).then_inc(dve_step, 1)
            own()
            ve.tensor_tensor(w_top[:, 1, :], w_top[:, 0, :], e_diff, ALU.mult).then_inc(dve_step, 1)
            own()
            ve.tensor_scalar(w_all[:, :, 0:EXPERTS], R_one[:, 0, :].rearrange("p (b e) -> p b e", b=BLK), 0.0, None,
                             ALU.mult).then_inc(dve_step, 1)
            own()
            for ch in range(2):
                for b in range(BLK):
                    ve.scalar_tensor_tensor(w_all[:, b, 0:EXPERTS], R_one[:, ch, b * EXPERTS:(b + 1) * EXPERTS],
                                            w_top[:, ch, b:b + 1], w_all[:, b, 0:EXPERTS], ALU.mult, ALU.add
                                            ).then_inc(dve_step, 1)
                own(2)
            for j in range(1, KT, 2):
                ve.wait_ge(gather_done, j + 1)
                ve.tensor_copy(xsT[:, j, 0:PAIRS], ps[:, j % 4, :]).then_inc(gather_taken_v, 1)

            def windows(n, u, starts, e, w):
                for h in range(2):
                    ve.tensor_copy(xw[:, u, :, h * WIN:(h + 1) * WIN], xsT[:, :, bass.ds(starts[h], WIN)])
                shape = [P, BLK, 2, WIN]
                rows = (col_no[:, 0:WIN] if w is None else col_no[:, bass.ds(w * WIN, WIN)])
                ve.tensor_tensor(put[:, u], rows.unsqueeze(1).unsqueeze(1).broadcast_to(shape),
                                 rank[:, :, bass.ds(e, 2)].unsqueeze(3).broadcast_to(shape), ALU.is_equal
                                 ).then_inc(rows_found, 1)
                ve.wait_ge(rows_found, n + 1)
                ve.tensor_tensor(put[:, u], put[:, u], w_all[:, :, bass.ds(e, 2)].unsqueeze(3).broadcast_to(shape),
                                 ALU.mult).then_inc(windows_copied, 1)

            def gated(n):
                ve.wait_ge(silu_done, n + 1)
                ve.tensor_tensor(act_e, act_g, ps[:, 0, FE:2 * FE], ALU.mult).then_inc(act_ready, 1)

            def result():
                ve.tensor_copy(y_sb[:, 512:1024], ps[:, 3, :]).then_inc(y_taken_v, 1)

            def load(lo, n):
                return nc.values_load_multi_w_load_instructions(
                    wins_i[:].rearrange("o w e -> o (w e)")[0:1, bass.ds(lo, n)], engines=(ENG.DVE,), min_val=0,
                    max_val=PAIRS)[1]

            ve.wait_ge(gather_taken_v, 4)
            ve.wait_ge(gather_taken_a, 4)
            too_many = ve.value_load(flag_i[0:1, 0:1], min_val=0, max_val=1)
            ve.sem_inc(y_taken_v, 1)
            ve.sem_inc(act_ready, 1)
            with ve.If(too_many < 1):
                windows(0, 0, load(0, 2), 0, None)
                with ve.Fori(0, EXPERTS // SLOTS) as i:
                    starts = load(i * SLOTS + 2, SLOTS)
                    for u in range(2):
                        gated(i * 2 + u)
                        windows(i * 2 + (u + 1), 1 - u, starts[2 * u:2 * u + 2], i * SLOTS + (2 * u + 2), None)
                        ve.wait_ge(chunk_used, i * SLOTS + (USED0 + 2 * u + 2))
                        result()
            with ve.Else():
                with ve.Fori(0, EXPERTS // 2) as i:
                    with ve.Fori(0, WINDOWS) as w:
                        n = i * WINDOWS + w
                        windows(n, 0, load(w * (EXPERTS + SLOTS) + i * 2, 2), i * 2, w)
                        gated(n)
                        ve.wait_ge(w_y_done, n + 1)
                        result()
            for j in range(KT):
                ve.wait_ge(comb_done, 1)
                ve.scalar_tensor_tensor(xT[:, j, :], ps[:, 4 + j // 2, (j % 2) * L:(j % 2 + 1) * L], mod[:, 40 + j:41 + j], xT[:, j, :], ALU.mult,
                                        ALU.add).then_inc(comb_taken, 1)
            ve.wait_ge(ssq_ready[2], 1)
            ve.wait_ge(ssq_ready[3], 1)
            ve.tensor_scalar(rstd[:, 1, :], ps[:, 6, 0:L], D * EPS, EPS, ALU.add, ALU.mult).then_inc(dve_step, 1)
            own()
            ve.tensor_tensor(rstd[:, 1, :], rstd[:, 1, :], ps[:, 5, 0:L], ALU.add).then_inc(both_ssq, 1)
            ve.wait_ge(std_ready[3], 1)
            ve.reciprocal(rstd[:, 1, :], rstd[:, 1, :]).then_inc(dve_step, 1)
            own()
            for k in range(KT):
                ve.scalar_tensor_tensor(hT[:, k, :], xT[:, k, :], gains[:, 0, k:k + 1], rstd[:, 1, :],
                                        ALU.mult, ALU.mult).then_inc(scaled[3], 1)
            rstd_of(2)
            scale(2, xT, par(parA, PA_ROWS, "g_final"))

            ve.wait_ge(lru_par_a, 3)
            ve.tensor_tensor(m4, t8[:, 0:4], t8[:, 4:8], ALU.add).then_inc(dve_step, 1)
            ve.tensor_tensor(u4, u4, t4, ALU.add).then_inc(dve_step, 1)
            own(2)
            ve.reciprocal(m4, m4).then_inc(dve_step, 1)
            ve.tensor_scalar(lru_c, u4, LRU_C, None, ALU.mult).then_inc(dve_step, 1)
            ve.tensor_scalar(lru_nc, u4, -LRU_C, None, ALU.mult).then_inc(lru_par, 1)
            own(2)
            ve.tensor_tensor(lb, t8[:, 0:4], m4, ALU.mult).then_inc(dve_step, 1)
            own()
            ve.tensor_scalar(one_lb, lb, -1.0, 1.0, ALU.mult, ALU.add).then_inc(dve_step, 1)
            ve.memset(lx[:, :, 1:4], 0.0).then_inc(dve_step, 1)
            own(2)
            ve.wait_ge(f_sig, 1)
            for h in range(HG):
                ve.tensor_scalar(f_[:, h, :], f_[:, h, :], one_lb[:, h:h + 1], lb[:, h:h + 1], ALU.mult, ALU.add
                                 ).then_inc(dve_step, 1)
            own(HG)
            ve.tensor_scalar(k_, f_, -1.0, 1.0, ALU.mult, ALU.add).then_inc(f_ready, 1)
            ve.wait_ge(q_sig, 1)
            ve.tensor_tensor(raw_q, raw_q, a_, ALU.mult).then_inc(dve_step, 1)
            own()
            ve.wait_ge(f_ln, 1)
            for h in range(HG):
                ve.tensor_tensor_scan(b_[:, h, :], reset, f_[:, h, :], 0.0, ALU.mult, ALU.add).then_inc(b_ready, 1)
            ve.wait_ge(b_ready, HG)
            ve.wait_ge(f_ready, 1)
            flat = "p h (c j) -> p (h c) j"
            bc = b_.rearrange(flat, j=CHUNK)
            ve.tensor_tensor(ks.rearrange(flat, j=CHUNK),
                             bc[:, :, CHUNK - 1:CHUNK].broadcast_to([P, HG * CHUNKS, CHUNK]), bc, ALU.subtract
                             ).then_inc(last_diff, 1)
            ve.wait_ge(decay_ready, 1)
            ve.tensor_tensor(raw_q, raw_q, eb, ALU.mult).then_inc(qd_ready, 1)
            ve.wait_ge(decay_ready, 2)
            ve.tensor_tensor(kd, kd, k_, ALU.mult).then_inc(kd_ready, 1)
            ve.wait_ge(last_exp, 1)
            ve.tensor_tensor(ks, ks, k_, ALU.mult).then_inc(ks_ready, 1)
            ve.wait_ge(u2_taken, 14)
            cw, cb = PB_ROWS["conv_w"][0], PB_ROWS["conv_b"][0]
            for tap in range(CONV):
                for j in range(4):
                    w_tap = parB[:, cw + 4 * tap + j:cw + 4 * tap + j + 1]
                    if tap == 0:
                        ve.tensor_scalar(xc[:, j, :], lx[:, j, 1:1 + L], w_tap, parB[:, cb + j:cb + j + 1], ALU.mult,
                                         ALU.add).then_inc(dve_step, 1)
                    else:
                        ve.scalar_tensor_tensor(xc[:, j, :], lx[:, j, 1 + tap:1 + tap + L], w_tap, xc[:, j, :],
                                                ALU.mult, ALU.add
                                                ).then_inc(xc_ready if tap == CONV - 1 else dve_step, 1)
                if tap < CONV - 1:
                    own(4)
            for b in range(BLK):
                ve.wait_ge(hsc_done, b + 1)
                ve.scalar_tensor_tensor(sc_[:, b], ps[:, 6 + b, :].rearrange("p (h t) -> p h t", h=HG), BIG,
                                        in_chunk.unsqueeze(1).broadcast_to([P, HG, P]), ALU.min, ALU.mult
                                        ).then_inc(hsc_ready, 1)
            for ch in range(CHUNKS - 1):
                ve.wait_ge(kv_done, ch + 1)
                if ch == 0:
                    ve.tensor_copy(state(1), ps[:, 4, :]).then_inc(state_ready, 1)
                    continue
                ve.wait_ge(state_ready, ch)
                for h in range(HG):
                    n = slice(h * P, (h + 1) * P)
                    last = ch * CHUNK + CHUNK - 1
                    i = ve.scalar_tensor_tensor(state(ch + 1)[:, n], state(ch)[:, n], eb[:, h, last:last + 1],
                                                ps[:, 4 + ch % 4, n], ALU.mult, ALU.add)
                i.then_inc(state_ready, 1)
            ve.wait_ge(u2_taken, 18)
            ve.wait_ge(ks_ready, 1)
            ve.tensor_tensor(k_, lg, lg, ALU.mult).then_inc(dve_step, 1)
            own()
            ve.tensor_scalar(k_, k_, 0.044715, 1.0, ALU.mult, ALU.add).then_inc(dve_step, 1)
            own()
            ve.tensor_tensor(k_, k_, lg, ALU.mult).then_inc(gelu_in, 1)
            ve.wait_ge(decays_ready, 8)
            ve.tensor_scalar(r_, th, 1.0, None, ALU.add).then_inc(dve_step, 1)
            ve.tensor_tensor(ig, ig, xc, ALU.mult).then_inc(dve_step, 1)
            own(2)
            ve.reciprocal(r_, r_).then_inc(dve_step, 1)
            own()
            ve.tensor_tensor(th, th, r_, ALU.mult).then_inc(half_power, 1)
            ve.wait_ge(power_root, 1)
            ve.tensor_tensor(ig, ig, th, ALU.mult).then_inc(dve_step, 1)
            own()
            for j in range(4):
                ve.tensor_tensor_scan(xc[:, j, :], a_[:, j, :], ig[:, j, :], 0.0, ALU.mult, ALU.add
                                      ).then_inc(dve_step, 1)
            own(4)
            ve.wait_ge(gelu_sig, 1)
            ve.tensor_tensor(lg, lg, k_, ALU.mult).then_inc(dve_step, 1)
            own()
            ve.tensor_tensor(mixT[:, 4:8, :], xc, lg, ALU.mult).then_inc(mix2_ready, 4)
            ve.wait_ge(g_sig, 1)
            ve.scalar_tensor_tensor(g_, g_, par(parB, PB_ROWS, "hg_norm"), ks, ALU.mult, ALU.mult).then_inc(dve_step, 1)
            own()
            for i in range(2):
                h2 = slice(2 * i, 2 * i + 2)
                ve.wait_ge(o_std, i + 1)
                ve.reciprocal(b_[:, h2, :], b_[:, h2, :]).then_inc(dve_step, 1)
                ve.tensor_tensor(g_[:, h2, :], g_[:, h2, :], o_[:, h2, :], ALU.mult).then_inc(dve_step, 1)
                own(2)
                ve.tensor_tensor(mixT[:, h2, :], g_[:, h2, :], b_[:, h2, :], ALU.mult).then_inc(mix2_ready, 2)
            for m in range(KT):
                ve.wait_ge(mo_done, KT + m // 2 * 2 + 2)
                ve.tensor_tensor(xT[:, m, :], ps[:, m // 2, (m % 2) * L:(m % 2 + 1) * L], xT[:, m, :], ALU.add
                                 ).then_inc(mo_taken, 1)

            rstd_of(4)
            for t in range(FT + 1):
                if t < FT:
                    ve.wait_ge(ffn_done, t + 1)
                    if t >= 2:
                        ve.wait_ge(ffn_taken, t - 1)
                    ve.tensor_tensor(silu_t[:, t % 2, :], ps[:, t % 4, 0:L], rstd[:, 0, :], ALU.mult
                                     ).then_inc(gate_scaled, 1)
                    ve.tensor_tensor(ffn[:, t, :], ps[:, t % 4, L:2 * L], rstd[:, 0, :], ALU.mult
                                     ).then_inc(up_scaled, 1)
                if t:
                    ve.wait_ge(ffn_silu, t)
                    ve.wait_ge(up_scaled, t)
                    ve.tensor_tensor(ffn[:, t - 1, :], ffn[:, t - 1, :], silu_t[:, (t - 1) % 2, :], ALU.mult
                                     ).then_inc(ffn_taken, 1)
            for i in range(4):
                ve.wait_ge(down_done, i + 1)
                ve.tensor_tensor(xT[:, 2 * i:2 * i + 2, :], ps[:, 4 + i, :].rearrange("p (k t) -> p k t", k=2),
                                 xT[:, 2 * i:2 * i + 2, :], ALU.add).then_inc(down_taken, 1)
            rstd_of(6)
            scale(5, hT, par(parB, PB_ROWS, "final2"))
            for b in range(BLK):
                ve.wait_ge(otr_done, 2 * b + 2)
                ve.tensor_copy(tok[:, b, 512:1024], ps[:, 2 * b + 1, :]).then_inc(otr_taken_v, 1)


_INS = ['x', 'c', 'w_ada', 'b_ada', 'g_mix', 'w_in', 'b_forget', 'g_out_a', 'g_out_b', 'w_out', 'g_ffn',
        'w_group', 'b_group', 'w_router', 'b_router', 'w_gate', 'w_up', 'w_down', 'g_final',
        'mix_norm_w_2', 'w_in_2', 'hg_lb_2', 'hg_norm_w_2', 'conv_w_2', 'conv_b_2', 'lru_wa_2', 'lru_ba_2',
        'lru_wx_2', 'lru_bx_2', 'lru_a_2', 'w_out_2', 'ffn_norm_w_2', 'w_gate_up_2', 'w_down_2',
        'final_norm_w_2']


def kernel(**inputs):
    import numpy as np
    import concourse.bacc as bacc
    from concourse.bass_utils import run_bass_kernel_spmd

    nc = bacc.Bacc("TRN2", target_bir_lowering=False, num_devices=1)
    arrays, args = {}, []
    for name in _INS:
        a = np.ascontiguousarray(inputs[name])
        arrays[f"in_{name}"] = a
        args.append(nc.dram_tensor(f"in_{name}", a.shape, mybir.dt.from_np(a.dtype), kind="ExternalInput").ap())
    args.append(nc.dram_tensor("out_y", (1, L, D), F32, kind="ExternalOutput").ap())
    build(nc, *args)
    r = run_bass_kernel_spmd(nc, [arrays], core_ids=[0])
    return r.results[0]["out_y"]
```
